# Optimizing a Trainium2 kernel written in Bass

```python
import jax, jax.numpy as jnp
from jax import lax
import numpy as np

D_MODEL = 1024
BATCH = 1
SEQ = 512
DEPTH = 1

GRID_W = 64
CTX_LEN = 256
N_Q_HEADS = 8
N_KV_HEADS = 2
HEAD_DIM = 64
GROUP = N_Q_HEADS // N_KV_HEADS
ATTN_DIM = N_Q_HEADS * HEAD_DIM
KV_DIM = N_KV_HEADS * HEAD_DIM
CONV_DIM = D_MODEL - ATTN_DIM
MIX_DIM = ATTN_DIM + CONV_DIM
CONV_K = 3
OFF_K = ATTN_DIM
OFF_V = OFF_K + KV_DIM
OFF_B = OFF_V + KV_DIM
OFF_C = OFF_B + CONV_DIM
OFF_U = OFF_C + CONV_DIM
MIX_IN_DIM = OFF_U + CONV_DIM
D_FF = 2816
N_MOD = 9
ROPE_THETA = 10000.0
Q_BLOCK = 128
ATTN_SCALE = HEAD_DIM ** -0.5
EPS = 1e-6


def rmsnorm(x, g):
    x32 = x.astype(jnp.float32)
    y = x32 * lax.rsqrt(jnp.mean(x32 * x32, axis=-1, keepdims=True) + EPS)
    return (y * g.astype(jnp.float32)).astype(x.dtype)

def modulate(h, shift, scale):
    return h * (1 + scale) + shift

def swiglu(h, w_in, w_out):
    gate, up = jnp.split(h @ w_in, 2, axis=-1)
    return (jax.nn.silu(gate) * up) @ w_out

def axial_rope_tables(n_tokens):
    rows = n_tokens // GRID_W
    row = jnp.repeat(jnp.arange(rows, dtype=jnp.float32), GRID_W)
    col = jnp.tile(jnp.arange(GRID_W, dtype=jnp.float32), rows)
    n_freq = HEAD_DIM // 4
    inv = ROPE_THETA ** (-jnp.arange(n_freq, dtype=jnp.float32) / n_freq)
    ang = jnp.concatenate([row[:, None] * inv, col[:, None] * inv], axis=-1)
    return jnp.cos(ang)[:, None, :], jnp.sin(ang)[:, None, :]

def apply_rope(x, cos, sin):
    xr = x.astype(jnp.float32).reshape(x.shape[:-1] + (HEAD_DIM // 2, 2))
    x0, x1 = xr[..., 0], xr[..., 1]
    out = jnp.stack([x0 * cos - x1 * sin, x0 * sin + x1 * cos], axis=-1)
    return out.reshape(x.shape).astype(x.dtype)

def gqa_softmax(q, k, v):
    s = jnp.einsum('bqkgd,bskd->bkgqs', q, k, preferred_element_type=jnp.float32) * ATTN_SCALE
    p = jax.nn.softmax(s, axis=-1).astype(v.dtype)
    return jnp.einsum('bkgqs,bskd->bqkgd', p, v)

def latent_attention(q, k, v, kc, vc):
    b, s = q.shape[:2]
    nb = s // Q_BLOCK
    k_all = jnp.concatenate([kc, k], axis=1)
    v_all = jnp.concatenate([vc, v], axis=1)
    qb = q.reshape(b, nb, Q_BLOCK, N_KV_HEADS, GROUP, HEAD_DIM).transpose(1, 0, 2, 3, 4, 5)
    o = lax.map(lambda qi: gqa_softmax(qi, k_all, v_all), qb)
    return o.transpose(1, 0, 2, 3, 4, 5).reshape(b, s, ATTN_DIM)

def context_attention(q, kc, vc):
    b, l = q.shape[:2]
    o = gqa_softmax(q.reshape(b, l, N_KV_HEADS, GROUP, HEAD_DIM), kc, vc)
    return o.reshape(b, l, ATTN_DIM)

def short_conv3(u, w):
    up = jnp.pad(u, ((0, 0), (1, 1), (0, 0)))
    return up[:, :-2] * w[0] + up[:, 1:-1] * w[1] + up[:, 2:] * w[2]

def split_heads(p, q_norm, k_norm):
    b, l = p.shape[:2]
    q = rmsnorm(p[..., :OFF_K].reshape(b, l, N_Q_HEADS, HEAD_DIM), q_norm)
    k = rmsnorm(p[..., OFF_K:OFF_V].reshape(b, l, N_KV_HEADS, HEAD_DIM), k_norm)
    v = p[..., OFF_V:OFF_B].reshape(b, l, N_KV_HEADS, HEAD_DIM)
    gb, gc, u = p[..., OFF_B:OFF_C], p[..., OFF_C:OFF_U], p[..., OFF_U:]
    return q, k, v, gb, gc, u

def first_inputs(seed: int = 0) -> dict:
    key = jax.random.key(seed)
    ks = jax.random.split(key, 24)
    f32 = jnp.float32
    nrm = lambda k, shape, s: jax.random.normal(k, shape, f32) * s
    gain = lambda k, shape: 1.0 + 0.05 * jax.random.normal(k, shape, f32)
    return {
        "x": nrm(ks[0], (BATCH, SEQ, D_MODEL), 1.0),
        "c": nrm(ks[1], (BATCH, D_MODEL), 1.0),
        "ctx": nrm(ks[2], (BATCH, CTX_LEN, D_MODEL), 1.0),
        "c_ctx": nrm(ks[3], (D_MODEL,), 1.0),
        "w_ada": nrm(ks[4], (DEPTH, D_MODEL, N_MOD * D_MODEL), 0.5 * D_MODEL ** -0.5),
        "b_ada": nrm(ks[5], (DEPTH, N_MOD * D_MODEL), 0.02),
        "norm_ffn1": gain(ks[6], (DEPTH, D_MODEL)),
        "w_ffn1_in": nrm(ks[7], (DEPTH, D_MODEL, 2 * D_FF), D_MODEL ** -0.5),
        "w_ffn1_out": nrm(ks[8], (DEPTH, D_FF, D_MODEL), D_FF ** -0.5),
        "norm_mix": gain(ks[9], (DEPTH, D_MODEL)),
        "w_mix_in": nrm(ks[10], (DEPTH, D_MODEL, MIX_IN_DIM), D_MODEL ** -0.5),
        "q_norm": gain(ks[11], (DEPTH, HEAD_DIM)),
        "k_norm": gain(ks[12], (DEPTH, HEAD_DIM)),
        "conv_w": nrm(ks[13], (DEPTH, CONV_K, CONV_DIM), CONV_K ** -0.5),
        "attn_out_norm": gain(ks[14], (DEPTH, ATTN_DIM)),
        "conv_out_norm": gain(ks[15], (DEPTH, CONV_DIM)),
        "w_mix_out": nrm(ks[16], (DEPTH, MIX_DIM, D_MODEL), MIX_DIM ** -0.5),
        "norm_ffn2": gain(ks[17], (DEPTH, D_MODEL)),
        "w_ffn2_in": nrm(ks[18], (DEPTH, D_MODEL, 2 * D_FF), D_MODEL ** -0.5),
        "w_ffn2_out": nrm(ks[19], (DEPTH, D_FF, D_MODEL), D_FF ** -0.5),
        "final_norm": gain(ks[20], (D_MODEL,)),
    }

def first_block(x, c, ctx, c_ctx, w_ada, b_ada, norm_ffn1, w_ffn1_in, w_ffn1_out,
              norm_mix, w_mix_in, q_norm, k_norm, conv_w, attn_out_norm, conv_out_norm,
              w_mix_out, norm_ffn2, w_ffn2_in, w_ffn2_out, final_norm):
    b, s, d = x.shape
    cos, sin = axial_rope_tables(s)

    for l in range(DEPTH):
        update_ctx = l < DEPTH - 1
        m = (jax.nn.silu(c) @ w_ada[l] + b_ada[l]).reshape(b, 1, N_MOD, d)
        mc = (jax.nn.silu(c_ctx) @ w_ada[l] + b_ada[l]).reshape(1, 1, N_MOD, d)

        x = x + 0.5 * m[:, :, 2] * swiglu(modulate(rmsnorm(x, norm_ffn1[l]), m[:, :, 0], m[:, :, 1]),
                                          w_ffn1_in[l], w_ffn1_out[l])
        ctx = ctx + 0.5 * mc[:, :, 2] * swiglu(modulate(rmsnorm(ctx, norm_ffn1[l]), mc[:, :, 0], mc[:, :, 1]),
                                               w_ffn1_in[l], w_ffn1_out[l])

        px = modulate(rmsnorm(x, norm_mix[l]), m[:, :, 3], m[:, :, 4]) @ w_mix_in[l]
        pc = modulate(rmsnorm(ctx, norm_mix[l]), mc[:, :, 3], mc[:, :, 4]) @ w_mix_in[l]
        q, k, v, gb, gc, u = split_heads(px, q_norm[l], k_norm[l])
        qc, kc, vc, gbc, gcc, uc = split_heads(pc, q_norm[l], k_norm[l])

        a = latent_attention(apply_rope(q, cos, sin), apply_rope(k, cos, sin), v, kc, vc)
        sc = gb * short_conv3(gc * u, conv_w[l])
        mix = jnp.concatenate([rmsnorm(a, attn_out_norm[l]), rmsnorm(sc, conv_out_norm[l])], axis=-1)
        x = x + m[:, :, 5] * (mix @ w_mix_out[l])

        if update_ctx:
            ac = context_attention(qc, kc, vc)
            scc = gbc * short_conv3(gcc * uc, conv_w[l])
            mixc = jnp.concatenate([rmsnorm(ac, attn_out_norm[l]), rmsnorm(scc, conv_out_norm[l])], axis=-1)
            ctx = ctx + mc[:, :, 5] * (mixc @ w_mix_out[l])
            ctx = ctx + 0.5 * mc[:, :, 8] * swiglu(modulate(rmsnorm(ctx, norm_ffn2[l]), mc[:, :, 6], mc[:, :, 7]),
                                                   w_ffn2_in[l], w_ffn2_out[l])

        x = x + 0.5 * m[:, :, 8] * swiglu(modulate(rmsnorm(x, norm_ffn2[l]), m[:, :, 6], m[:, :, 7]),
                                          w_ffn2_in[l], w_ffn2_out[l])

    return rmsnorm(x, final_norm)


D_MIX = D_MODEL
RET_HEADS = 4
RET_WIDTH = D_MIX // 2
RET_DK = RET_WIDTH // RET_HEADS
RET_DV = RET_WIDTH // RET_HEADS
GLA_HEADS = 4
GLA_WIDTH = D_MIX - RET_WIDTH
GLA_DV = GLA_WIDTH // GLA_HEADS
GLA_DK = GLA_DV // 2
GLA_RANK = 16
GLA_GATE_NORM = 16.0
CHUNK = 64
ROPE_BASE = 10000.0
N_KEYS = 128
N_EXPERTS = N_KEYS * N_KEYS
PEER_HEADS = 8
PEER_TOPK = 16
PEER_DQ = 256
PEER_BLOCK = 128
N_MOD_2 = 6
IN_SIZES = (RET_WIDTH, RET_WIDTH, RET_WIDTH, RET_WIDTH,
            GLA_HEADS * GLA_DK, GLA_HEADS * GLA_DK, GLA_WIDTH, GLA_WIDTH,
            GLA_RANK, GLA_RANK)
IN_COLS = sum(IN_SIZES)


F32 = jnp.float32

def rmsnorm_2(x, w):
    xf = x.astype(F32)
    y = xf * lax.rsqrt(jnp.mean(xf * xf, axis=-1, keepdims=True) + EPS)
    return (y * w.astype(F32)).astype(x.dtype)

def head_rmsnorm(o):
    o = o * lax.rsqrt(jnp.mean(o * o, axis=-1, keepdims=True) + EPS)
    B, H, L, d = o.shape
    return o.transpose(0, 2, 1, 3).reshape(B, L, H * d)

def modulate_2(h, shift, scale):
    return h * (1 + scale) + shift

def to_heads(t, n_heads):
    B, L, W = t.shape
    return t.reshape(B, L, n_heads, W // n_heads).transpose(0, 2, 1, 3)

def flip_seq(t):
    return jnp.flip(t, axis=2)

def axial_rope(rows, cols):
    r, c = jnp.meshgrid(jnp.arange(rows, dtype=F32), jnp.arange(cols, dtype=F32), indexing="ij")
    n_freq = RET_DK // 4
    inv = ROPE_BASE ** (-jnp.arange(n_freq, dtype=F32) / n_freq)
    ang = jnp.concatenate([r.reshape(-1, 1) * inv, c.reshape(-1, 1) * inv], axis=-1)
    return jnp.cos(ang), jnp.sin(ang)

def apply_rope_2(t, cos, sin):
    t1, t2 = jnp.split(t, 2, axis=-1)
    return jnp.concatenate([t1 * cos - t2 * sin, t2 * cos + t1 * sin], axis=-1)

def to_chunks(t):
    B, H, L, d = t.shape
    return t.reshape(B, H, L // CHUNK, CHUNK, d).transpose(2, 0, 1, 3, 4)

def from_chunks(t):
    n, B, H, C, d = t.shape
    return t.transpose(1, 2, 0, 3, 4).reshape(B, H, n * C, d)

def retention_scan(q, k, v, log_gamma, s0):
    idx = jnp.arange(CHUNK, dtype=F32)
    rel = idx[:, None] - idx[None, :]
    lg = log_gamma[:, None, None]
    decay_mask = jnp.where(rel >= 0, jnp.exp(lg * jnp.maximum(rel, 0.0)), 0.0)
    q_dec = jnp.exp(log_gamma[:, None] * (idx + 1.0))[None, :, :, None]
    k_dec = jnp.exp(log_gamma[:, None] * (CHUNK - 1.0 - idx))[None, :, :, None]
    chunk_dec = jnp.exp(log_gamma * CHUNK)[None, :, None, None]

    def step(s, inp):
        qc, kc, vc = inp
        scores = jnp.einsum("bhid,bhjd->bhij", qc, kc) * decay_mask
        out = (jnp.einsum("bhij,bhjv->bhiv", scores, vc)
               + jnp.einsum("bhid,bhdv->bhiv", qc * q_dec, s))
        s = chunk_dec * s + jnp.einsum("bhjd,bhjv->bhdv", kc * k_dec, vc)
        return s, out

    s, out = lax.scan(step, s0, (to_chunks(q), to_chunks(k), to_chunks(v)))
    return from_chunks(out), s

def gla_scan(q, k, v, log_a, s0):
    causal = (jnp.arange(CHUNK)[:, None] >= jnp.arange(CHUNK)[None, :])

    def step(s, inp):
        qc, kc, vc, ac = inp
        G = jnp.cumsum(ac, axis=2)
        G_last = G[:, :, -1:, :]
        q_t = qc * jnp.exp(G)
        k_t = kc * jnp.exp(-G)
        scores = jnp.where(causal, jnp.einsum("bhid,bhjd->bhij", q_t, k_t), 0.0)
        out = (jnp.einsum("bhij,bhjv->bhiv", scores, vc)
               + jnp.einsum("bhid,bhdv->bhiv", q_t, s))
        s = (jnp.exp(G_last[:, :, 0, :])[..., None] * s
             + jnp.einsum("bhjd,bhjv->bhdv", kc * jnp.exp(G_last - G), vc))
        return s, out

    s, out = lax.scan(step, s0, (to_chunks(q), to_chunks(k), to_chunks(v), to_chunks(log_a)))
    return from_chunks(out), s

def retention_final_state(k, v, log_gamma):
    L = k.shape[2]
    w = jnp.exp(log_gamma[:, None] * (L - 1.0 - jnp.arange(L, dtype=F32)))
    return jnp.einsum("bhld,bhle->bhde", k * w[None, :, :, None], v)

def gla_final_state(k, v, log_a):
    G = jnp.cumsum(log_a, axis=2)
    return jnp.einsum("bhld,bhle->bhde", k * jnp.exp(G[:, :, -1:, :] - G), v)

def project(h, w_in, gk_up_f, gk_bias_f, gk_up_b, gk_bias_b, rope):
    p = (h @ w_in).astype(F32)
    splits = [int(s) for s in np.cumsum(IN_SIZES)[:-1]]
    rq, rk, rv, rg, gq, gk, gv, gg, lr_f, lr_b = jnp.split(p, splits, axis=-1)
    rq = to_heads(rq, RET_HEADS)
    rk = to_heads(rk, RET_HEADS) * (RET_DK ** -0.5)
    rv = to_heads(rv, RET_HEADS)
    if rope is not None:
        rq = apply_rope_2(rq, *rope)
        rk = apply_rope_2(rk, *rope)
    gq = to_heads(gq, GLA_HEADS) * (GLA_DK ** -0.5)
    gk = to_heads(gk, GLA_HEADS)
    gv = to_heads(gv, GLA_HEADS)
    la_f = to_heads(jax.nn.log_sigmoid(lr_f @ gk_up_f.astype(F32) + gk_bias_f.astype(F32)) / GLA_GATE_NORM, GLA_HEADS)
    la_b = to_heads(jax.nn.log_sigmoid(lr_b @ gk_up_b.astype(F32) + gk_bias_b.astype(F32)) / GLA_GATE_NORM, GLA_HEADS)
    return (rq, rk, rv, rg, gq, gk, gv, gg, la_f, la_b)

def bidir_mix(feats, lg_f, lg_b, states):
    rq, rk, rv, rg, gq, gk, gv, gg, la_f, la_b = feats
    s_rf, s_rb, s_gf, s_gb = states
    o_rf, s_rf = retention_scan(rq, rk, rv, lg_f, s_rf)
    o_rb, s_rb = retention_scan(flip_seq(rq), flip_seq(rk), flip_seq(rv), lg_b, s_rb)
    o_gf, s_gf = gla_scan(gq, gk, gv, la_f, s_gf)
    o_gb, s_gb = gla_scan(flip_seq(gq), flip_seq(gk), flip_seq(gv), flip_seq(la_b), s_gb)
    ret = head_rmsnorm(o_rf + flip_seq(o_rb)) * jax.nn.silu(rg)
    gla = head_rmsnorm(o_gf + flip_seq(o_gb)) * jax.nn.silu(gg)
    return jnp.concatenate([ret, gla], axis=-1), (s_rf, s_rb, s_gf, s_gb)

def context_final_states(feats, lg_f, lg_b):
    _, rk, rv, _, _, gk, gv, _, la_f, la_b = feats
    return (retention_final_state(rk, rv, lg_f),
            retention_final_state(flip_seq(rk), flip_seq(rv), lg_b),
            gla_final_state(gk, gv, la_f),
            gla_final_state(flip_seq(gk), flip_seq(gv), flip_seq(la_b)))

def zero_states(b):
    return (jnp.zeros((b, RET_HEADS, RET_DK, RET_DV), F32),
            jnp.zeros((b, RET_HEADS, RET_DK, RET_DV), F32),
            jnp.zeros((b, GLA_HEADS, GLA_DK, GLA_DV), F32),
            jnp.zeros((b, GLA_HEADS, GLA_DK, GLA_DV), F32))

def peer_ffn(h, w_q, k1, k2, down, up):
    B, L, D = h.shape
    half = PEER_DQ // 2
    blocks = h.reshape(-1, PEER_BLOCK, D)

    def block(xb):
        q = (xb @ w_q).astype(F32).reshape(PEER_BLOCK, PEER_HEADS, 2, half)
        s1 = jnp.einsum("thd,hnd->thn", q[:, :, 0], k1.astype(F32))
        s2 = jnp.einsum("thd,hnd->thn", q[:, :, 1], k2.astype(F32))
        v1, i1 = lax.top_k(s1, PEER_TOPK)
        v2, i2 = lax.top_k(s2, PEER_TOPK)
        cand_s = (v1[..., :, None] + v2[..., None, :]).reshape(PEER_BLOCK, PEER_HEADS, PEER_TOPK * PEER_TOPK)
        cand_i = (i1[..., :, None] * N_KEYS + i2[..., None, :]).reshape(PEER_BLOCK, PEER_HEADS, PEER_TOPK * PEER_TOPK)
        top_s, pos = lax.top_k(cand_s, PEER_TOPK)
        idx = jnp.take_along_axis(cand_i, pos, axis=-1)
        g = jax.nn.softmax(top_s, axis=-1)
        u = down[idx]
        act = jax.nn.gelu(jnp.einsum("thkd,td->thk", u, xb).astype(F32), approximate=False)
        return jnp.einsum("thk,thkd->td", (g * act).astype(xb.dtype), up[idx])

    return lax.map(block, blocks).reshape(B, L, D)

def trunk_layer(x, xc, c, c_ctx, w_mod, b_mod, norm1_w, norm2_w, w_in,
                ret_decay_f, ret_decay_b, gk_up_f, gk_bias_f, gk_up_b, gk_bias_b,
                w_out, peer_w_q, peer_k1, peer_k2, peer_down, peer_up, rope, update_ctx):
    mod = (jax.nn.silu(c) @ w_mod + b_mod)[:, None, :]
    mod_c = (jax.nn.silu(c_ctx) @ w_mod + b_mod)[None, None, :]
    sh1, sc1, g1, sh2, sc2, g2 = jnp.split(mod, N_MOD_2, axis=-1)
    csh1, csc1, cg1, csh2, csc2, cg2 = jnp.split(mod_c, N_MOD_2, axis=-1)
    lg_f = jax.nn.log_sigmoid(ret_decay_f.astype(F32))
    lg_b = jax.nn.log_sigmoid(ret_decay_b.astype(F32))

    feats_c = project(modulate_2(rmsnorm_2(xc, norm1_w), csh1, csc1),
                      w_in, gk_up_f, gk_bias_f, gk_up_b, gk_bias_b, None)
    if update_ctx:
        yc, ctx_states = bidir_mix(feats_c, lg_f, lg_b, zero_states(xc.shape[0]))
    else:
        ctx_states = context_final_states(feats_c, lg_f, lg_b)

    feats = project(modulate_2(rmsnorm_2(x, norm1_w), sh1, sc1),
                    w_in, gk_up_f, gk_bias_f, gk_up_b, gk_bias_b, rope)
    y, _ = bidir_mix(feats, lg_f, lg_b, ctx_states)
    x = x + g1 * (y.astype(x.dtype) @ w_out)
    x = x + g2 * peer_ffn(modulate_2(rmsnorm_2(x, norm2_w), sh2, sc2),
                          peer_w_q, peer_k1, peer_k2, peer_down, peer_up)
    if update_ctx:
        xc = xc + cg1 * (yc.astype(xc.dtype) @ w_out)
        xc = xc + cg2 * peer_ffn(modulate_2(rmsnorm_2(xc, norm2_w), csh2, csc2),
                                 peer_w_q, peer_k1, peer_k2, peer_down, peer_up)
    return x, xc

def second_inputs(seed: int = 0) -> dict:
    key = jax.random.key(seed)
    ks = jax.random.split(key, 24)

    def nrm(k, shape, s):
        return jax.random.normal(k, shape, F32) * s

    base_logit = jnp.asarray(np.log(2.0 ** (5 + np.arange(RET_HEADS)) - 1.0), F32)[None, :]
    return {
        "x": nrm(ks[0], (BATCH, SEQ, D_MODEL), 1.0),
        "c": nrm(ks[1], (BATCH, D_MODEL), 1.0),
        "ctx": nrm(ks[2], (BATCH, CTX_LEN, D_MODEL), 1.0),
        "c_ctx": nrm(ks[3], (D_MODEL,), 1.0),
        "w_mod": nrm(ks[4], (DEPTH, D_MODEL, N_MOD_2 * D_MODEL), 0.5 * D_MODEL ** -0.5),
        "b_mod": nrm(ks[5], (DEPTH, N_MOD_2 * D_MODEL), 0.02),
        "norm1_w": 1.0 + nrm(ks[6], (DEPTH, D_MODEL), 0.02),
        "norm2_w": 1.0 + nrm(ks[7], (DEPTH, D_MODEL), 0.02),
        "w_in": nrm(ks[8], (DEPTH, D_MODEL, IN_COLS), D_MODEL ** -0.5),
        "ret_decay_f": base_logit + nrm(ks[9], (DEPTH, RET_HEADS), 0.05),
        "ret_decay_b": base_logit + nrm(ks[10], (DEPTH, RET_HEADS), 0.05),
        "gla_gk_up_f": nrm(ks[11], (DEPTH, GLA_RANK, GLA_HEADS * GLA_DK), GLA_RANK ** -0.5),
        "gla_gk_bias_f": nrm(ks[12], (DEPTH, GLA_HEADS * GLA_DK), 0.1),
        "gla_gk_up_b": nrm(ks[13], (DEPTH, GLA_RANK, GLA_HEADS * GLA_DK), GLA_RANK ** -0.5),
        "gla_gk_bias_b": nrm(ks[14], (DEPTH, GLA_HEADS * GLA_DK), 0.1),
        "w_out": nrm(ks[15], (DEPTH, D_MIX, D_MODEL), D_MIX ** -0.5),
        "peer_w_q": nrm(ks[16], (DEPTH, D_MODEL, PEER_HEADS * PEER_DQ), D_MODEL ** -0.5),
        "peer_k1": nrm(ks[17], (DEPTH, PEER_HEADS, N_KEYS, PEER_DQ // 2), (PEER_DQ // 2) ** -0.5),
        "peer_k2": nrm(ks[18], (DEPTH, PEER_HEADS, N_KEYS, PEER_DQ // 2), (PEER_DQ // 2) ** -0.5),
        "peer_down": nrm(ks[19], (DEPTH, N_EXPERTS, D_MODEL), D_MODEL ** -0.5),
        "peer_up": nrm(ks[20], (DEPTH, N_EXPERTS, D_MODEL), 0.5),
        "norm_f_w": 1.0 + nrm(ks[21], (D_MODEL,), 0.02),
    }

def second_block(x, c, ctx, c_ctx, w_mod, b_mod, norm1_w, norm2_w, w_in,
              ret_decay_f, ret_decay_b, gla_gk_up_f, gla_gk_bias_f, gla_gk_up_b, gla_gk_bias_b,
              w_out, peer_w_q, peer_k1, peer_k2, peer_down, peer_up, norm_f_w):
    L = x.shape[1]
    ROWS = L // GRID_W
    rope = axial_rope(ROWS, GRID_W)
    xc = ctx
    for li in range(DEPTH):
        x, xc = trunk_layer(x, xc, c, c_ctx, w_mod[li], b_mod[li], norm1_w[li], norm2_w[li], w_in[li],
                            ret_decay_f[li], ret_decay_b[li], gla_gk_up_f[li], gla_gk_bias_f[li],
                            gla_gk_up_b[li], gla_gk_bias_b[li], w_out[li], peer_w_q[li],
                            peer_k1[li], peer_k2[li], peer_down[li], peer_up[li], rope,
                            li < DEPTH - 1)
    return rmsnorm_2(x, norm_f_w)


def setup_inputs(seed=0):
    out = dict(first_inputs(seed))
    for name, value in second_inputs(seed + 1).items():
        if name != "x":
            out[name + "_2"] = value
    return out


def reference(
    x, c, ctx, c_ctx, w_ada, b_ada, norm_ffn1, w_ffn1_in, w_ffn1_out, norm_mix, w_mix_in,
    q_norm, k_norm, conv_w, attn_out_norm, conv_out_norm, w_mix_out, norm_ffn2, w_ffn2_in,
    w_ffn2_out, final_norm, c_2, ctx_2, c_ctx_2, w_mod_2, b_mod_2, norm1_w_2, norm2_w_2, w_in_2,
    ret_decay_f_2, ret_decay_b_2, gla_gk_up_f_2, gla_gk_bias_f_2, gla_gk_up_b_2,
    gla_gk_bias_b_2, w_out_2, peer_w_q_2, peer_k1_2, peer_k2_2, peer_down_2, peer_up_2,
    norm_f_w_2,
):
    x = first_block(
        x, c, ctx, c_ctx, w_ada, b_ada, norm_ffn1, w_ffn1_in, w_ffn1_out, norm_mix, w_mix_in,
        q_norm, k_norm, conv_w, attn_out_norm, conv_out_norm, w_mix_out, norm_ffn2, w_ffn2_in,
        w_ffn2_out, final_norm,
    )
    return second_block(
        x, c_2, ctx_2, c_ctx_2, w_mod_2, b_mod_2, norm1_w_2, norm2_w_2, w_in_2, ret_decay_f_2,
        ret_decay_b_2, gla_gk_up_f_2, gla_gk_bias_f_2, gla_gk_up_b_2, gla_gk_bias_b_2, w_out_2,
        peer_w_q_2, peer_k1_2, peer_k2_2, peer_down_2, peer_up_2, norm_f_w_2,
    )


_drawn_inputs = setup_inputs


def setup_inputs(seed=0):
    import zlib

    import numpy as np

    out = dict(_drawn_inputs(seed))
    spreads = {}
    factors = {'norm_ffn1': 4.836,
     'q_norm': 8.0,
     'k_norm': 8.0,
     'attn_out_norm': 3.888,
     'conv_out_norm': 3.896,
     'norm_ffn2': 5.283,
     'norm1_w_2': 5.11,
     'norm2_w_2': 4.561,
     'gla_gk_bias_f_2': 7.121,
     'gla_gk_bias_b_2': 7.716,
     'norm_f_w_2': 2.837}
    for name, (base, spread) in spreads.items():
        noise = np.random.default_rng([zlib.crc32(name.encode()), seed]).standard_normal(out[name].shape)
        drawn = base * np.exp(spread * noise) if base else spread * noise
        out[name] = __import__('jax').numpy.asarray(drawn.astype(out[name].dtype))
    for name, factor in factors.items():
        out[name] = (out[name] * factor).astype(out[name].dtype)
    return out
```

```python
from contextlib import ExitStack

import concourse.bass as bass
import numpy as np
from concourse import mybir

F32 = mybir.dt.float32
U32 = mybir.dt.uint32
I32 = mybir.dt.int32
ALU = mybir.AluOpType
ACT = mybir.ActivationFunctionType
AX_X = mybir.AxisListType.X
ds = bass.ds

P = 128
D = 1024
KD = D // P
T = 512
C = 256
TC = T + C
HALF = TC // 2
FF = 2816
FT = FF // P
EPS = 1e-6
COLS = 512
SLOT = 4096
MOD_COLS = 256
ADA_TILES = 9 * KD
MOD_TILES = 6 * KD
ADA_BLOCKS = 9 * D // MOD_COLS
HEADS, KV_HEADS, HD = 8, 2, 64
RET_SCALE = 128 ** -0.5
GLA_SCALE = 64 ** -0.5
CHUNK = 64
NCH = T // CHUNK
GATE_NORM = 16.0
PEER_H, PEER_K, N_KEYS = 8, 16, 128
SLOTS = PEER_H * PEER_K
RING = 8
CREDIT = 2

UNIT = {}
_at = 0
for _name, _n in (("tokens", 6), ("ffn1_in", 44), ("ffn1_out", 16), ("q", 4), ("k", 1), ("v", 2), ("gb", 4),
                  ("gc", 4), ("u", 4), ("rope_q", 4), ("rope_k", 1), ("kdup", 2), ("scores", 32),
                  ("mix_out", 8), ("ffn2_in", 22), ("ffn2_out", 8), ("tokens2", 2), ("rq", 4), ("rk", 4),
                  ("rv", 6), ("rg", 4), ("gq", 2), ("gk", 2), ("gv", 6), ("gg", 4), ("lr", 1),
                  ("rope_r", 8), ("decay", 4), ("ret", 24), ("gla0", 9), ("gla1", 9), ("w_out", 8),
                  ("peer_q", 16), ("keys", 2), ("peer_s", 8), ("xb", 4), ("xtok", 4), ("rows", 2)):
    UNIT[_name] = _at
    _at += _n

SLOT_OF, SLOT_END = {}, []
for _name, _ends in (("ffn1_in", [UNIT["ffn1_in"] + 4 * (i + 1) for i in range(11)]),
                     ("ffn1_out", [UNIT["ffn1_out"] + 2 * (i + 1) for i in range(8)]),
                     ("mix_in", [UNIT["q"] + 4, UNIT["gb"] + 2, UNIT["gc"] + 2, UNIT["u"] + 2, UNIT["u"] + 4]),
                     ("mix_out", [UNIT["mix_out"] + 4, UNIT["mix_out"] + 8]),
                     ("ffn2_in", [UNIT["ffn2_in"] + 2 * (i + 1) for i in range(11)]),
                     ("ffn2_out", [UNIT["ffn2_out"] + i + 1 for i in range(8)]),
                     ("proj", [UNIT[n] for n in ("rk", "rv", "rg", "gq", "gv", "gg", "lr", "rope_r")]),
                     ("w_out", [UNIT["w_out"] + 4, UNIT["w_out"] + 8]),
                     ("peer_q", [UNIT["peer_q"] + 4 * (i + 1) for i in range(4)])):
    SLOT_OF[_name] = len(SLOT_END)
    SLOT_END += _ends

ROWS = {}
_at = 0
for _name, _n in (("c", 8), ("c_ctx", 8), ("norm_ffn1", 8), ("norm_mix", 8), ("attn_out_norm", 4),
                  ("conv_out_norm", 4), ("norm_ffn2", 8), ("final_norm", 8), ("c_2", 8), ("c_ctx_2", 8),
                  ("norm1_w_2", 8), ("norm2_w_2", 8), ("norm_f_w_2", 8), ("conv_w", 12),
                  ("q_norm", 1), ("k_norm", 1), ("gla_gk_bias_f_2", 2), ("gla_gk_bias_b_2", 2)):
    ROWS[_name] = (_at, _n)
    _at += _n
N_ROWS = _at
N_BIAS = ADA_TILES + MOD_TILES

CONST = {}
_at = 0
for _name, _n in (("ident", P), ("ones", P), ("blk64", P), ("swap_pairs", P), ("swap_halves", P),
                  ("dup0", P), ("dup1", P), ("causal_f", P), ("causal_b", P), ("chunk_reset", TC),
                  ("head_rows", 2), ("iota16", 16), ("eps", 1), ("zero", P)):
    CONST[_name] = (_at, _n)
    _at += _n
N_CONST = _at
N_DX, N_DC = 896, 640
N_DIST = 2 * (N_DX + N_DC)
N_VEC_DMAS = 26


def flat(ap):
    if len(ap.shape) == 1:
        return ap
    return ap.rearrange("a b -> (a b)")


def constants():
    t = np.zeros((P, N_CONST), np.float32)

    def put(name, value):
        at, n = CONST[name]
        t[:, at:at + n] = value

    p = np.arange(P)
    put("ident", np.eye(P))
    put("ones", 1.0)
    put("blk64", p[:, None] // 64 == p[None, :] // 64)
    pairs, halves = np.zeros((P, P)), np.zeros((P, P))
    pairs[p[0::2] + 1, p[0::2]], pairs[p[0::2], p[0::2] + 1] = -1.0, 1.0
    halves[p[:64] + 64, p[:64]], halves[p[:64], p[:64] + 64] = -1.0, 1.0
    put("swap_pairs", pairs)
    put("swap_halves", halves)
    for kv in range(KV_HEADS):
        put(f"dup{kv}", p[:, None] == kv * 64 + p[None, :] % 64)
    same = p[:, None] // CHUNK == p[None, :] // CHUNK
    put("causal_f", same & (p[:, None] <= p[None, :]))
    put("causal_b", same & (p[:, None] >= p[None, :]))
    reset = np.ones(TC)
    reset[0:T:CHUNK], reset[T] = 0.0, 0.0
    put("chunk_reset", reset[None, :])
    put("head_rows", np.stack([p < 64, p >= 64], 1) * GLA_SCALE)
    put("iota16", np.arange(16)[None, :])
    put("eps", EPS)
    tok, rope = np.arange(T), []
    for name, dim, place in (("pairs", HD, (p % 64) // 2), ("halves", 128, p % 64)):
        n = dim // 4
        inv = (np.float32(10000.0) ** (-np.arange(n, dtype=np.float32) / n)).astype(np.float32)
        ang = np.concatenate([(tok // 64).astype(np.float32)[:, None] * inv,
                              (tok % 64).astype(np.float32)[:, None] * inv], 1).T
        rope += [np.cos(ang)[place], np.sin(ang)[place]]
    rel = np.arange(N_DX)[None, :] - 384 - p[:, None]
    e = np.arange(N_DC)[None, :]
    dist = np.concatenate([np.maximum(rel, 0), np.maximum(-rel, 0), e + P - p[:, None], 640 + p[:, None] - e], 1)
    return {"const": t, "dist": dist.astype(np.float32), "rope": np.concatenate(rope, 1).astype(np.float32)}


def build(nc, a, out):
    with ExitStack() as ctx:
        def sb(name, cols, dt=F32, parts=P):
            return ctx.enter_context(nc.sbuf_tensor(name, [parts, cols], dt))

        def pb(name, shape):
            return ctx.enter_context(nc.psum_tensor(name, shape, F32))

        def sem(name):
            return ctx.enter_context(nc.semaphore(name))

        acc = pb("acc", [P, 4, 512])
        mod_ps = pb("mod_ps", [P, 512])
        sums = pb("sums", [P, 2, 512])
        misc = pb("misc", [P, 512])

        cst = sb("cst", N_CONST)
        resid = sb("resid", KD * TC)
        hid = sb("hid", KD * TC)
        wring = sb("wring", 2 * SLOT)
        modw = sb("modw", 2 * 2048)
        arena = sb("arena", 20480)
        rows1 = sb("rows1", P)
        rows2 = sb("rows2", P)
        vec = sb("vec", 256)
        cond = sb("cond", 32)
        mods = sb("mods", 2 * N_BIAS)
        gains = sb("gains", 5 * 16)
        halfg = sb("halfg", 2 * 16)
        squares = sb("squares", 2 * TC)
        std = sb("std", TC)
        rstd = sb("rstd", TC)
        tmp = sb("tmp", TC)
        dec = sb("dec", 80)
        gkup = sb("gkup", 2 * 256, parts=32)
        small = sb("small", 128)

        def c_(name, parts=P):
            at, n = CONST[name]
            return cst[0:parts, at:at + n]

        def v_(name, j=0, n=1):
            at = ROWS[name][0] + j
            return vec[:, at:at + n]

        ident, ones = c_("ident"), c_("ones")
        x_ = resid[:, :].rearrange("p (j t) -> p j t", j=KD)
        h768 = hid[:, :].rearrange("p (j t) -> p j t", j=KD)
        h512 = hid[:, 0:KD * T].rearrange("p (j t) -> p j t", j=KD)
        W = wring[:, :].rearrange("p (s n) -> p s n", s=2)
        Wk = wring[:, :].rearrange("p (s k n) -> p s k n", s=2, k=KD)
        Wf = W[:, :, 0:FT * P].rearrange("p s (f n) -> p s f n", f=FT)
        Wlr = W[:, :, 0:KD * 32].rearrange("p s (k n) -> p s k n", k=KD)
        Mw = modw[:, :].rearrange("p (s k n) -> p s k n", s=2, k=KD)
        cnd = cond[:, :].rearrange("p (b k c) -> p b k c", b=2, k=KD)
        mod = mods[:, :].rearrange("p (t c) -> p t c", c=2)
        gain = gains[:, :].rearrange("p (n k c) -> p n k c", n=5, k=KD)
        hgate = halfg[:, :].rearrange("p (n k c) -> p n k c", n=2, k=KD)
        sq = squares[:, :].rearrange("p (s t) -> p s t", s=2)

        def ar(at, *shape):
            n = int(np.prod(shape))
            v = arena[:, at:at + n]
            if len(shape) == 2:
                return v.rearrange("p (a b) -> p a b", a=shape[0])
            if len(shape) == 3:
                return v.rearrange("p (a b c) -> p a b c", a=shape[0], b=shape[1])
            return v

        def hi(at, *shape):
            n = int(np.prod(shape))
            v = hid[:, at:at + n]
            if len(shape) == 2:
                return v.rearrange("p (a b) -> p a b", a=shape[0])
            if len(shape) == 3:
                return v.rearrange("p (a b c) -> p a b c", a=shape[0], b=shape[1])
            return v

        tok = ar(0, 6, D)
        tok2 = ar(18432, 2, D)
        ff768, ff512 = ar(0, FT, TC), ar(0, FT, T)
        sg = ar(FT * TC, 2, 512)
        qT, kT = ar(0, 4, T), ar(2048, TC)
        kdup, vtok = ar(2816, 2, TC), ar(4352, 6, P)
        gb, cu, gc = ar(5120, 4, T), ar(7168, 4, T + 2), ar(9224, 4, T)
        prob, mixT = ar(11272, 3, TC), ar(13576, KD, T)
        probT = hid[:, :].rearrange("p (h r t) -> p h r t", h=2, r=6)
        cos_pairs, sin_pairs = hi(0, T), hi(T, T)
        yT = ar(0, KD, T)
        rq, rk, rv = ar(4096, 4, T), ar(6144, 4, TC), ar(9216, 6, 512)
        gq, gk = ar(12288, 2, T), ar(13312, 2, TC)
        lr = arena[0:32, 14848:14848 + TC]
        la = ar(15616, 2, 2, TC)
        retP = ar(18688, 2, T)
        gv = modw[:, 0:3072].rearrange("p (b n) -> p b n", b=6)
        cos_halves, sin_halves = modw[:, 3072:3072 + T], modw[:, 3072 + T:4096]
        dist = hi(0, N_DIST)
        DX, DC = hi(3072, 2, N_DX), hi(4864, 2, N_DC)
        gG, gE, gkt, gS = ar(6144, 2, TC), ar(7680, 2, TC), ar(9216, 2, T), ar(10240, 2, NCH, P)
        gla_decay = dec[:, 48:64].rearrange("p (a c) -> p a c", a=2)
        gkd, gkd_tok, gqz, gP = hi(0, 2, TC), hi(1536, 6, 256), hi(3072, 4, T), hi(5120, 2, T)
        og = ar(15616, 4, T)
        pq, s_all, xb = ar(0, 16, T), ar(8192, 4, 2048), ar(16384, 4, D)
        down = wring[:, :].rearrange("p (s n) -> p s n", s=RING)
        up = ar(0, RING, D)
        knat, kTr = hi(4096, 16, P), modw[:, 0:2048].rearrange("p (a n) -> p a n", a=16)
        xtok = hi(0, 4, D)
        diag, rowsrc = hi(4096, 16, P), hi(4096, 16, P)
        g2row, nfrow = resid[:, 0:D], resid[:, D:2 * D]
        junk, fin = resid[:, 2 * D:3 * D], resid[:, 3 * D:4 * D]
        idx_all = resid[:, 4096:4608].bitcast(U32)
        g_all = resid[:, 4608:5120]

        def pm(at, n):
            return modw[:, 2048 + at:2048 + at + n]

        s_cur, s_less = pm(0, 256), pm(256, 256)
        onehot = pm(512, 512)
        key_top, key_at = pm(1024, 32), pm(1056, 32).bitcast(U32)
        key_no, chosen = pm(1088, 32), pm(1120, 32)
        cand_at, cand_half = pm(1152, 16).bitcast(U32), pm(1168, 32).bitcast(U32)
        cand_no = pm(1200, 32)
        stage = [pm(1232 + 16 * i, 16).bitcast(U32) for i in range(2)]
        p_top, p_exp, p_dot, p_act, p_w = (pm(1264 + 16 * i, 16) for i in range(5))
        p_neg, p_sum, p_inv, p_ssq, p_std, p_rstd = (pm(1344 + i, 1) for i in range(6))
        cand, cand_less = pm(1360, 256), pm(1616, 256)

        tok_loaded, tok2_loaded = sem("tok_loaded"), sem("tok2_loaded")
        const_loaded, vec_loaded = sem("const_loaded"), sem("vec_loaded")
        dist_loaded, keys_loaded = sem("dist_loaded"), sem("keys_loaded")
        w_loaded = [sem(f"w_loaded{i}") for i in range(2)]
        mod_loaded = [sem(f"mod_loaded{i}") for i in range(2)]
        mod_used = sem("mod_used")
        acc_ready = sem("acc_ready")
        acc_free = [sem(f"acc_free{i}") for i in range(2)]
        rows_zeroed, vec_turned, vec_ready, cond_ready = sem("rows_zeroed"), sem("vec_turned"), sem("vec_ready"), sem("cond_ready")
        sq_ready, sq_used, std_ready, rstd_ready = sem("sq_ready"), sem("sq_used"), sem("std_ready"), sem("rstd_ready")
        h_scaled, h_ready, x1_ready = sem("h_scaled"), sem("h_ready"), sem("x1_ready")
        silu_ready = sem("silu_ready")
        dve_step, act_step = sem("dve_step"), sem("act_step")
        normed = sem("normed")
        copied = sem("copied")
        negmax_ready, exp_ready, prob_ready = sem("negmax_ready"), sem("exp_ready"), sem("prob_ready")
        probT_ready, probT_act, probT_dve = sem("probT_ready"), sem("probT_act"), sem("probT_dve")
        o_ready, o_copied = sem("o_ready"), sem("o_copied")

        mods_ready, conv_ready = sem("mods_ready"), sem("conv_ready")
        pairs_loaded, halves_loaded = sem("pairs_loaded"), sem("halves_loaded")
        decay_abs, decay_exp, la_ready, ln_ready = sem("decay_abs"), sem("decay_exp"), sem("la_ready"), sem("ln_ready")
        dist_arg, dist_exp, dist_done = sem("dist_arg"), sem("dist_exp"), sem("dist_done")
        gla_arg, gla_exp, gla_kd, gla_qk = sem("gla_arg"), sem("gla_exp"), sem("gla_kd"), sem("gla_qk")
        gla_states, gla_o = sem("gla_states"), sem("gla_o")
        rowsrc_ready, tile_read, tile_done = sem("rowsrc_ready"), sem("tile_read"), sem("tile_done")
        down_loaded = [sem(f"down_loaded{i}") for i in range(RING)]
        up_loaded = [sem(f"up_loaded{i}") for i in range(RING)]
        idx_ready, stage_ready, pool_go = sem("idx_ready"), sem("stage_ready"), sem("pool_go")
        top_ready, p_exp_ready, topk_step, dve_go = sem("top_ready"), sem("p_exp_ready"), sem("topk_step"), sem("dve_go")
        dots_done, gelu_ready, weights_ready = sem("dots_done"), sem("gelu_ready"), sem("weights_ready")
        diag_ready, up_used = sem("diag_ready"), sem("up_used")
        ssq_ready, fstd_ready, fin_step, fin_ready = sem("ssq_ready"), sem("fstd_ready"), sem("fin_step"), sem("fin_ready")
        out_stored, inv_ready = sem("out_stored"), sem("inv_ready")

        block = ctx.enter_context(nc.Block())

        class Tally:
            def __init__(self):
                self.sq = self.job = self.step = 0

        def pairs(eng, steps, body, first=0):
            for s in range(first):
                body(s // 2, s % 2)
            if steps // 2 > first // 2:
                with eng.Fori(first // 2, steps // 2) as i:
                    for p in range(2):
                        body(i, p)
            if steps % 2:
                body(steps // 2, 0)

        def emptied(eng, u):
            eng.wait_ge(acc_free[u % 2], u // 2 + CREDIT)

        @block.tensor
        def _(pe):
            n = Tally()
            for p in range(2):
                pe.sem_inc(acc_free[p], 1)

            def begin(u):
                pe.wait_ge(acc_free[u % 2], u // 2 + 1)
                return 2 * (u % 2)

            def product(o, w, x, k, last):
                return nc.tensor.matmul(o, w, x, start=(k == 0), stop=(k == last))

            def stat(tiles, t, weights):
                for j in range(tiles):
                    pe.wait_ge(sq_ready, n.sq + 1)
                    if j == 0 and n.job:
                        pe.wait_ge(std_ready, n.job)
                    s = n.sq % 2
                    if t == T:
                        mm = product(sums[:, 0, :], weights, sq[:, s, 0:T], j, tiles - 1)
                    else:
                        for hf in range(2):
                            mm = product(sums[:, hf, 0:HALF], weights, sq[:, s, hf * HALF:(hf + 1) * HALF], j, tiles - 1)
                    mm.then_inc(sq_used, 1)
                    n.sq += 1
                n.job += 1

            def mod_block(slot, uses, column, block_of):
                pe.wait_ge(mod_loaded[slot], 16 * uses)
                for ct in range(2):
                    for k in range(KD):
                        mm = product(mod_ps[:, ds(column + 2 * ct, 2)], Mw[:, slot, k, ct * P:(ct + 1) * P],
                                     cnd[:, block_of, k, :], k, KD - 1)
                mm.then_inc(mod_used, 1)

            def slot_ready(s):
                pe.wait_ge(w_loaded[s % 2], 32 * (s // 2 + 1))
                return s % 2

            def to_features(u, src):
                b = begin(u)
                for j in range(KD):
                    mm = nc.tensor.transpose(acc[:, b + j // 4, (j % 4) * P:(j % 4 + 1) * P],
                                             src[:, j * P:(j + 1) * P], ident)
                mm.then_inc(acc_ready, 1)

            pe.wait_ge(const_loaded, 16)
            pe.wait_ge(vec_loaded, 16 * N_VEC_DMAS)
            nc.tensor.transpose(misc[:, 0:N_ROWS], rows1[0:N_ROWS, :], ident[0:N_ROWS, 0:N_ROWS])
            nc.tensor.transpose(misc[:, 128:128 + N_BIAS], rows2[0:N_BIAS, :],
                                ident[0:N_BIAS, 0:N_BIAS]).then_inc(vec_turned, 1)
            pe.wait_ge(tok_loaded, 16 * 6)
            for r in range(6):
                to_features(UNIT["tokens"] + r, tok[:, r, :])

            pe.wait_ge(cond_ready, 4)
            with pe.Fori(0, 6) as i:
                for q in range(2):
                    mod_block(q, i + 1, i * 8 + 4 * q, 0)
            stat(KD, TC, ones)

            def ffn_in(name, width, halves, block_of, first_block):
                units = 2 * halves
                src = h768 if halves == 2 else h512
                base, s0 = UNIT[name], SLOT_OF[name]

                def step(i, p):
                    s, it = (s0 + p) % 2, i * 2 + p
                    pe.wait_ge(w_loaded[s], (i + (s0 + p) // 2 + 1) * 32)
                    for q in range(units):
                        sub, hf = q // halves, q % halves
                        u0 = base + p * units + q
                        b = 2 * (u0 % 2)
                        pe.wait_ge(acc_free[u0 % 2], i * units + (u0 // 2 + 1))
                        for m in range(2):
                            for k in range(KD):
                                col = m * 256 + sub * P
                                mm = product(acc[:, b + m, 0:width], Wk[:, s, k, col:col + P],
                                             src[:, k, hf * width:(hf + 1) * width], k, KD - 1)
                        mm.then_inc(acc_ready, 1)
                    for q in range(2):
                        mod_block(q, it + (first_block // 2 + 1), it * 8 + (4 * first_block + 4 * q), block_of)
                pairs(pe, 11, step)
                for q in range(2):
                    mod_block(q, 11 + first_block // 2 + 1, 4 * (first_block + 22 + q), block_of)

            def ffn_out(name, width, halves, ff):
                base, s0 = UNIT[name], SLOT_OF[name]

                def step(i, p):
                    s = (s0 + p) % 2
                    pe.wait_ge(w_loaded[s], (i + (s0 + p) // 2 + 1) * 32)
                    for hf in range(halves):
                        u0 = base + p * halves + hf
                        b = 2 * (u0 % 2)
                        pe.wait_ge(acc_free[u0 % 2], i * halves + (u0 // 2 + 1))
                        for f in range(FT):
                            mm = product(acc[:, b, 0:width], Wf[:, s, f, :],
                                         ff[:, f, hf * width:(hf + 1) * width], f, FT - 1)
                        mm.then_inc(acc_ready, 1)
                emptied(pe, base - 1)
                emptied(pe, base - 2)
                pairs(pe, 8, step)

            pe.wait_ge(h_ready, 8)
            ffn_in("ffn1_in", HALF, 2, 0, 12)
            ffn_out("ffn1_out", HALF, 2, ff768)
            stat(KD, TC, ones)

            pe.wait_ge(h_ready, 16)
            s = slot_ready(SLOT_OF["mix_in"])

            def feature_tile(u, s, col, src, width=T, halves=1, rows=P):
                b = begin(u)
                for hf in range(halves):
                    for k in range(KD):
                        mm = product(acc[0:rows, b + hf, 0:width], Wk[:, s, k, col:col + rows],
                                     src[:, k, hf * width:(hf + 1) * width], k, KD - 1)
                mm.then_inc(acc_ready, 1)

            for t in range(4):
                feature_tile(UNIT["q"] + t, s, t * P, h768)
            s = slot_ready(SLOT_OF["mix_in"] + 1)
            feature_tile(UNIT["k"], s, 0, h768, HALF, 2)
            for v in range(2):
                b = begin(UNIT["v"] + v)
                for r in range(3):
                    at = (3 * v + r) * P
                    for k in range(KD):
                        mm = product(acc[:, b, r * P:(r + 1) * P], h768[:, k, at:at + P], Wk[:, s, k, P:2 * P], k, KD - 1)
                mm.then_inc(acc_ready, 1)
            for g in range(12):
                if g in (2, 6, 10):
                    s = slot_ready(SLOT_OF["mix_in"] + 2 + (g - 2) // 4)
                feature_tile(UNIT["gb"] + g, s, 256 + g * P if g < 2 else ((g - 2) % 4) * P, h768)

            for t in range(4):
                stat(1, T, c_("blk64"))
            stat(1, TC, c_("blk64"))
            for t in range(5):
                u = UNIT["rope_q"] + t
                b = begin(u)
                pe.wait_ge(normed, t + 1)
                nc.tensor.matmul(acc[:, b, :], c_("swap_pairs"), qT[:, t, :] if t < 4 else kT[:, 0:T],
                                 start=True, stop=True).then_inc(acc_ready, 1)
            pe.wait_ge(copied, 5)
            for kv in range(KV_HEADS):
                b = begin(UNIT["kdup"] + kv)
                for hf in range(2):
                    mm = nc.tensor.matmul(acc[:, b + hf, 0:HALF], c_(f"dup{kv}"), kT[:, hf * HALF:(hf + 1) * HALF],
                                          start=True, stop=True)
                mm.then_inc(acc_ready, 1)
            stat(4, T, ones)

            pe.wait_ge(std_ready, n.job)
            emptied(pe, UNIT["kdup"])
            emptied(pe, UNIT["kdup"] + 1)

            def scores(u):
                h, t = u // 4, u % 4
                b = begin(UNIT["scores"] + u)
                rows = slice(64 * (h % 2), 64 * (h % 2) + 64)
                for hf in range(2):
                    mm = nc.tensor.matmul(acc[:, b + hf, 0:HALF], qT[rows, h // 2, t * P:(t + 1) * P],
                                          kdup[rows, h // 4, hf * HALF:(hf + 1) * HALF], start=True, stop=True)
                mm.then_inc(acc_ready, 1)

            def turn(u):
                pe.wait_ge(prob_ready, u + 1)
                if u:
                    pe.wait_ge(probT_act, u)
                    pe.wait_ge(probT_dve, u)
                for r in range(6):
                    mm = nc.tensor.transpose(sums[:, r // 3, (r % 3) * P:(r % 3 + 1) * P],
                                             prob[:, u % 3, r * P:(r + 1) * P], ident)
                mm.then_inc(probT_ready, 1)

            def outputs(h):
                pe.wait_ge(probT_act, 4 * (h + 1))
                pe.wait_ge(probT_dve, 4 * (h + 1))
                if h:
                    pe.wait_ge(o_copied, h)
                at, kv = 64 * (h % 2), h // 4
                for r in range(6):
                    mm = product(misc[at:at + 64, :], vtok[:, r, kv * HD:(kv + 1) * HD], probT[:, h % 2, r, :], r, 5)
                mm.then_inc(o_ready, 1)

            for step in range(32 + 3):
                if step < 32:
                    scores(step)
                if 2 <= step < 34:
                    turn(step - 2)
                if step >= 6 and (step - 6) % 4 == 0:
                    outputs((step - 6) // 4)
            stat(4, T, ones)

            def gemm512(name, slot_name, tiles, src):
                for t in range(tiles):
                    if t % 4 == 0:
                        s = slot_ready(SLOT_OF[slot_name] + t // 4)
                    feature_tile(UNIT[name] + t, s, (t % 4) * P, src)

            pe.wait_ge(normed, 5 + 8)
            gemm512("mix_out", "mix_out", 8, mixT)
            stat(KD, T, ones)

            pe.wait_ge(h_ready, 24)
            ffn_in("ffn2_in", T, 1, 1, ADA_BLOCKS)
            ffn_out("ffn2_out", T, 1, ff512)
            pe.wait_ge(tok2_loaded, 32)
            for r in range(2):
                to_features(UNIT["tokens2"] + r, tok2[:, r, :])
            stat(KD, T, ones)
            stat(KD, TC, ones)

            pe.wait_ge(h_ready, 32)
            p0 = SLOT_OF["proj"]

            def token_tiles(name, s):
                for r in range(6):
                    b = begin(UNIT[name] + r)
                    for k in range(KD):
                        mm = product(acc[:, b, :], h768[:, k, r * P:(r + 1) * P], Wk[:, s, k, :], k, KD - 1)
                    mm.then_inc(acc_ready, 1)

            s = slot_ready(p0)
            for t in range(4):
                feature_tile(UNIT["rq"] + t, s, t * P, h768)
            s = slot_ready(p0 + 1)
            for t in range(4):
                feature_tile(UNIT["rk"] + t, s, t * P, h768, HALF, 2)
            token_tiles("rv", slot_ready(p0 + 2))
            s = slot_ready(p0 + 3)
            for t in range(4):
                feature_tile(UNIT["rg"] + t, s, t * P, h768)
            s = slot_ready(p0 + 4)
            for t in range(2):
                feature_tile(UNIT["gq"] + t, s, t * P, h768)
            for t in range(2):
                feature_tile(UNIT["gk"] + t, s, 256 + t * P, h768, HALF, 2)
            token_tiles("gv", slot_ready(p0 + 5))
            s = slot_ready(p0 + 6)
            for t in range(4):
                feature_tile(UNIT["gg"] + t, s, t * P, h768)
            s = slot_ready(p0 + 7)
            b = begin(UNIT["lr"])
            for hf in range(2):
                for k in range(KD):
                    mm = product(acc[0:32, b + hf, 0:HALF], Wlr[:, s, k, :], h768[:, k, hf * HALF:(hf + 1) * HALF], k, KD - 1)
            mm.then_inc(acc_ready, 1)

            for t in range(8):
                src = rq[:, t, :] if t < 4 else rk[:, t - 4, 0:T]
                emptied(pe, UNIT["rq"] + t)
                b = begin(UNIT["rope_r"] + t)
                nc.tensor.matmul(acc[:, b, :], c_("swap_halves"), src, start=True, stop=True).then_inc(acc_ready, 1)
            emptied(pe, UNIT["lr"])
            for u in range(4):
                b = begin(UNIT["decay"] + u)
                at = (u // 2) * 256 + (u % 2) * P
                for hf in range(2):
                    mm = nc.tensor.matmul(acc[:, b + hf, 0:HALF], gkup[:, at:at + P], lr[:, hf * HALF:(hf + 1) * HALF],
                                          start=True, stop=True)
                mm.then_inc(acc_ready, 1)
            pe.wait_ge(copied, 5 + 8)
            outs = [misc, mod_ps]

            def ret_scores(u):
                h, r = u // 6, u % 6
                b = begin(UNIT["ret"] + u)
                nc.tensor.matmul(acc[:, b, :], rk[:, h, r * P:(r + 1) * P], rq[:, h, :],
                                 start=True, stop=True).then_inc(acc_ready, 1)

            def ret_outputs(u):
                h, r = u // 6, u % 6
                emptied(pe, UNIT["ret"] + u)
                if r == 0 and h >= 2:
                    pe.wait_ge(o_copied, 8 + h - 1)
                mm = product(outs[h % 2][:, :], rv[:, r, h * P:(h + 1) * P], retP[:, u % 2, :], r, 5)
                mm.then_inc(o_ready, 1)

            for u in range(25):
                if u < 24:
                    ret_scores(u)
                if u >= 1:
                    ret_outputs(u - 1)
            for h in range(4):
                stat(1, T, ones)

            banks = [mod_ps[:, :], misc[:, :], sums[:, 0, :], sums[:, 1, :]]
            pe.wait_ge(std_ready, n.job)
            pe.wait_ge(o_copied, 12)
            for d in range(2):
                base = UNIT[f"gla{d}"]
                for pr in range(2):
                    pe.wait_ge(gla_kd, 2 * d + pr + 1)
                    b = begin(base + pr)
                    for r in range(6):
                        mm = nc.tensor.transpose(acc[:, b + r // 4, (r % 4) * P:(r % 4 + 1) * P],
                                                 gkd[:, pr, r * P:(r + 1) * P], ident)
                    mm.then_inc(acc_ready, 1)
                emptied(pe, base)
                emptied(pe, base + 1)
                b = begin(base + 2)
                for pr in range(2):
                    for hh in range(2):
                        h, at = 2 * pr + hh, pr * P + hh * 64
                        for r in range(2):
                            mm = product(acc[hh * 64:hh * 64 + 64, b, pr * P:(pr + 1) * P], gkd_tok[:, 4 + r, at:at + 64],
                                         gv[:, 4 + r, h * P:(h + 1) * P], r, 1)
                mm.then_inc(acc_ready, 1)
                for pr in range(2):
                    b = begin(base + 3 + pr)
                    for c in range(NCH):
                        rows = slice(64 * (c % 2), 64 * (c % 2) + 64)
                        for hh in range(2):
                            h, at = 2 * pr + hh, pr * P + hh * 64
                            mm = nc.tensor.matmul(acc[hh * 64:hh * 64 + 64, b + c % 2, (c // 2) * P:(c // 2 + 1) * P],
                                                  gkd_tok[rows, c // 2, at:at + 64], gv[rows, c // 2, h * P:(h + 1) * P],
                                                  start=True, stop=True)
                    mm.then_inc(acc_ready, 1)
                def gla_out(h):
                    emptied(pe, base + 5 + h)
                    for r in range(4):
                        nc.tensor.matmul(banks[h][:, r * P:(r + 1) * P], gv[:, r, h * P:(h + 1) * P],
                                         gP[:, h % 2, r * P:(r + 1) * P], start=(d == 0 and r == 0), stop=False,
                                         skip_group_check=True)
                    for c in range(NCH):
                        mm = nc.tensor.matmul(banks[h][:, c * 64:c * 64 + 64], gS[:, h // 2, c, :],
                                              gqz[:, h, c * 64:c * 64 + 64], start=False,
                                              stop=(d == 1 and c == NCH - 1), skip_group_check=True)
                    mm.then_inc(gla_o, 1)

                pe.wait_ge(gla_qk, 6 * (d + 1))
                for h in range(4):
                    b = begin(base + 5 + h)
                    for r in range(4):
                        mm = nc.tensor.matmul(acc[:, b, r * P:(r + 1) * P], gkt[:, h // 2, r * P:(r + 1) * P],
                                              gqz[:, h, r * P:(r + 1) * P], start=True, stop=True)
                    mm.then_inc(acc_ready, 1)
                    if h == 0:
                        pe.wait_ge(gla_states, 12 * (d + 1))
                        emptied(pe, base + 3)
                        emptied(pe, base + 4)
                    else:
                        gla_out(h - 1)
                gla_out(3)
            pe.wait_ge(o_copied, 16)
            for h in range(4):
                stat(1, T, ones)

            pe.wait_ge(normed, 5 + 8 + 8)
            gemm512("w_out", "w_out", 8, yT)
            stat(KD, T, ones)
            pe.wait_ge(h_ready, 40)
            gemm512("peer_q", "peer_q", 16, h512)
            pe.wait_ge(keys_loaded, 32)
            for g in range(2):
                b = begin(UNIT["keys"] + g)
                for j in range(8):
                    mm = nc.tensor.transpose(acc[:, b + j // 4, (j % 4) * P:(j % 4 + 1) * P], knat[:, 8 * g + j, :], ident)
                mm.then_inc(acc_ready, 1)
            emptied(pe, UNIT["keys"])
            emptied(pe, UNIT["keys"] + 1)
            for u in range(8):
                b = begin(UNIT["peer_s"] + u)
                for j in range(8):
                    a8 = 8 * (u % 2) + j
                    mm = nc.tensor.matmul(acc[:, b + j // 4, (j % 4) * P:(j % 4 + 1) * P],
                                          pq[:, a8, (u // 2) * P:(u // 2 + 1) * P], kTr[:, a8, :], start=True, stop=True)
                mm.then_inc(acc_ready, 1)
            for name, src in (("xb", h512), ("xtok", x_)):
                for t in range(4):
                    b = begin(UNIT[name] + t)
                    for j in range(KD):
                        mm = nc.tensor.transpose(acc[:, b + j // 4, (j % 4) * P:(j % 4 + 1) * P],
                                                 src[:, j, t * P:(t + 1) * P], ident)
                    mm.then_inc(acc_ready, 1)
            pe.wait_ge(rowsrc_ready, 16)
            for w in range(2):
                b = begin(UNIT["rows"] + w)
                for j in range(KD):
                    mm = nc.tensor.matmul(acc[:, b + j // 4, (j % 4) * P:(j % 4 + 1) * P], rowsrc[:, (w * KD + j), :],
                                          ident, start=True, stop=True)
                mm.then_inc(acc_ready, 1)
            emptied(pe, UNIT["rows"])
            emptied(pe, UNIT["rows"] + 1)

            with pe.Fori(0, 4) as t:
                pe.wait_ge(tile_read, t + 1)
                for hf in range(2):
                    nc.tensor.matmul(acc[:, hf, :], c_("zero"), cst[:, 0:512], start=True, stop=False, skip_group_check=True)
                with pe.Fori(0, PEER_H) as h:
                    for k in range(PEER_K):
                        pe.wait_ge(diag_ready, (t * PEER_H + h) * PEER_K + (k + 1))
                        pe.wait_ge(up_loaded[k % RING], (t * PEER_H + h) * 32 + (16 * (k // RING) + 16))
                        for hf in range(2):
                            mm = nc.tensor.matmul(acc[:, hf, :], diag[:, k, :], up[:, k % RING, hf * 512:(hf + 1) * 512],
                                                  start=False, stop=False, skip_group_check=True)
                        mm.then_inc(up_used, 1)
                for hf in range(2):
                    mm = nc.tensor.matmul(acc[:, hf, :], c_("zero"), cst[:, 0:512], start=False, stop=True, skip_group_check=True)
                mm.then_inc(tile_done, 1)

        @block.scalar
        def _(act):
            n = Tally()

            def link(ins):
                n.step += 1
                ins.then_inc(act_step, 1)
                act.wait_ge(act_step, n.step)

            def run(o, i, func, **kw):
                return nc.scalar.activation(o, i, func, **kw)

            def unit(u):
                act.wait_ge(acc_ready, u + 1)
                return 2 * (u % 2)

            def wide(b, cols=1024):
                return acc[:, b:b + 2, :].rearrange("p a n -> p (a n)")[:, 0:cols]

            def stat(tiles, t, inv_n, source):
                for j in range(tiles):
                    if n.sq >= 2:
                        act.wait_ge(sq_used, n.sq - 1)
                    run(sq[:, n.sq % 2, 0:t], source(j), ACT.Square).then_inc(sq_ready, 1)
                    n.sq += 1
                act.wait_ge(sq_used, n.sq)
                if n.job:
                    act.wait_ge(rstd_ready, n.job)
                n.job += 1
                if t == T:
                    ins = run(std[:, 0:T], sums[:, 0, :], ACT.Sqrt, scale=inv_n, bias=c_("eps"))
                else:
                    ins = run(std[:, :].rearrange("p (a t) -> p a t", a=2), sums[:, :, 0:HALF], ACT.Sqrt,
                              scale=inv_n, bias=c_("eps"))
                ins.then_inc(std_ready, 1)

            def shift(norm, hid_, tile, t, stage):
                act.wait_ge(mods_ready, stage)
                for j in range(KD):
                    act.wait_ge(h_scaled, 8 * norm + j + 1)
                    ins = run(hid_[:, j, 0:T], hid_[:, j, 0:T], ACT.Identity, bias=mod[:, tile + j, 0:1])
                    if t == TC:
                        ins = run(hid_[:, j, T:TC], hid_[:, j, T:TC], ACT.Identity, bias=mod[:, tile + j, 1:2])
                    ins.then_inc(h_ready, 1)

            def silus(name, width, halves):
                units, base = 2 * halves, UNIT[name]

                def step(i, p):
                    for q in range(units):
                        u0 = base + p * units + q
                        act.wait_ge(acc_ready, i * 2 * units + (u0 + 1))
                        run(sg[:, u0 % 2, 0:width], acc[:, 2 * (u0 % 2), 0:width], ACT.Silu).then_inc(silu_ready, 1)
                pairs(act, 11, step)

            act.dma_start(cst[:, :], a["const"]).then_inc(const_loaded, 16)
            for name in ("c", "c_ctx", "norm_ffn1", "norm_mix", "attn_out_norm", "conv_out_norm", "norm_ffn2",
                         "final_norm", "c_2", "c_ctx_2", "norm1_w_2", "norm2_w_2", "norm_f_w_2",
                         "gla_gk_bias_f_2", "gla_gk_bias_b_2"):
                at, rows = ROWS[name]
                act.dma_start(rows1[at:at + rows, :], flat(a[name]).rearrange("(r q) -> r q", q=P)).then_inc(vec_loaded, 16)
            at, rows = ROWS["conv_w"]
            act.dma_start(rows1[at:at + rows, :], a["conv_w"].rearrange("l k (j q) -> (l k j) q", q=P)).then_inc(vec_loaded, 16)
            for name in ("q_norm", "k_norm"):
                for hf in range(2):
                    at = ROWS[name][0]
                    act.dma_start(rows1[at:at + 1, hf * 64:(hf + 1) * 64], a[name]).then_inc(vec_loaded, 16)
            act.dma_start(rows2[0:ADA_TILES, :], flat(a["b_ada"]).rearrange("(r q) -> r q", q=P)).then_inc(vec_loaded, 16)
            act.dma_start(rows2[ADA_TILES:N_BIAS, :], flat(a["b_mod_2"]).rearrange("(r q) -> r q", q=P)).then_inc(vec_loaded, 16)
            act.dma_start(dec[:, 0:4], a["ret_decay_f_2"].to_broadcast([P, 4])).then_inc(vec_loaded, 16)
            act.dma_start(dec[:, 4:8], a["ret_decay_b_2"].to_broadcast([P, 4])).then_inc(vec_loaded, 16)
            act.wait_ge(rows_zeroed, 1)
            act.dma_start(gkup[0:16, 0:256], a["gla_gk_up_f_2"][0]).then_inc(vec_loaded, 16)
            act.dma_start(gkup[16:32, 256:512], a["gla_gk_up_b_2"][0]).then_inc(vec_loaded, 16)

            act.wait_ge(vec_ready, 1)
            for blk, pair in enumerate((("c", "c_ctx"), ("c_2", "c_ctx_2"))):
                for w, name in enumerate(pair):
                    run(cnd[:, blk, :, w], v_(name, 0, KD), ACT.Silu).then_inc(cond_ready, 1)
            act.wait_ge(decay_abs, 1)
            run(dec[:, 16:24], dec[:, 8:16], ACT.Exp, scale=-1.0).then_inc(decay_exp, 1)
            for r in range(1, 6, 2):
                u = UNIT["tokens"] + r
                b = unit(u)
                run(x_[:, :, r * P:(r + 1) * P], wide(b).rearrange("p (j t) -> p j t", j=KD), ACT.Copy).then_inc(acc_free[u % 2], 1)

            emptied(act, UNIT["tokens"] + 4)
            emptied(act, UNIT["tokens"] + 5)
            stat(KD, TC, 1.0 / D, lambda j: x_[:, j, :])
            shift(0, h768, 0, TC, 1)
            silus("ffn1_in", HALF, 2)

            def updated(name, j, units):
                for q in range(units):
                    emptied(act, UNIT[name] + units * j + q)
                return x_[:, j, :] if units == 2 else x_[:, j, 0:T]

            stat(KD, TC, 1.0 / D, lambda j: updated("ffn1_out", j, 2))
            shift(1, h768, 3 * KD, TC, 2)

            def take(name, t, o, func=ACT.Copy, cols=T):
                u = UNIT[name] + t
                b = unit(u)
                src = acc[:, b, 0:T] if cols == T else acc[:, b:b + 2, 0:HALF]
                run(o, src, func).then_inc(acc_free[u % 2], 1)

            def halves(o):
                return o.rearrange("p (a t) -> p a t", a=2)

            for t in range(4):
                take("q", t, qT[:, t, :])
            take("k", 0, halves(kT), cols=TC)
            for v in range(2):
                u = UNIT["v"] + v
                b = unit(u)
                run(vtok[:, 3 * v:3 * v + 3, :], acc[:, b, 0:3 * P].rearrange("p (r n) -> p r n", r=3), ACT.Copy).then_inc(acc_free[u % 2], 1)
            for t in range(4):
                take("gb", t, gb[:, t, :])
            for t in range(4):
                take("gc", t, gc[:, t, :])

            def own(u, src):
                emptied(act, u)
                return src

            for t in range(4):
                stat(1, T, 1.0 / HD, lambda j, t=t: own(UNIT["q"] + t, qT[:, t, :]))
            stat(1, TC, 1.0 / HD, lambda j: own(UNIT["k"], kT))
            for kv in range(KV_HEADS):
                take("kdup", kv, halves(kdup[:, kv, :]), cols=TC)

            def branch(j):
                act.wait_ge(conv_ready, j + 1)
                return mixT[:, 4 + j, :]
            stat(4, T, 1.0 / 512, branch)

            for step in range(32 + 4):
                if step < 32:
                    u = UNIT["scores"] + step
                    act.wait_ge(negmax_ready, step + 1)
                    if step >= 3:
                        act.wait_ge(probT_ready, step - 2)
                    b = unit(u)
                    run(halves(prob[:, step % 3, :]), acc[:, b:b + 2, 0:HALF], ACT.Exp, scale=HD ** -0.5,
                        bias=small[:, step % 2:step % 2 + 1], accum_out=small[:, 2 + step % 2:3 + step % 2]).then_inc(exp_ready, 1)
                if 3 <= step < 35:
                    u = step - 3
                    act.wait_ge(probT_ready, u + 1)
                    if u >= 8:
                        act.wait_ge(o_ready, u // 4 - 1)
                    run(probT[:, (u // 4) % 2, 0:3, (u % 4) * P:(u % 4 + 1) * P],
                        sums[:, 0, 0:HALF].rearrange("p (r n) -> p r n", r=3), ACT.Copy).then_inc(probT_act, 1)
                if step >= 7 and (step - 7) % 4 == 0 or step == 35:
                    h = (step - 7) // 4
                    act.wait_ge(o_ready, h + 1)
                    rows = slice(64 * (h % 2), 64 * (h % 2) + 64)
                    run(mixT[rows, h // 2, :], misc[rows, :], ACT.Copy).then_inc(o_copied, 1)

            def heads(j):
                act.wait_ge(o_copied, 8)
                return mixT[:, j, :]
            stat(4, T, 1.0 / 512, heads)

            stat(KD, T, 1.0 / D, lambda j: updated("mix_out", j, 1))
            shift(2, h512, 6 * KD, T, 2)
            silus("ffn2_in", T, 1)
            stat(KD, T, 1.0 / D, lambda j: updated("ffn2_out", j, 1))

            def renormed(j):
                act.wait_ge(x1_ready, j + 1)
                emptied(act, UNIT["tokens2"])
                emptied(act, UNIT["tokens2"] + 1)
                return x_[:, j, :]
            stat(KD, TC, 1.0 / D, renormed)
            shift(3, h768, ADA_TILES, TC, 3)

            for t in range(4):
                take("rq", t, rq[:, t, :])
            for t in range(4):
                take("rk", t, halves(rk[:, t, :]), cols=TC)
            for t in range(4):
                take("rg", t, yT[:, t, :], ACT.Silu)
            for t in range(2):
                take("gq", t, gq[:, t, :])
            for t in range(2):
                take("gk", t, halves(gk[:, t, :]), cols=TC)
            for t in range(4):
                take("gg", t, yT[:, 4 + t, :], ACT.Silu)

            soft = sq[:, 0, :]
            for u in range(4):
                emptied(act, UNIT["decay"] + u)
                if u:
                    act.wait_ge(la_ready, u)
                link(run(soft, la[:, u // 2, u % 2, :], ACT.Abs))
                link(run(soft, soft, ACT.Exp, scale=-1.0))
                run(soft, soft, ACT.Ln, bias=1.0).then_inc(ln_ready, 1)

            def ret_out(h):
                act.wait_ge(o_ready, 8 + 6 * (h + 1))
                run(rq[:, h, :], [misc, mod_ps][h % 2][:, :], ACT.Copy).then_inc(o_copied, 1)

            for h in range(4):
                act.wait_ge(dist_arg, h + 1)
                if h:
                    act.wait_ge(dist_done, h)
                run(DX[:, h % 2, :], DX[:, h % 2, :], ACT.Exp)
                run(DC[:, h % 2, :], dist[:, 2 * N_DX:2 * N_DX + N_DC], ACT.Exp, scale=dec[:, 8 + h:9 + h])
                run(sq[:, 1, 0:N_DC], dist[:, 2 * N_DX + N_DC:], ACT.Exp, scale=dec[:, 12 + h:13 + h]).then_inc(dist_exp, 1)
                if h:
                    ret_out(h - 1)
            ret_out(3)
            for h in range(4):
                def head(j, h=h):
                    act.wait_ge(o_copied, 9 + h)
                    return rq[:, h, :]
                stat(1, T, 1.0 / P, head)

            for d in range(2):
                base = UNIT[f"gla{d}"]
                e = (gE if d == 0 else gkd)[:, :, 0:T]
                g = (gG if d == 0 else gE)[:, :, 0:T]
                act.wait_ge(gla_arg, 2 * d + 1)
                run(gla_decay,
                    gG[:, :, 0:T].rearrange("p a (c i) -> p a c i", i=CHUNK)[:, :, :, CHUNK - 1],
                    ACT.Exp, scale=1.0 / GATE_NORM)
                if d:
                    act.wait_ge(acc_ready, UNIT["gla0"] + 2)
                run(e, g, ACT.Exp, scale=1.0 / GATE_NORM).then_inc(gla_exp, 1)
                act.wait_ge(gla_qk, 6 * d + 4)
                run(e, g, ACT.Exp, scale=-1.0 / GATE_NORM).then_inc(gla_exp, 1)
                act.wait_ge(gla_arg, 2 * d + 2)
                run(gE, gE, ACT.Exp, scale=1.0 / GATE_NORM).then_inc(gla_exp, 1)
                for pr in range(2):
                    u = base + pr
                    b = unit(u)
                    run(gkd_tok[:, :, pr * P:(pr + 1) * P], wide(b, 6 * P).rearrange("p (r n) -> p r n", r=6),
                        ACT.Copy).then_inc(acc_free[u % 2], 1)
            banks = [mod_ps[:, :], misc[:, :], sums[:, 0, :], sums[:, 1, :]]
            for h in range(4):
                act.wait_ge(gla_o, 4 + h + 1)
                run(og[:, h, :], banks[h], ACT.Copy).then_inc(o_copied, 1)
            for h in range(4):
                def head(j, h=h):
                    act.wait_ge(o_copied, 13 + h)
                    return og[:, h, :]
                stat(1, T, 1.0 / P, head)

            stat(KD, T, 1.0 / D, lambda j: updated("w_out", j, 1))
            shift(4, h512, ADA_TILES + 3 * KD, T, 3)
            for t in range(0, 16, 2):
                take("peer_q", t, pq[:, t, :])
            for u0 in range(0, 8, 2):
                u = UNIT["peer_s"] + u0
                b = unit(u)
                run(s_all[:, u0 // 2, 0:1024], wide(b), ACT.Copy).then_inc(acc_free[u % 2], 1)
            for name, dst in (("xb", xb), ("xtok", xtok)):
                for t in range(0, 4, 2):
                    u = UNIT[name] + t
                    b = unit(u)
                    run(dst[:, t, :], wide(b), ACT.Copy).then_inc(acc_free[u % 2], 1)
            for w, dst in enumerate((g2row, nfrow)):
                u = UNIT["rows"] + w
                b = unit(u)
                run(dst, wide(b), ACT.Copy).then_inc(acc_free[u % 2], 1)

            def softmax_exp(count):
                act.wait_ge(top_ready, count)
                run(p_exp, p_top, ACT.Exp, bias=p_neg, accum_out=p_sum).then_inc(p_exp_ready, 1)

            def expert_weights(i):
                act.wait_ge(dots_done, (i + 1) * PEER_K + RING)
                run(p_act, p_dot, ACT.Gelu).then_inc(gelu_ready, 1)
                act.wait_ge(weights_ready, i + 1)
                for k in range(PEER_K):
                    act.wait_ge(up_used, i * PEER_K + (k + 1))
                    run(diag[:, k, :], ident, ACT.Copy, scale=p_w[:, k:k + 1]).then_inc(diag_ready, 1)

            def final_std(t):
                act.wait_ge(ssq_ready, t + 1)
                run(p_std, p_ssq, ACT.Sqrt, scale=1.0 / D, bias=c_("eps")).then_inc(fstd_ready, 1)

            with act.Fori(0, PEER_H) as h:
                softmax_exp(h + 1)
            with act.Fori(0, 3) as t:
                with act.Fori(0, PEER_H) as h:
                    softmax_exp(t * PEER_H + (h + (PEER_H + 1)))
                    expert_weights(t * PEER_H + h)
                final_std(t)
            with act.Fori(0, PEER_H) as h:
                expert_weights(h + 3 * PEER_H)
            final_std(3)

        @block.vector
        def _(dve):
            n = Tally()
            V = nc.vector

            def link(ins):
                n.step += 1
                ins.then_inc(dve_step, 1)
                dve.wait_ge(dve_step, n.step)

            def unit(u):
                dve.wait_ge(acc_ready, u + 1)
                return 2 * (u % 2)

            def free(ins, u):
                ins.then_inc(acc_free[u % 2], 1)

            def wide(b, cols=1024):
                return acc[:, b:b + 2, :].rearrange("p a n -> p (a n)")[:, 0:cols]

            def halves(o):
                return o.rearrange("p (a t) -> p a t", a=2)

            def stat(t):
                n.job += 1
                dve.wait_ge(std_ready, n.job)
                V.reciprocal(rstd[:, 0:t], std[:, 0:t]).then_inc(rstd_ready, 1)
                dve.wait_ge(rstd_ready, n.job)

            def scale(norm, hid_, t):
                for j in range(KD):
                    ins = V.scalar_tensor_tensor(hid_[:, j, 0:T], x_[:, j, 0:T], gain[:, norm, j, 0:1], rstd[:, 0:T],
                                                 ALU.mult, ALU.mult)
                    if t == TC:
                        ins = V.scalar_tensor_tensor(hid_[:, j, T:TC], x_[:, j, T:TC], gain[:, norm, j, 1:2], rstd[:, T:TC],
                                                     ALU.mult, ALU.mult)
                    ins.then_inc(h_scaled, 1)

            def modulation(stage, first, last, used, gain_of, half_of):
                dve.wait_ge(mod_used, CREDIT + used)
                link(V.tensor_tensor(mod[:, first:last, :],
                                     mod_ps[:, 2 * first:2 * last].rearrange("p (t c) -> p t c", c=2),
                                     vec[:, 128 + first:128 + last].unsqueeze(2).to_broadcast([P, last - first, 2]), ALU.add))
                for norm, name, tile in gain_of:
                    ins = V.scalar_tensor_tensor(gain[:, norm], mod[:, tile:tile + KD, :], 1.0,
                                                 v_(name, 0, KD).unsqueeze(2).to_broadcast([P, KD, 2]), ALU.add, ALU.mult)
                for ffn, tile in half_of:
                    ins = V.tensor_scalar(hgate[:, ffn], mod[:, tile:tile + KD, :], 0.5, None, ALU.mult)
                ins.then_inc(mods_ready, 1)
                dve.wait_ge(mods_ready, stage)

            def swiglu(name, width, sides, done):
                units, base = 2 * sides, UNIT[name]

                def step(i, p):
                    for q in range(units):
                        u0 = base + p * units + q
                        sub, hf = q // sides, q % sides
                        dve.wait_ge(silu_ready, i * 2 * units + (done + p * units + q + 1))
                        free(V.tensor_tensor(arena[:, ds(i * 4 * width * sides + ((2 * p + sub) * sides + hf) * width, width)],
                                             sg[:, u0 % 2, 0:width], acc[:, 2 * (u0 % 2) + 1, 0:width], ALU.mult), u0)
                pairs(dve, 11, step)

            def residual(name, sides, ffn):
                base = UNIT[name]

                def step(i, p):
                    for hf in range(sides):
                        u0 = base + p * sides + hf
                        dve.wait_ge(acc_ready, i * 2 * sides + (u0 + 1))
                        at, b = 0, 2 * (u0 % 2)
                        parts = [(0, 0, T)] if sides == 1 else [(0, 0, HALF)] if hf == 0 else [(0, HALF, T), (1, T, TC)]
                        for kind, lo, hi_ in parts:
                            x1 = resid[:, ds(i * 2 * TC + (p * TC + lo), hi_ - lo)]
                            ins = V.scalar_tensor_tensor(x1, acc[:, b, at:at + hi_ - lo],
                                                         halfg[:, ds(i * 4 + (16 * ffn + 2 * p + kind), 1)], x1,
                                                         ALU.mult, ALU.add)
                            at += hi_ - lo
                        free(ins, u0)
                pairs(dve, KD, step)

            V.memset(gkup[:, :], 0.0).then_inc(rows_zeroed, 1)
            dve.wait_ge(vec_turned, 1)
            V.tensor_copy(vec[:, 0:N_ROWS], misc[:, 0:N_ROWS])
            V.tensor_copy(vec[:, 128:128 + N_BIAS], misc[:, 128:128 + N_BIAS]).then_inc(vec_ready, 1)
            dve.wait_ge(vec_ready, 1)
            dve.wait_ge(vec_loaded, 16 * N_VEC_DMAS)
            V.scalar_tensor_tensor(dec[:, 8:16], dec[:, 0:8], -1.0, dec[:, 0:8], ALU.mult, ALU.max).then_inc(decay_abs, 1)
            dve.wait_ge(decay_exp, 1)
            z, s_, s2, series, least = (dec[:, 16 + 8 * i:24 + 8 * i] for i in range(5))
            link(V.tensor_scalar(s2, z, 2.0, None, ALU.add))
            link(V.reciprocal(s2, s2))
            link(V.tensor_tensor(s_, z, s2, ALU.mult))
            link(V.tensor_tensor(s2, s_, s_, ALU.mult))
            link(V.tensor_scalar(series, s2, 1.0 / 19, None, ALU.mult))
            for odd in range(17, 1, -2):
                link(V.scalar_tensor_tensor(series, series, 1.0 / odd, s2, ALU.add, ALU.mult))
            link(V.scalar_tensor_tensor(series, series, 1.0, s_, ALU.add, ALU.mult))
            link(V.tensor_scalar(least, dec[:, 0:8], 0.0, None, ALU.min))
            link(V.scalar_tensor_tensor(dec[:, 8:16], series, -2.0, least, ALU.mult, ALU.add))

            for r in range(0, 6, 2):
                u = UNIT["tokens"] + r
                b = unit(u)
                free(V.tensor_copy(x_[:, :, r * P:(r + 1) * P], wide(b).rearrange("p (j t) -> p j t", j=KD)), u)

            modulation(1, 0, 3 * KD, 12, [(0, "norm_ffn1", KD)], [(0, 2 * KD)])
            stat(TC)
            scale(0, h768, TC)
            swiglu("ffn1_in", HALF, 2, 0)
            modulation(2, 3 * KD, ADA_TILES, ADA_BLOCKS, [(1, "norm_mix", 4 * KD), (2, "norm_ffn2", 7 * KD)], [(1, 8 * KD)])
            residual("ffn1_out", 2, 0)
            stat(TC)
            scale(1, h768, TC)

            V.memset(cu[:, :, 0:1], 0.0)
            V.memset(cu[:, :, T + 1:T + 2], 0.0)
            for t in range(4):
                u = UNIT["u"] + t
                emptied(dve, UNIT["gc"] + t)
                b = unit(u)
                free(V.tensor_tensor(cu[:, t, 1:T + 1], acc[:, b, :], gc[:, t, :], ALU.mult), u)
            for t in range(5):
                width, dst = (T, qT[:, t, :]) if t < 4 else (TC, kT)
                if t:
                    dve.wait_ge(normed, t)
                stat(width)
                V.scalar_tensor_tensor(dst, dst, v_("q_norm" if t < 4 else "k_norm"), rstd[:, 0:width],
                                       ALU.mult, ALU.mult).then_inc(normed, 1)

            def rope(u, dst, cos, sin, before):
                b = unit(u)
                if before:
                    dve.wait_ge(copied, before)
                free(V.tensor_tensor(tmp[:, 0:T], acc[:, b, :], sin, ALU.mult), u)
                link(V.tensor_tensor(dst, dst, cos, ALU.mult))
                V.tensor_tensor(dst, dst, tmp[:, 0:T], ALU.add).then_inc(copied, 1)

            dve.wait_ge(pairs_loaded, 16)
            for t in range(5):
                rope(UNIT["rope_q"] + t, qT[:, t, :] if t < 4 else kT[:, 0:T], cos_pairs, sin_pairs, t)
            for t in range(4):
                y = mixT[:, 4 + t, :]
                emptied(dve, UNIT["gb"] + t)
                link(V.tensor_scalar(y, cu[:, t, 0:T], v_("conv_w", t), None, ALU.mult))
                for tap in (1, 2):
                    link(V.scalar_tensor_tensor(y, cu[:, t, tap:tap + T], v_("conv_w", tap * 4 + t), y, ALU.mult, ALU.add))
                V.tensor_tensor(y, y, gb[:, t, :], ALU.mult).then_inc(conv_ready, 1)

            def branch_norm(first, name):
                stat(T)
                for t in range(4):
                    y = mixT[:, first + t, :]
                    V.scalar_tensor_tensor(y, y, v_(name, t), rstd[:, 0:T], ALU.mult, ALU.mult).then_inc(normed, 1)
            branch_norm(4, "conv_out_norm")

            for step in range(32 + 3):
                if step < 32:
                    b = unit(UNIT["scores"] + step)
                    top = small[:, 8 + step % 2:9 + step % 2]
                    link(V.tensor_reduce(top, acc[:, b:b + 2, 0:HALF], mybir.AxisListType.XY, ALU.max))
                    V.tensor_scalar(small[:, step % 2:step % 2 + 1], top, -HD ** -0.5, None, ALU.mult).then_inc(negmax_ready, 1)
                if 1 <= step < 33:
                    u = step - 1
                    inv = small[:, 16 + u % 4:17 + u % 4]
                    dve.wait_ge(exp_ready, u + 1)
                    free(V.reciprocal(inv, small[:, 2 + u % 2:3 + u % 2]), UNIT["scores"] + u)
                    emptied(dve, UNIT["scores"] + u)
                    V.tensor_scalar(prob[:, u % 3, :], prob[:, u % 3, :], inv, None, ALU.mult).then_inc(prob_ready, 1)
                if step >= 3:
                    u = step - 3
                    dve.wait_ge(probT_ready, u + 1)
                    if u >= 8:
                        dve.wait_ge(o_ready, u // 4 - 1)
                    V.tensor_copy(probT[:, (u // 4) % 2, 3:6, (u % 4) * P:(u % 4 + 1) * P],
                                  sums[:, 1, 0:HALF].rearrange("p (r n) -> p r n", r=3)).then_inc(probT_dve, 1)
            branch_norm(0, "attn_out_norm")

            def gated_residual(name, gate_tile):
                for j in range(KD):
                    u = UNIT[name] + j
                    b = unit(u)
                    free(V.scalar_tensor_tensor(x_[:, j, 0:T], acc[:, b, :], mod[:, gate_tile + j, 0:1], x_[:, j, 0:T],
                                                ALU.mult, ALU.add), u)
            gated_residual("mix_out", 5 * KD)

            stat(T)
            scale(2, h512, T)
            swiglu("ffn2_in", T, 1, 44)
            blk2 = ADA_TILES
            modulation(3, blk2, N_BIAS, 60, [(3, "norm1_w_2", blk2 + KD), (4, "norm2_w_2", blk2 + 4 * KD)], [])
            residual("ffn2_out", 1, 1)
            for r in range(2):
                u = UNIT["tokens2"] + r
                b = unit(u)
                free(V.tensor_copy(x_[:, :, T + r * P:T + (r + 1) * P], wide(b).rearrange("p (j t) -> p j t", j=KD)), u)
            stat(T)
            for j in range(KD):
                V.scalar_tensor_tensor(x_[:, j, 0:T], x_[:, j, 0:T], v_("final_norm", j), rstd[:, 0:T],
                                       ALU.mult, ALU.mult).then_inc(x1_ready, 1)
            stat(TC)
            scale(3, h768, TC)

            def take(name, t, o, src):
                u = UNIT[name] + t
                b = unit(u)
                free(V.tensor_copy(o, src(b)), u)

            for r in range(6):
                take("rv", r, rv[:, r, :], lambda b: acc[:, b, :])
            for r in range(6):
                take("gv", r, gv[:, r, :], lambda b: acc[:, b, :])
            take("lr", 0, halves(lr), lambda b: acc[0:32, b:b + 2, 0:HALF])

            dve.wait_ge(halves_loaded, 16)
            for t in range(8):
                rope(UNIT["rope_r"] + t, rq[:, t, :] if t < 4 else rk[:, t - 4, 0:T], cos_halves, sin_halves, 5 + t)

            soft = sq[:, 0, :]
            for u in range(4):
                b = unit(UNIT["decay"] + u)
                free(V.tensor_scalar(halves(la[:, u // 2, u % 2, :]), acc[:, b:b + 2, 0:HALF],
                                     v_(("gla_gk_bias_f_2", "gla_gk_bias_b_2")[u // 2], u % 2), None, ALU.add), UNIT["decay"] + u)
            for u in range(4):
                dve.wait_ge(ln_ready, u + 1)
                z = la[:, u // 2, u % 2, :]
                V.scalar_tensor_tensor(z, z, 0.0, soft, ALU.min, ALU.subtract).then_inc(la_ready, 1)

            def distances(h):
                x1 = DX[:, h % 2, :]
                link(V.tensor_scalar(x1, dist[:, 0:N_DX], dec[:, 8 + h:9 + h], None, ALU.mult))
                V.scalar_tensor_tensor(x1, dist[:, N_DX:2 * N_DX], dec[:, 12 + h:13 + h], x1,
                                       ALU.mult, ALU.add).then_inc(dist_arg, 1)

            dve.wait_ge(dist_loaded, 16)
            distances(0)
            distances(1)
            for h in range(4):
                dve.wait_ge(dist_exp, h + 1)
                V.tensor_tensor(DX[:, h % 2, 384:384 + P], DX[:, h % 2, 384:384 + P], ident, ALU.add)
                V.tensor_tensor(DC[:, h % 2, :], DC[:, h % 2, :], sq[:, 1, 0:N_DC], ALU.add).then_inc(dist_done, 1)
                dve.wait_ge(dist_done, h + 1)
                for r in range(6):
                    u = 6 * h + r
                    b = unit(UNIT["ret"] + u)
                    if u >= 2:
                        dve.wait_ge(o_ready, 8 + u - 1)
                    decay = DX[:, h % 2, 384 - P * r:384 - P * r + T] if r < 4 else DC[:, h % 2, P - P * (r - 4):P - P * (r - 4) + T]
                    free(V.scalar_tensor_tensor(retP[:, u % 2, :], acc[:, b, :], RET_SCALE, decay, ALU.mult, ALU.mult), UNIT["ret"] + u)
                if h + 2 < 4:
                    emptied(dve, UNIT["ret"] + 6 * h + 5)
                    distances(h + 2)

            def head_norm(o, gate):
                stat(T)
                link(V.tensor_tensor(o, o, rstd[:, 0:T], ALU.mult))
                V.tensor_tensor(gate, gate, o, ALU.mult).then_inc(normed, 1)
            for h in range(4):
                head_norm(rq[:, h, :], yT[:, h, :])

            def chunks(x1):
                return x1.rearrange("p (c i) -> p c i", i=CHUNK)

            dve.wait_ge(o_ready, 8 + 24)
            for d in range(2):
                base = UNIT[f"gla{d}"]
                for pr in range(2):
                    ins = V.tensor_tensor_scan(gG[:, pr, :], c_("chunk_reset"), la[:, d, pr, :], 0.0, ALU.mult, ALU.add)
                if d == 0:
                    ins.then_inc(gla_arg, 1)
                    dve.wait_ge(gla_arg, 1)
                else:
                    link(ins)
                    for pr in range(2):
                        G4 = chunks(gG[:, pr, 0:T])
                        ins = V.tensor_tensor(chunks(gE[:, pr, 0:T]), G4[:, :, CHUNK - 1:CHUNK].to_broadcast([P, NCH, CHUNK]), G4, ALU.subtract)
                    link(ins)
                    for pr in range(2):
                        ins = V.tensor_tensor(gE[:, pr, 0:T], gE[:, pr, 0:T], la[:, d, pr, 0:T], ALU.add)
                    ins.then_inc(gla_arg, 1)
                    dve.wait_ge(gla_o, 4)
                e = gE if d == 0 else gkd
                dve.wait_ge(gla_exp, 3 * d + 1)
                for h in range(4):
                    V.scalar_tensor_tensor(gqz[:, h, :], gq[:, h // 2, :], c_("head_rows")[:, h % 2:h % 2 + 1], e[:, h // 2, 0:T],
                                           ALU.mult, ALU.mult).then_inc(gla_qk, 1)
                dve.wait_ge(gla_exp, 3 * d + 2)
                for pr in range(2):
                    V.tensor_tensor(gkt[:, pr, :], gk[:, pr, 0:T], e[:, pr, 0:T], ALU.mult).then_inc(gla_qk, 1)
                dve.wait_ge(gla_qk, 6 * (d + 1))
                for pr in range(2):
                    if d == 0:
                        G4 = chunks(gG[:, pr, 0:T])
                        V.tensor_tensor(chunks(gE[:, pr, 0:T]), G4[:, :, CHUNK - 1:CHUNK].to_broadcast([P, NCH, CHUNK]), G4, ALU.subtract)
                        ins = V.tensor_tensor(gE[:, pr, T:TC], gG[:, pr, TC - 1:TC].to_broadcast([P, C]), gG[:, pr, T:TC], ALU.subtract)
                    else:
                        ins = V.tensor_tensor(gE[:, pr, :], gG[:, pr, :], la[:, d, pr, :], ALU.subtract)
                ins.then_inc(gla_arg, 1)
                dve.wait_ge(gla_exp, 3 * d + 3)
                for pr in range(2):
                    V.tensor_tensor(gkd[:, pr, :], gk[:, pr, :], gE[:, pr, :], ALU.mult).then_inc(gla_kd, 1)
                link(V.memset(gP[:, :, :], 0.0))
                u = base + 2
                b = unit(u)
                order = list(range(NCH)) if d == 0 else list(range(NCH - 1, -1, -1))
                free(V.tensor_copy(gS[:, :, order[0], :], acc[:, b, 0:2 * P].rearrange("p (a v) -> p a v", a=2)), u)
                emptied(dve, u)
                for pr in range(2):
                    u = base + 3 + pr
                    b = unit(u)
                    for i in range(NCH - 1):
                        c = order[i]
                        ins = V.scalar_tensor_tensor(gS[:, pr, order[i + 1], :], gS[:, pr, c, :], gla_decay[:, pr, c:c + 1],
                                                     acc[:, b + c % 2, (c // 2) * P:(c // 2 + 1) * P], ALU.mult, ALU.add)
                        if i < NCH - 2:
                            ins.then_inc(gla_states, 1)
                            dve.wait_ge(gla_states, 12 * d + 6 * pr + i + 1)
                        else:
                            free(ins, u)
                mask = c_(("causal_f", "causal_b")[d]).bitcast(I32).unsqueeze(1).to_broadcast([P, 4, P])
                for h in range(4):
                    u = base + 5 + h
                    b = unit(u)
                    if h >= 2:
                        dve.wait_ge(gla_o, 4 * d + h - 1)
                    free(V.copy_predicated(gP[:, h % 2, :].rearrange("p (r n) -> p r n", r=4), mask,
                                           acc[:, b, :].rearrange("p (r n) -> p r n", r=4)), u)
            for h in range(4):
                head_norm(og[:, h, :], yT[:, 4 + h, :])

            gated_residual("w_out", ADA_TILES + 2 * KD)
            stat(T)
            scale(4, h512, T)
            for t in range(1, 16, 2):
                take("peer_q", t, pq[:, t, :], lambda b: acc[:, b, :])
            for g in range(2):
                take("keys", g, kTr[:, 8 * g:8 * g + 8, :], lambda b: wide(b).rearrange("p (j n) -> p j n", j=8))
            for g in range(2):
                emptied(dve, UNIT["keys"] + g)
            for w in range(2):
                for j in range(KD):
                    col = mod[:, ADA_TILES + 5 * KD + j, 0:1] if w == 0 else v_("norm_f_w_2", j)
                    V.tensor_scalar(rowsrc[:, w * KD + j, :], ones, col, None, ALU.mult).then_inc(rowsrc_ready, 1)
            for u0 in range(1, 8, 2):
                take("peer_s", u0, s_all[:, u0 // 2, 1024:2048], wide)
            for name, dst in (("xb", xb), ("xtok", xtok)):
                for t in range(1, 4, 2):
                    take(name, t, dst[:, t, :], wide)
            for w in range(2):
                emptied(dve, UNIT["rows"] + w)

            TOPK_STEPS = 14

            def topk(i):
                done = [0]

                def step(ins):
                    done[0] += 1
                    ins.then_inc(topk_step, 1)
                    dve.wait_ge(topk_step, i * TOPK_STEPS + done[0])
                    dve.sem_inc(dve_go, 1)

                side = [slice(0, P), slice(P, 2 * P)]
                step(V.tensor_copy(s_cur, arena[:, ds(i * 256 + 8192, 256)]))
                for m in range(2):
                    ins = V.max(key_top[:, 16 * m:16 * m + 8], s_cur[:, side[m]])
                step(ins)
                for m in range(2):
                    V.max_index(key_at[:, 16 * m:16 * m + 8], key_top[:, 16 * m:16 * m + 8], s_cur[:, side[m]])
                    ins = V.match_replace(s_less[:, side[m]], key_top[:, 16 * m:16 * m + 8], s_cur[:, side[m]], -3e38)
                step(ins)
                for m in range(2):
                    ins = V.max(key_top[:, 16 * m + 8:16 * m + 16], s_less[:, side[m]])
                step(ins)
                for m in range(2):
                    V.max_index(key_at[:, 16 * m + 8:16 * m + 16], key_top[:, 16 * m + 8:16 * m + 16], s_less[:, side[m]])
                step(V.tensor_tensor(cand.rearrange("p (a b) -> p a b", a=16), key_top[:, 0:16].unsqueeze(2).to_broadcast([P, 16, 16]),
                                     key_top[:, 16:32].unsqueeze(1).to_broadcast([P, 16, 16]), ALU.add))
                V.tensor_copy(key_no, key_at)
                step(V.max(p_top[:, 0:8], cand))
                V.max_index(cand_at[:, 0:8], p_top[:, 0:8], cand)
                step(V.match_replace(cand_less, p_top[:, 0:8], cand, -3e38))
                step(V.max(p_top[:, 8:16], cand_less))
                V.tensor_scalar(p_neg, p_top[:, 0:1], -1.0, None, ALU.mult).then_inc(top_ready, 1)
                step(V.max_index(cand_at[:, 8:16], p_top[:, 8:16], cand_less))
                V.tensor_scalar(cand_half[:, 0:16], cand_at, 4, None, ALU.logical_shift_right)
                step(V.tensor_scalar(cand_half[:, 16:32], cand_at, 15, None, ALU.bitwise_and))
                step(V.tensor_copy(cand_no, cand_half))
                pick = onehot.rearrange("p (k j) -> p k j", k=32)
                step(V.tensor_tensor(pick, cand_no.unsqueeze(2).to_broadcast([P, 32, 16]),
                                     c_("iota16").unsqueeze(1).to_broadcast([P, 32, 16]), ALU.is_equal))
                for m in range(2):
                    half = pick[:, 16 * m:16 * m + 16, :]
                    ins = V.tensor_tensor(half, half, key_no[:, 16 * m:16 * m + 16].unsqueeze(1).to_broadcast([P, 16, 16]), ALU.mult)
                step(ins)
                step(V.tensor_reduce(chosen, pick, AX_X, ALU.add))
                V.scalar_tensor_tensor(idx_all[:, ds(i * PEER_K, PEER_K)], chosen[:, 0:16], float(N_KEYS), chosen[:, 16:32],
                                       ALU.mult, ALU.add).then_inc(idx_ready, 1)
                assert done[0] == TOPK_STEPS

            def softmax(i):
                dve.wait_ge(p_exp_ready, i + 1)
                dve.sem_inc(dve_go, 1)
                V.reciprocal(p_inv, p_sum).then_inc(inv_ready, 1)
                dve.wait_ge(inv_ready, i + 1)
                V.tensor_scalar(g_all[:, ds(i * PEER_K, PEER_K)], p_exp, p_inv, None, ALU.mult)

            def dots(t, h):
                i = t * PEER_H + h
                for s in range(PEER_K):
                    dve.wait_ge(down_loaded[s % RING], i * 32 + 16 * (s // RING + 1))
                    V.scalar_tensor_tensor(down[:, s % RING, :], down[:, s % RING, :], 1.0, arena[:, ds(t * D + 16384, D)], ALU.mult, ALU.mult,
                                           accum_out=p_dot[:, s:s + 1]).then_inc(dots_done, 1)

            def weights(i):
                dve.wait_ge(gelu_ready, i + 1)
                V.tensor_tensor(p_w, p_act, g_all[:, ds(i * PEER_K, PEER_K)], ALU.mult).then_inc(weights_ready, 1)

            def finish(t):
                dve.wait_ge(tile_done, t + 1)
                dve.wait_ge(out_stored, t * 16 + 16)
                step = t * 3

                def fin_link(ins, k):
                    ins.then_inc(fin_step, 1)
                    dve.wait_ge(fin_step, step + k)
                    dve.sem_inc(dve_go, 1)

                V.tensor_tensor(fin, acc[:, 0:2, :].rearrange("p a n -> p (a n)"), g2row, ALU.mult).then_inc(tile_read, 1)
                dve.wait_ge(tile_read, t + 2)
                fin_link(V.tensor_tensor(fin, fin, hid[:, ds(t * D, D)], ALU.add), 1)
                V.scalar_tensor_tensor(junk, fin, 1.0, fin, ALU.mult, ALU.mult, accum_out=p_ssq).then_inc(ssq_ready, 1)
                dve.wait_ge(fstd_ready, t + 1)
                dve.sem_inc(dve_go, 1)
                fin_link(V.reciprocal(p_rstd, p_std), 2)
                fin_link(V.scalar_tensor_tensor(fin, fin, p_rstd, nfrow, ALU.mult, ALU.mult), 3)
                dve.sem_inc(fin_ready, 1)

            with dve.Fori(0, PEER_H) as h:
                topk(h)
                softmax(h)
            with dve.Fori(0, 3) as t:
                with dve.Fori(0, PEER_H) as h:
                    topk(t * PEER_H + (h + PEER_H))
                    dots(t, h)
                    softmax(t * PEER_H + (h + PEER_H))
                    weights(t * PEER_H + h)
                finish(t)
            with dve.Fori(0, PEER_H) as h:
                dots(3, h)
                weights(h + 3 * PEER_H)
            finish(3)

        @block.gpsimd
        def _(pool):
            pool.sem_inc(dots_done, RING)
            pool.sem_inc(up_used, PEER_K)
            with pool.Fori(0, 2 * PEER_H) as pair:
                for p in range(2):
                    i = pair * 2 + p
                    pool.wait_ge(idx_ready, i + 1)
                    pool.sem_inc(pool_go, 1)
                    nc.gpsimd.tensor_copy(stage[p], idx_all[:, ds(i * PEER_K, PEER_K)]).then_inc(stage_ready, 1)
                    pool.wait_ge(stage_ready, i + 1)
                    pool.sem_inc(pool_go, 1)
                    for s in range(PEER_K):
                        pool.wait_ge(dots_done, i * PEER_K + (s + 1))
                        pool.sem_inc(pool_go, 1)
                        nc.gpsimd.indirect_dma_start(down[:, s % RING, :], None, a["peer_down_2"][0],
                                                     bass.IndirectOffsetOnAxis(ap=stage[p][:, s:s + 1], axis=0)
                                                     ).then_inc(down_loaded[s % RING], 16)
                    for s in range(PEER_K):
                        pool.wait_ge(up_used, i * PEER_K + (s + RING + 1))
                        pool.sem_inc(pool_go, 1)
                        nc.gpsimd.indirect_dma_start(up[:, s % RING, :], None, a["peer_up_2"][0],
                                                     bass.IndirectOffsetOnAxis(ap=stage[p][:, s:s + 1], axis=0)
                                                     ).then_inc(up_loaded[s % RING], 16)

        @block.sync
        def _(sp):
            sp.sem_inc(mod_used, CREDIT)
            sp.sem_inc(out_stored, 16)
            sp.sem_inc(tile_read, 1)

            def features(w):
                return w.rearrange("(k p) n -> p k n", p=P)

            def load(dst, src, slot):
                sp.dma_start(dst, src).then_inc(w_loaded[slot], 16)

            def slot_free(s):
                if s >= 2:
                    sp.wait_ge(acc_ready, SLOT_END[s - 2])

            def mod_load(slot, block_no, w, col):
                sp.wait_ge(mod_used, block_no + 1)
                sp.dma_start(Mw[:, slot, :, :], features(w)[:, :, ds(col, MOD_COLS)]).then_inc(mod_loaded[slot], 16)

            def columns(s, w, col, cols=COLS):
                slot_free(s)
                for hf in range(2):
                    k = slice(4 * hf, 4 * hf + 4)
                    dst = Wk[:, s % 2, k, 0:cols] if cols > 32 else Wlr[:, s % 2, k, :]
                    load(dst, features(w)[:, k, col:col + cols], s % 2)

            def ffn_in(name, w, units, w_mod, first_block, col0):
                s0 = SLOT_OF[name]

                def step(i, p):
                    it, slot = i * 2 + p, (s0 + p) % 2
                    if isinstance(i, int):
                        slot_free(s0 + it)
                    else:
                        sp.wait_ge(acc_ready, it * units + (UNIT[name] - units))
                    for m in range(2):
                        load(Wk[:, slot, :, m * 256:(m + 1) * 256], features(w)[:, :, ds(it * 256 + m * FF, 256)], slot)
                    for q in range(2):
                        mod_load(q, it * 2 + (first_block + q), w_mod, it * 2 * MOD_COLS + (col0 + q * MOD_COLS))
                pairs(sp, 11, step, first=2)
                for q in range(2):
                    mod_load(q, first_block + 22 + q, w_mod, 22 * MOD_COLS + col0 + q * MOD_COLS)

            def ffn_out(name, w, units):
                s0 = SLOT_OF[name]

                def step(i, p):
                    it, slot = i * 2 + p, (s0 + p) % 2
                    if isinstance(i, int):
                        slot_free(s0 + it)
                    else:
                        sp.wait_ge(acc_ready, it * units + (UNIT[name] - units))
                    for m in range(2):
                        f = slice(11 * m, 11 * m + 11)
                        load(Wf[:, slot, f, :], w.rearrange("(f p) n -> p f n", p=P)[:, f, ds(it * P, P)], slot)
                pairs(sp, 8, step, first=2)

            for r in range(4):
                sp.dma_start(tok[:, r, :], a["x"][0][r * P:(r + 1) * P, :]).then_inc(tok_loaded, 16)
            for r in range(2):
                sp.dma_start(tok[:, 4 + r, :], a["ctx"][0][r * P:(r + 1) * P, :]).then_inc(tok_loaded, 16)
            with sp.Fori(0, 6) as i:
                for q in range(2):
                    mod_load(q, i * 2 + q, a["w_ada"][0], i * 2 * MOD_COLS + q * MOD_COLS)

            ffn_in("ffn1_in", a["w_ffn1_in"][0], 4, a["w_ada"][0], 12, 12 * MOD_COLS)
            ffn_out("ffn1_out", a["w_ffn1_out"][0], 2)
            for j in range(5):
                columns(SLOT_OF["mix_in"] + j, a["w_mix_in"][0], j * COLS, COLS if j < 4 else 256)
            sp.wait_ge(acc_ready, UNIT["rope_q"])
            sp.dma_start(hid[:, 0:2 * T], a["rope"][:, 0:2 * T]).then_inc(pairs_loaded, 16)
            for j in range(2):
                columns(SLOT_OF["mix_out"] + j, a["w_mix_out"][0], j * COLS)
            for r in range(2):
                sp.dma_start(tok2[:, r, :], a["ctx_2"][0][r * P:(r + 1) * P, :]).then_inc(tok2_loaded, 16)
            ffn_in("ffn2_in", a["w_ffn2_in"][0], 2, a["w_mod_2"][0], ADA_BLOCKS, 0)
            ffn_out("ffn2_out", a["w_ffn2_out"][0], 1)

            sp.wait_ge(mod_used, CREDIT + 60)
            sp.dma_start(modw[:, 3072:3072 + 2 * T], a["rope"][:, 2 * T:4 * T]).then_inc(halves_loaded, 16)
            for j in range(8):
                columns(SLOT_OF["proj"] + j, a["w_in_2"][0], j * COLS, COLS if j < 7 else 32)
            sp.wait_ge(acc_ready, UNIT["rope_r"])
            sp.dma_start(dist, a["dist"]).then_inc(dist_loaded, 16)
            for j in range(2):
                columns(SLOT_OF["w_out"] + j, a["w_out_2"][0], j * COLS)
            sp.wait_ge(acc_ready, UNIT["w_out"] + 1)
            for m, name in enumerate(("peer_k1_2", "peer_k2_2")):
                sp.dma_start(knat.rearrange("p (h m) n -> p h m n", m=2)[:, :, m, :],
                             a[name][0].rearrange("h n d -> n h d")).then_inc(keys_loaded, 16)
            for j in range(4):
                columns(SLOT_OF["peer_q"] + j, a["peer_w_q_2"][0], j * COLS)

            with sp.Fori(0, 4) as t:
                sp.wait_ge(fin_ready, t + 1)
                sp.dma_start(out[0][ds(t * P, P), :], fin).then_inc(out_stored, 16)
            sp.wait_ge(out_stored, 16 + 4 * 16)


def kernel(**inputs):
    import concourse.bacc as bacc
    from concourse.bass_utils import run_bass_kernel_spmd

    nc = bacc.Bacc("TRN2", target_bir_lowering=False, num_devices=1)
    arrays, aps = {}, {}
    for name, value in {**inputs, **constants()}.items():
        value = np.ascontiguousarray(value)
        arrays[f"in_{name}"] = value
        aps[name] = nc.dram_tensor(f"in_{name}", value.shape, mybir.dt.from_np(value.dtype), kind="ExternalInput").ap()
    out = nc.dram_tensor("out", (1, T, D), F32, kind="ExternalOutput").ap()
    build(nc, aps, out)
    result = run_bass_kernel_spmd(nc, [arrays], core_ids=[0])
    return result.results[0]["out"]
```

```python
from contextlib import ExitStack

import concourse.bass as bass
import numpy as np
from concourse import mybir

F32 = mybir.dt.float32
U32 = mybir.dt.uint32
I32 = mybir.dt.int32
ALU = mybir.AluOpType
ACT = mybir.ActivationFunctionType
AX_X = mybir.AxisListType.X
ds = bass.ds

P = 128
D = 1024
KD = D // P
T = 512
C = 256
TC = T + C
HALF = TC // 2
FF = 2816
FT = FF // P
EPS = 1e-6
COLS = 512
SLOT = 4096
FIRST_MODS = 2 * KD
ADA_TILES = 9 * KD
MOD_TILES = 6 * KD
ADA_LATER, MOD_PER_SLOT = ADA_TILES - FIRST_MODS, (5, 4)
N_LATER = ADA_LATER + MOD_TILES
HEADS, KV_HEADS, HD = 8, 2, 64
RET_SCALE = 128 ** -0.5
GLA_SCALE = 64 ** -0.5
CHUNK = 64
NCH = T // CHUNK
GATE_NORM = 16.0
PEER_H, PEER_K, N_KEYS = 8, 16, 128
SLOTS = PEER_H * PEER_K
RING = 8
CREDIT = 2

UNIT = {}
_at = 0
for _name, _n in (("tokens", 6), ("ffn1_in", 44), ("ffn1_out", 16), ("q", 4), ("k", 1), ("v", 2), ("gb", 4),
                  ("gc", 4), ("u", 4), ("rope_q", 4), ("rope_k", 1), ("kdup", 2), ("scores", 32),
                  ("mix_out", 8), ("ffn2_in", 22), ("ffn2_out", 8), ("tokens2", 2), ("rq", 4), ("rk", 4),
                  ("rv", 6), ("rg", 4), ("gq", 2), ("gk", 2), ("gv", 6), ("gg", 4), ("lr", 1),
                  ("rope_r", 8), ("decay", 4), ("ret", 24), ("gla0", 9), ("gla1", 9), ("w_out", 8),
                  ("peer_q", 16), ("keys", 2), ("peer_s", 8), ("xb", 4), ("xtok", 4), ("rows", 2)):
    UNIT[_name] = _at
    _at += _n

SLOT_OF, SLOT_END = {}, []
for _name, _ends in (("ffn1_in", [UNIT["ffn1_in"] + 4 * (i + 1) for i in range(11)]),
                     ("ffn1_out", [UNIT["ffn1_out"] + 2 * (i + 1) for i in range(8)]),
                     ("mix_in", [UNIT["q"] + 4, UNIT["gb"] + 2, UNIT["gc"] + 2, UNIT["u"] + 2, UNIT["u"] + 4]),
                     ("mix_out", [UNIT["mix_out"] + 4, UNIT["mix_out"] + 8]),
                     ("ffn2_in", [UNIT["ffn2_in"] + 2 * (i + 1) for i in range(11)]),
                     ("ffn2_out", [UNIT["ffn2_out"] + i + 1 for i in range(8)]),
                     ("proj", [UNIT[n] for n in ("rk", "rv", "rg", "gq", "gv", "gg", "lr", "rope_r")]),
                     ("w_out", [UNIT["w_out"] + 4, UNIT["w_out"] + 8]),
                     ("peer_q", [UNIT["peer_q"] + 4 * (i + 1) for i in range(4)])):
    SLOT_OF[_name] = len(SLOT_END)
    SLOT_END += _ends

ROWS = {}
_at = 0
for _name, _n in (("c", 8), ("c_ctx", 8), ("norm_ffn1", 8), ("norm_mix", 8), ("attn_out_norm", 4),
                  ("conv_out_norm", 4), ("norm_ffn2", 8), ("final_norm", 8), ("c_2", 8), ("c_ctx_2", 8),
                  ("norm1_w_2", 8), ("norm2_w_2", 8), ("norm_f_w_2", 8), ("conv_w", 12),
                  ("q_norm", 1), ("k_norm", 1), ("gla_gk_bias_f_2", 2), ("gla_gk_bias_b_2", 2)):
    ROWS[_name] = (_at, _n)
    _at += _n
N_ROWS = _at
N_BIAS = ADA_TILES + MOD_TILES

CONST = {}
_at = 0
for _name, _n in (("ident", P), ("ones", P), ("blk64", P), ("swap_pairs", P), ("swap_halves", P),
                  ("dup0", P), ("dup1", P), ("causal_f", P), ("causal_b", P), ("chunk_reset", TC),
                  ("head_rows", 2), ("iota16", 16), ("eps", 1), ("zero", P), ("mean1024", P), ("mean512", P), ("mean128", P)):
    CONST[_name] = (_at, _n)
    _at += _n
N_CONST = _at
N_DX, N_DC = 896, 640
N_DIST = T + N_DC
N_VEC_DMAS = 26


def flat(ap):
    if len(ap.shape) == 1:
        return ap
    return ap.rearrange("a b -> (a b)")


def constants():
    t = np.zeros((P, N_CONST), np.float32)

    def put(name, value):
        at, n = CONST[name]
        t[:, at:at + n] = value

    p = np.arange(P)
    put("ident", np.eye(P))
    put("ones", 1.0)
    put("blk64", (p[:, None] // 64 == p[None, :] // 64) / 64)
    pairs, halves = np.zeros((P, P)), np.zeros((P, P))
    pairs[p[0::2] + 1, p[0::2]], pairs[p[0::2], p[0::2] + 1] = -1.0, 1.0
    halves[p[:64] + 64, p[:64]], halves[p[:64], p[:64] + 64] = -1.0, 1.0
    put("swap_pairs", pairs)
    put("swap_halves", halves)
    for kv in range(KV_HEADS):
        put(f"dup{kv}", p[:, None] == kv * 64 + p[None, :] % 64)
    same = p[:, None] // CHUNK == p[None, :] // CHUNK
    put("causal_f", same & (p[:, None] <= p[None, :]))
    put("causal_b", same & (p[:, None] >= p[None, :]))
    reset = np.ones(TC)
    reset[0:T:CHUNK], reset[T] = 0.0, 0.0
    put("chunk_reset", reset[None, :])
    put("head_rows", np.stack([p < 64, p >= 64], 1) * GLA_SCALE)
    put("iota16", np.arange(16)[None, :])
    put("eps", EPS)
    for n in (1024, 512, 128):
        put(f"mean{n}", 1.0 / n)
    tok, rope = np.arange(T), []
    for name, dim, place in (("pairs", HD, (p % 64) // 2), ("halves", 128, p % 64)):
        n = dim // 4
        inv = (np.float32(10000.0) ** (-np.arange(n, dtype=np.float32) / n)).astype(np.float32)
        ang = np.concatenate([(tok // 64).astype(np.float32)[:, None] * inv,
                              (tok % 64).astype(np.float32)[:, None] * inv], 1).T
        rope += [np.cos(ang)[place], np.sin(ang)[place]]
    dist = np.arange(N_DIST)[None, :] - 384 - p[:, None]
    return {"const": t, "dist": dist.astype(np.float32), "rope": np.concatenate(rope, 1).astype(np.float32)}


def build(nc, a, out):
    with ExitStack() as ctx:
        def sb(name, cols, dt=F32, parts=P):
            return ctx.enter_context(nc.sbuf_tensor(name, [parts, cols], dt))

        def pb(name, shape):
            return ctx.enter_context(nc.psum_tensor(name, shape, F32))

        def sem(name):
            return ctx.enter_context(nc.semaphore(name))

        acc = pb("acc", [P, 4, 512])
        mod_ps = pb("mod_ps", [P, 512])
        sums = pb("sums", [P, 2, 512])
        misc = pb("misc", [P, 512])

        cst = sb("cst", N_CONST)
        resid = sb("resid", KD * TC)
        hid = sb("hid", KD * TC)
        wring = sb("wring", 2 * SLOT)
        modw = sb("modw", 2 * 2048)
        arena = sb("arena", 20480)
        rows1 = sb("rows1", P)
        rows2 = sb("rows2", P)
        vec = sb("vec", 256)
        cond = sb("cond", 32)
        mods = sb("mods", 2 * N_BIAS)
        gains = sb("gains", 5 * 16)
        halfg = sb("halfg", 2 * 16)
        squares = sb("squares", 2 * TC)
        rstd = sb("rstd", TC)
        tmp = sb("tmp", TC)
        logs = tmp
        dec = sb("dec", 80)
        gkup = sb("gkup", 2 * 256, parts=32)
        small = sb("small", 128)
        partials = sb("partials", 2 * 2 * P)

        def c_(name, parts=P):
            at, n = CONST[name]
            return cst[0:parts, at:at + n]

        def v_(name, j=0, n=1):
            at = ROWS[name][0] + j
            return vec[:, at:at + n]

        ident, ones = c_("ident"), c_("ones")
        x_ = resid[:, :].rearrange("p (j t) -> p j t", j=KD)
        h768 = hid[:, :].rearrange("p (j t) -> p j t", j=KD)
        h512 = hid[:, 0:KD * T].rearrange("p (j t) -> p j t", j=KD)
        W = wring[:, :].rearrange("p (s n) -> p s n", s=2)
        Wk = wring[:, :].rearrange("p (s k n) -> p s k n", s=2, k=KD)
        Wf = W[:, :, 0:FT * P].rearrange("p s (f n) -> p s f n", f=FT)
        Wlr = W[:, :, 0:KD * 32].rearrange("p s (k n) -> p s k n", k=KD)
        Mw = modw[:, 0:2048].rearrange("p (s k n) -> p s k n", s=2, k=KD)
        cnd = cond[:, :].rearrange("p (b k c) -> p b k c", b=2, k=KD)
        mod = mods[:, :].rearrange("p (t c) -> p t c", c=2)
        gain = gains[:, :].rearrange("p (n k c) -> p n k c", n=5, k=KD)
        hgate = halfg[:, :].rearrange("p (n k c) -> p n k c", n=2, k=KD)
        sq = squares[:, :].rearrange("p (s t) -> p s t", s=2)

        def ar(at, *shape):
            n = int(np.prod(shape))
            v = arena[:, at:at + n]
            if len(shape) == 2:
                return v.rearrange("p (a b) -> p a b", a=shape[0])
            if len(shape) == 3:
                return v.rearrange("p (a b c) -> p a b c", a=shape[0], b=shape[1])
            return v

        def hi(at, *shape):
            n = int(np.prod(shape))
            v = hid[:, at:at + n]
            if len(shape) == 2:
                return v.rearrange("p (a b) -> p a b", a=shape[0])
            if len(shape) == 3:
                return v.rearrange("p (a b c) -> p a b c", a=shape[0], b=shape[1])
            return v

        Mfirst = [ar(6144 + 2048 * i, KD, 256) for i in range(7)] + [modw[:, 2048:4096].rearrange("p (k n) -> p k n", k=KD)]
        partial = partials[:, :].rearrange("p (s c n) -> p s c n", s=2, c=2)
        tok = ar(0, 6, D)
        tok2 = ar(18432, 2, D)
        ff768, ff512 = ar(0, FT, TC), ar(0, FT, T)
        sg = ar(FT * TC, 2, 512)
        qT, kT = ar(0, 4, T), ar(2048, TC)
        kdup, vtok = ar(2816, 2, TC), ar(4352, 6, P)
        gb, cu, gc = ar(5120, 4, T), ar(7168, 4, T + 2), ar(9224, 4, T)
        prob, mixT = ar(11272, 3, TC), ar(13576, KD, T)
        probT = hid[:, :].rearrange("p (h r t) -> p h r t", h=2, r=6)
        cos_pairs, sin_pairs = hi(0, T), hi(T, T)
        yT = ar(0, KD, T)
        rq, rk, rv = ar(4096, 4, T), ar(6144, 4, TC), ar(9216, 6, 512)
        gq, gk = ar(12288, 2, T), ar(13312, 2, TC)
        lr = arena[0:32, 14848:14848 + TC]
        la = ar(15616, 2, 2, TC)
        retP = ar(18688, 2, T)
        gv = modw[:, 0:3072].rearrange("p (b n) -> p b n", b=6)
        cos_halves, sin_halves = modw[:, 3072:3072 + T], modw[:, 3072 + T:4096]
        dist = hi(0, N_DIST)
        DX, DC = hi(3072, 2, N_DX), hi(4864, 2, N_DC)
        gG, gE, gkt, gS = ar(6144, 2, TC), ar(7680, 2, TC), ar(9216, 2, T), ar(10240, 2, NCH, P)
        gla_decay = dec[:, 48:64].rearrange("p (a c) -> p a c", a=2)
        gkd, gkd_tok, gqz, gP = hi(0, 2, TC), hi(1536, 6, 256), hi(3072, 4, T), hi(5120, 2, T)
        og = ar(15616, 4, T)
        pq, s_all, xb = ar(0, 16, T), ar(8192, 4, 2048), ar(16384, 4, D)
        down = wring[:, :].rearrange("p (s n) -> p s n", s=RING)
        up = ar(0, RING, D)
        knat, kTr = hi(4096, 16, P), modw[:, 0:2048].rearrange("p (a n) -> p a n", a=16)
        xtok = hi(0, 4, D)
        diag, rowsrc = hi(4096, 16, P), hi(4096, 16, P)
        g2row, nfrow = resid[:, 0:D], resid[:, D:2 * D]
        junk, fin = resid[:, 2 * D:3 * D], resid[:, 3 * D:4 * D]
        idx_all = squares[:, 0:512].bitcast(U32)
        g_all = squares[:, 512:1024]

        def pm(at, n):
            return modw[:, 2048 + at:2048 + at + n]

        s_cur, s_less = pm(0, 256), pm(256, 256)
        onehot = pm(512, 512)
        key_top, key_at = pm(1024, 32), pm(1056, 32).bitcast(U32)
        key_no, chosen = pm(1088, 32), pm(1120, 32)
        cand_at, cand_half = pm(1152, 16).bitcast(U32), pm(1168, 32).bitcast(U32)
        cand_no = pm(1200, 32)
        stage = [pm(1232 + 16 * i, 16).bitcast(U32) for i in range(2)]
        p_top, p_exp, p_dot, p_act, p_w = (pm(1264 + 16 * i, 16) for i in range(5))
        p_neg, p_sum, p_inv, p_ssq, p_std, p_rstd = (pm(1344 + i, 1) for i in range(6))
        cand, cand_less = pm(1360, 256), pm(1616, 256)

        tok_loaded, tok2_loaded = sem("tok_loaded"), sem("tok2_loaded")
        const_loaded, vec_loaded = sem("const_loaded"), sem("vec_loaded")
        dist_loaded, keys_loaded = sem("dist_loaded"), sem("keys_loaded")
        w_loaded = [sem(f"w_loaded{i}") for i in range(2)]
        mod_loaded = [sem(f"mod_loaded{i}") for i in range(2)]
        first_loaded = [sem(f"first_loaded{i}") for i in range(8)]
        first_used, mod_step, pool_go = sem("first_used"), sem("mod_step"), sem("pool_go")
        partial_ready, partial_used = sem("partial_ready"), sem("partial_used")
        acc_ready = sem("acc_ready")
        acc_free = [sem(f"acc_free{i}") for i in range(2)]
        rows_zeroed, vec_turned, vec_ready, cond_ready = sem("rows_zeroed"), sem("vec_turned"), sem("vec_ready"), sem("cond_ready")
        sq_ready, sq_used, rstd_ready = sem("sq_ready"), sem("sq_used"), sem("rstd_ready")
        h_scaled, h_ready, x1_ready = sem("h_scaled"), sem("h_ready"), sem("x1_ready")
        silu_ready = sem("silu_ready")
        dve_step, act_step = sem("dve_step"), sem("act_step")
        normed = sem("normed")
        copied = sem("copied")
        negmax_ready, exp_ready, prob_ready = sem("negmax_ready"), sem("exp_ready"), sem("prob_ready")
        probT_ready, probT_act, probT_dve = sem("probT_ready"), sem("probT_act"), sem("probT_dve")
        o_ready, o_copied = sem("o_ready"), sem("o_copied")

        mods_ready, conv_ready = sem("mods_ready"), sem("conv_ready")
        pairs_loaded, halves_loaded = sem("pairs_loaded"), sem("halves_loaded")
        decay_abs, decay_exp, la_ready, ln_ready = sem("decay_abs"), sem("decay_exp"), sem("la_ready"), sem("ln_ready")
        dist_arg, dist_exp, dist_done = sem("dist_arg"), sem("dist_exp"), sem("dist_done")
        gla_arg, gla_exp, gla_kd, gla_qk = sem("gla_arg"), sem("gla_exp"), sem("gla_kd"), sem("gla_qk")
        gla_states, gla_o = sem("gla_states"), sem("gla_o")
        rowsrc_ready, tile_read, tile_done = sem("rowsrc_ready"), sem("tile_read"), sem("tile_done")
        down_loaded = [sem(f"down_loaded{i}") for i in range(RING)]
        up_loaded = [sem(f"up_loaded{i}") for i in range(RING)]
        idx_ready, stage_ready = sem("idx_ready"), sem("stage_ready")
        top_ready, p_exp_ready, topk_step, dve_go = sem("top_ready"), sem("p_exp_ready"), sem("topk_step"), sem("dve_go")
        dots_done, gelu_ready, weights_ready = sem("dots_done"), sem("gelu_ready"), sem("weights_ready")
        diag_ready, up_used = sem("diag_ready"), sem("up_used")
        ssq_ready, fstd_ready, fin_ready = sem("ssq_ready"), sem("fstd_ready"), sem("fin_ready")
        out_stored, inv_ready = sem("out_stored"), sem("inv_ready")

        block = ctx.enter_context(nc.Block())

        class Tally:
            def __init__(self):
                self.sq = self.job = self.step = 0

        def pairs(eng, steps, body, first=0):
            for s in range(first):
                body(s // 2, s % 2)
            if steps // 2 > first // 2:
                with eng.Fori(first // 2, steps // 2) as i:
                    for p in range(2):
                        body(i, p)
            if steps % 2:
                body(steps // 2, 0)

        def emptied(eng, u):
            eng.wait_ge(acc_free[u % 2], u // 2 + CREDIT)

        @block.tensor
        def _(pe):
            n = Tally()
            for p in range(2):
                pe.sem_inc(acc_free[p], 1)

            def begin(u):
                pe.wait_ge(acc_free[u % 2], u // 2 + 1)
                return 2 * (u % 2)

            def product(o, w, x, k, last):
                return nc.tensor.matmul(o, w, x, start=(k == 0), stop=(k == last))

            def stat(tiles, t, weights):
                for j in range(tiles):
                    pe.wait_ge(sq_ready, n.sq + 1)
                    if j == 0 and n.job:
                        pe.wait_ge(rstd_ready, n.job)
                    s = n.sq % 2
                    if t == T:
                        mm = product(sums[:, 0, :], weights, sq[:, s, 0:T], j, tiles - 1)
                    else:
                        for hf in range(2):
                            mm = product(sums[:, hf, 0:HALF], weights, sq[:, s, hf * HALF:(hf + 1) * HALF], j, tiles - 1)
                    mm.then_inc(sq_used, 1)
                    n.sq += 1
                n.job += 1

            def mod_sum(p, m, column):
                pe.wait_ge(partial_ready, m + 1)
                for c in range(2):
                    mm = nc.tensor.matmul(mod_ps[:, ds(column + c, 1)], partial[:, p, c, :], ones[:, 0:1], start=True, stop=True)
                mm.then_inc(partial_used, 1)

            def slot_ready(s):
                pe.wait_ge(w_loaded[s % 2], 32 * (s // 2 + 1))
                return s % 2

            def to_features(u, src):
                b = begin(u)
                for j in range(KD):
                    mm = nc.tensor.transpose(acc[:, b + j // 4, (j % 4) * P:(j % 4 + 1) * P],
                                             src[:, j * P:(j + 1) * P], ident)
                mm.then_inc(acc_ready, 1)

            pe.wait_ge(const_loaded, 16)
            pe.wait_ge(tok_loaded, 16 * 6)
            for r in range(6):
                to_features(UNIT["tokens"] + r, tok[:, r, :])
            pe.wait_ge(vec_loaded, 16 * N_VEC_DMAS)
            nc.tensor.transpose(misc[:, 0:N_ROWS], rows1[0:N_ROWS, :], ident[0:N_ROWS, 0:N_ROWS])
            nc.tensor.transpose(misc[:, 128:128 + N_BIAS], rows2[0:N_BIAS, :],
                                ident[0:N_BIAS, 0:N_BIAS]).then_inc(vec_turned, 1)

            stat(KD, TC, c_("mean1024"))
            pe.wait_ge(cond_ready, 4)
            for i in range(8):
                pe.wait_ge(first_loaded[i], 16)
                for t in range(2):
                    for k in range(KD):
                        mm = product(mod_ps[:, 4 * i + 2 * t:4 * i + 2 * t + 2], Mfirst[i][:, k, t * P:(t + 1) * P], cnd[:, 0, k, :], k, KD - 1)
                mm.then_inc(first_used, 1)

            def ffn_in(name, width, halves, first, per, count):
                units = 2 * halves
                src = h768 if halves == 2 else h512
                base, s0 = UNIT[name], SLOT_OF[name]

                def step(i, p):
                    s, it = (s0 + p) % 2, i * 2 + p
                    pe.wait_ge(w_loaded[s], (i + (s0 + p) // 2 + 1) * 32)
                    for q in range(units):
                        sub, hf = q // halves, q % halves
                        u0 = base + p * units + q
                        b = 2 * (u0 % 2)
                        pe.wait_ge(acc_free[u0 % 2], i * units + (u0 // 2 + 1))
                        for m in range(2):
                            for k in range(KD):
                                col = m * 256 + sub * P
                                mm = product(acc[:, b + m, 0:width], Wk[:, s, k, col:col + P],
                                             src[:, k, hf * width:(hf + 1) * width], k, KD - 1)
                        mm.then_inc(acc_ready, 1)
                        for tile in range(q * per // units, (q + 1) * per // units):
                            m = it * per + (first + tile)
                            mod_sum((p * per + first + tile) % 2, m, m * 2 + 2 * FIRST_MODS)
                pairs(pe, 11, step)
                for m in range(first + 11 * per, first + count):
                    mod_sum(m % 2, m, m * 2 + 2 * FIRST_MODS)

            def ffn_out(name, width, halves, ff):
                base, s0 = UNIT[name], SLOT_OF[name]

                def step(i, p):
                    s = (s0 + p) % 2
                    pe.wait_ge(w_loaded[s], (i + (s0 + p) // 2 + 1) * 32)
                    for hf in range(halves):
                        u0 = base + p * halves + hf
                        b = 2 * (u0 % 2)
                        pe.wait_ge(acc_free[u0 % 2], i * halves + (u0 // 2 + 1))
                        for f in range(FT):
                            mm = product(acc[:, b, 0:width], Wf[:, s, f, :],
                                         ff[:, f, hf * width:(hf + 1) * width], f, FT - 1)
                        mm.then_inc(acc_ready, 1)
                emptied(pe, base - 1)
                emptied(pe, base - 2)
                pairs(pe, 8, step)

            pe.wait_ge(h_ready, 8)
            ffn_in("ffn1_in", HALF, 2, 0, MOD_PER_SLOT[0], ADA_LATER)
            ffn_out("ffn1_out", HALF, 2, ff768)
            stat(KD, TC, c_("mean1024"))

            pe.wait_ge(h_ready, 16)
            s = slot_ready(SLOT_OF["mix_in"])

            def feature_tile(u, s, col, src, width=T, halves=1, rows=P):
                b = begin(u)
                for hf in range(halves):
                    for k in range(KD):
                        mm = product(acc[0:rows, b + hf, 0:width], Wk[:, s, k, col:col + rows],
                                     src[:, k, hf * width:(hf + 1) * width], k, KD - 1)
                mm.then_inc(acc_ready, 1)

            for t in range(4):
                feature_tile(UNIT["q"] + t, s, t * P, h768)
            s = slot_ready(SLOT_OF["mix_in"] + 1)
            feature_tile(UNIT["k"], s, 0, h768, HALF, 2)
            for v in range(2):
                b = begin(UNIT["v"] + v)
                for r in range(3):
                    at = (3 * v + r) * P
                    for k in range(KD):
                        mm = product(acc[:, b, r * P:(r + 1) * P], h768[:, k, at:at + P], Wk[:, s, k, P:2 * P], k, KD - 1)
                mm.then_inc(acc_ready, 1)
            for g in range(12):
                if g in (2, 6, 10):
                    s = slot_ready(SLOT_OF["mix_in"] + 2 + (g - 2) // 4)
                feature_tile(UNIT["gb"] + g, s, 256 + g * P if g < 2 else ((g - 2) % 4) * P, h768)

            for t in range(4):
                stat(1, T, c_("blk64"))
            stat(1, TC, c_("blk64"))
            for t in range(5):
                u = UNIT["rope_q"] + t
                b = begin(u)
                pe.wait_ge(normed, t + 1)
                nc.tensor.matmul(acc[:, b, :], c_("swap_pairs"), qT[:, t, :] if t < 4 else kT[:, 0:T],
                                 start=True, stop=True).then_inc(acc_ready, 1)
            pe.wait_ge(copied, 5)
            for kv in range(KV_HEADS):
                b = begin(UNIT["kdup"] + kv)
                for hf in range(2):
                    mm = nc.tensor.matmul(acc[:, b + hf, 0:HALF], c_(f"dup{kv}"), kT[:, hf * HALF:(hf + 1) * HALF],
                                          start=True, stop=True)
                mm.then_inc(acc_ready, 1)
            stat(4, T, c_("mean512"))

            pe.wait_ge(rstd_ready, n.job)
            emptied(pe, UNIT["kdup"])
            emptied(pe, UNIT["kdup"] + 1)

            def scores(u):
                h, t = u // 4, u % 4
                b = begin(UNIT["scores"] + u) if u < 2 else 2 * (u % 2)
                if u >= 2:
                    pe.wait_ge(exp_ready, u - 1)
                rows = slice(64 * (h % 2), 64 * (h % 2) + 64)
                for hf in range(2):
                    mm = nc.tensor.matmul(acc[:, b + hf, 0:HALF], qT[rows, h // 2, t * P:(t + 1) * P],
                                          kdup[rows, h // 4, hf * HALF:(hf + 1) * HALF], start=True, stop=True)
                mm.then_inc(acc_ready, 1)

            def turn(u):
                pe.wait_ge(prob_ready, u + 1)
                if u:
                    pe.wait_ge(probT_act, u)
                    pe.wait_ge(probT_dve, u)
                for r in range(6):
                    mm = nc.tensor.transpose(sums[:, r // 3, (r % 3) * P:(r % 3 + 1) * P],
                                             prob[:, u % 3, r * P:(r + 1) * P], ident)
                mm.then_inc(probT_ready, 1)

            def outputs(h):
                pe.wait_ge(probT_act, 4 * (h + 1))
                pe.wait_ge(probT_dve, 4 * (h + 1))
                if h:
                    pe.wait_ge(o_copied, h)
                at, kv = 64 * (h % 2), h // 4
                for r in range(6):
                    mm = product(misc[at:at + 64, :], vtok[:, r, kv * HD:(kv + 1) * HD], probT[:, h % 2, r, :], r, 5)
                mm.then_inc(o_ready, 1)

            scores(0)
            for step in range(32 + 3):
                if step + 1 < 32:
                    scores(step + 1)
                if 2 <= step < 34:
                    turn(step - 2)
                if step >= 6 and (step - 6) % 4 == 0:
                    outputs((step - 6) // 4)
            stat(4, T, c_("mean512"))

            def gemm512(name, slot_name, tiles, src):
                for t in range(tiles):
                    if t % 4 == 0:
                        s = slot_ready(SLOT_OF[slot_name] + t // 4)
                    feature_tile(UNIT[name] + t, s, (t % 4) * P, src)

            pe.wait_ge(normed, 5 + 8)
            gemm512("mix_out", "mix_out", 8, mixT)
            stat(KD, T, c_("mean1024"))

            pe.wait_ge(h_ready, 24)
            ffn_in("ffn2_in", T, 1, ADA_LATER, MOD_PER_SLOT[1], MOD_TILES)
            ffn_out("ffn2_out", T, 1, ff512)
            pe.wait_ge(tok2_loaded, 32)
            for r in range(2):
                to_features(UNIT["tokens2"] + r, tok2[:, r, :])
            stat(KD, T, c_("mean1024"))
            stat(KD, TC, c_("mean1024"))

            pe.wait_ge(h_ready, 32)
            p0 = SLOT_OF["proj"]

            def token_tiles(name, s):
                for r in range(6):
                    b = begin(UNIT[name] + r)
                    for k in range(KD):
                        mm = product(acc[:, b, :], h768[:, k, r * P:(r + 1) * P], Wk[:, s, k, :], k, KD - 1)
                    mm.then_inc(acc_ready, 1)

            s = slot_ready(p0)
            for t in range(4):
                feature_tile(UNIT["rq"] + t, s, t * P, h768)
            s = slot_ready(p0 + 1)
            for t in range(4):
                feature_tile(UNIT["rk"] + t, s, t * P, h768, HALF, 2)
            token_tiles("rv", slot_ready(p0 + 2))
            s = slot_ready(p0 + 3)
            for t in range(4):
                feature_tile(UNIT["rg"] + t, s, t * P, h768)
            s = slot_ready(p0 + 4)
            for t in range(2):
                feature_tile(UNIT["gq"] + t, s, t * P, h768)
            for t in range(2):
                feature_tile(UNIT["gk"] + t, s, 256 + t * P, h768, HALF, 2)
            token_tiles("gv", slot_ready(p0 + 5))
            s = slot_ready(p0 + 6)
            for t in range(4):
                feature_tile(UNIT["gg"] + t, s, t * P, h768)
            s = slot_ready(p0 + 7)
            b = begin(UNIT["lr"])
            for hf in range(2):
                for k in range(KD):
                    mm = product(acc[0:32, b + hf, 0:HALF], Wlr[:, s, k, :], h768[:, k, hf * HALF:(hf + 1) * HALF], k, KD - 1)
            mm.then_inc(acc_ready, 1)

            for t in range(8):
                src = rq[:, t, :] if t < 4 else rk[:, t - 4, 0:T]
                emptied(pe, UNIT["rq"] + t)
                b = begin(UNIT["rope_r"] + t)
                nc.tensor.matmul(acc[:, b, :], c_("swap_halves"), src, start=True, stop=True).then_inc(acc_ready, 1)
            emptied(pe, UNIT["lr"])
            for u in range(4):
                b = begin(UNIT["decay"] + u)
                at = (u // 2) * 256 + (u % 2) * P
                for hf in range(2):
                    mm = nc.tensor.matmul(acc[:, b + hf, 0:HALF], gkup[:, at:at + P], lr[:, hf * HALF:(hf + 1) * HALF],
                                          start=True, stop=True)
                mm.then_inc(acc_ready, 1)
            pe.wait_ge(copied, 5 + 8)
            outs = [misc, mod_ps]

            def ret_scores(u):
                h, r = u // 6, u % 6
                b = begin(UNIT["ret"] + u)
                nc.tensor.matmul(acc[:, b, :], rk[:, h, r * P:(r + 1) * P], rq[:, h, :],
                                 start=True, stop=True).then_inc(acc_ready, 1)

            def ret_outputs(u):
                h, r = u // 6, u % 6
                emptied(pe, UNIT["ret"] + u)
                if r == 0 and h >= 2:
                    pe.wait_ge(o_copied, 8 + h - 1)
                mm = product(outs[h % 2][:, :], rv[:, r, h * P:(h + 1) * P], retP[:, u % 2, :], r, 5)
                mm.then_inc(o_ready, 1)

            for u in range(25):
                if u < 24:
                    ret_scores(u)
                if u >= 1:
                    ret_outputs(u - 1)
            for h in range(4):
                stat(1, T, c_("mean128"))

            banks = [mod_ps[:, :], misc[:, :], sums[:, 0, :], sums[:, 1, :]]
            pe.wait_ge(rstd_ready, n.job)
            pe.wait_ge(o_copied, 12)
            for d in range(2):
                base = UNIT[f"gla{d}"]
                for pr in range(2):
                    pe.wait_ge(gla_kd, 2 * d + pr + 1)
                    b = begin(base + pr)
                    for r in range(6):
                        mm = nc.tensor.transpose(acc[:, b + r // 4, (r % 4) * P:(r % 4 + 1) * P],
                                                 gkd[:, pr, r * P:(r + 1) * P], ident)
                    mm.then_inc(acc_ready, 1)
                emptied(pe, base)
                emptied(pe, base + 1)
                b = begin(base + 2)
                for pr in range(2):
                    for hh in range(2):
                        h, at = 2 * pr + hh, pr * P + hh * 64
                        for r in range(2):
                            mm = product(acc[hh * 64:hh * 64 + 64, b, pr * P:(pr + 1) * P], gkd_tok[:, 4 + r, at:at + 64],
                                         gv[:, 4 + r, h * P:(h + 1) * P], r, 1)
                mm.then_inc(acc_ready, 1)
                for pr in range(2):
                    b = begin(base + 3 + pr)
                    for c in range(NCH):
                        rows = slice(64 * (c % 2), 64 * (c % 2) + 64)
                        for hh in range(2):
                            h, at = 2 * pr + hh, pr * P + hh * 64
                            mm = nc.tensor.matmul(acc[hh * 64:hh * 64 + 64, b + c % 2, (c // 2) * P:(c // 2 + 1) * P],
                                                  gkd_tok[rows, c // 2, at:at + 64], gv[rows, c // 2, h * P:(h + 1) * P],
                                                  start=True, stop=True)
                    mm.then_inc(acc_ready, 1)
                def gla_out(h):
                    emptied(pe, base + 5 + h)
                    for r in range(4):
                        nc.tensor.matmul(banks[h][:, r * P:(r + 1) * P], gv[:, r, h * P:(h + 1) * P],
                                         gP[:, h % 2, r * P:(r + 1) * P], start=(d == 0 and r == 0), stop=False,
                                         skip_group_check=True)
                    for c in range(NCH):
                        mm = nc.tensor.matmul(banks[h][:, c * 64:c * 64 + 64], gS[:, h // 2, c, :],
                                              gqz[:, h, c * 64:c * 64 + 64], start=False,
                                              stop=(d == 1 and c == NCH - 1), skip_group_check=True)
                    mm.then_inc(gla_o, 1)

                pe.wait_ge(gla_qk, 6 * (d + 1))
                for h in range(4):
                    b = begin(base + 5 + h)
                    for r in range(4):
                        mm = nc.tensor.matmul(acc[:, b, r * P:(r + 1) * P], gkt[:, h // 2, r * P:(r + 1) * P],
                                              gqz[:, h, r * P:(r + 1) * P], start=True, stop=True)
                    mm.then_inc(acc_ready, 1)
                    if h == 0:
                        pe.wait_ge(gla_states, 12 * (d + 1))
                        emptied(pe, base + 3)
                        emptied(pe, base + 4)
                    else:
                        gla_out(h - 1)
                gla_out(3)
            pe.wait_ge(o_copied, 16)
            for h in range(4):
                stat(1, T, c_("mean128"))

            pe.wait_ge(normed, 5 + 8 + 8)
            gemm512("w_out", "w_out", 8, yT)
            stat(KD, T, c_("mean1024"))
            pe.wait_ge(h_ready, 40)
            gemm512("peer_q", "peer_q", 16, h512)
            pe.wait_ge(keys_loaded, 32)
            for g in range(2):
                b = begin(UNIT["keys"] + g)
                for j in range(8):
                    mm = nc.tensor.transpose(acc[:, b + j // 4, (j % 4) * P:(j % 4 + 1) * P], knat[:, 8 * g + j, :], ident)
                mm.then_inc(acc_ready, 1)
            emptied(pe, UNIT["keys"])
            emptied(pe, UNIT["keys"] + 1)
            for u in range(8):
                b = begin(UNIT["peer_s"] + u)
                for j in range(8):
                    a8 = 8 * (u % 2) + j
                    mm = nc.tensor.matmul(acc[:, b + j // 4, (j % 4) * P:(j % 4 + 1) * P],
                                          pq[:, a8, (u // 2) * P:(u // 2 + 1) * P], kTr[:, a8, :], start=True, stop=True)
                mm.then_inc(acc_ready, 1)
            for name, src in (("xb", h512), ("xtok", x_)):
                for t in range(4):
                    b = begin(UNIT[name] + t)
                    for j in range(KD):
                        mm = nc.tensor.transpose(acc[:, b + j // 4, (j % 4) * P:(j % 4 + 1) * P],
                                                 src[:, j, t * P:(t + 1) * P], ident)
                    mm.then_inc(acc_ready, 1)
            pe.wait_ge(rowsrc_ready, 16)
            for w in range(2):
                b = begin(UNIT["rows"] + w)
                for j in range(KD):
                    mm = nc.tensor.matmul(acc[:, b + j // 4, (j % 4) * P:(j % 4 + 1) * P], rowsrc[:, (w * KD + j), :],
                                          ident, start=True, stop=True)
                mm.then_inc(acc_ready, 1)
            emptied(pe, UNIT["rows"])
            emptied(pe, UNIT["rows"] + 1)

            for t in range(4):
                b = 2 * (t % 2)
                pe.wait_ge(tile_read, t + 1)
                for hf in range(2):
                    nc.tensor.matmul(acc[:, b + hf, :], c_("zero"), cst[:, 0:512], start=True, stop=False, skip_group_check=True)
                with pe.Fori(0, PEER_H) as h:
                    i = h + t * PEER_H
                    for k in range(PEER_K):
                        pe.wait_ge(diag_ready, i * PEER_K + (k + 1))
                        pe.wait_ge(up_loaded[k % RING], i * 32 + (16 * (k // RING) + 16))
                        for hf in range(2):
                            mm = nc.tensor.matmul(acc[:, b + hf, :], diag[:, k, :], up[:, k % RING, hf * 512:(hf + 1) * 512],
                                                  start=False, stop=False, skip_group_check=True)
                        mm.then_inc(up_used, 1)
                for hf in range(2):
                    mm = nc.tensor.matmul(acc[:, b + hf, :], c_("zero"), cst[:, 0:512], start=False, stop=True, skip_group_check=True)
                mm.then_inc(tile_done, 1)

        @block.scalar
        def _(act):
            n = Tally()

            def link(ins):
                n.step += 1
                ins.then_inc(act_step, 1)
                act.wait_ge(act_step, n.step)

            def run(o, i, func, **kw):
                return nc.scalar.activation(o, i, func, **kw)

            def unit(u):
                act.wait_ge(acc_ready, u + 1)
                return 2 * (u % 2)

            def wide(b, cols=1024):
                return acc[:, b:b + 2, :].rearrange("p a n -> p (a n)")[:, 0:cols]

            def halves(o):
                return o.rearrange("p (a t) -> p a t", a=2)

            def stat(tiles, t, source, used=0):
                for j in range(tiles):
                    if n.sq >= 2:
                        act.wait_ge(sq_used, n.sq - 1)
                    run(sq[:, n.sq % 2, 0:t], source(j), ACT.Square).then_inc(sq_ready, 1)
                    n.sq += 1
                act.wait_ge(sq_used, n.sq)
                o, mean = (logs[:, 0:T], sums[:, 0, :]) if t == T else (halves(logs[:, :]), sums[:, :, 0:HALF])
                link(run(o, mean, ACT.Ln, bias=c_("eps")))
                if used:
                    act.wait_ge(normed, used)
                run(rstd[:, 0:t], logs[:, 0:t], ACT.Exp, scale=-0.5).then_inc(rstd_ready, 1)

            def shift(norm, hid_, tile, t, stage):
                act.wait_ge(mods_ready, stage)
                for j in range(KD):
                    act.wait_ge(h_scaled, 8 * norm + j + 1)
                    ins = run(hid_[:, j, 0:T], hid_[:, j, 0:T], ACT.Identity, bias=mod[:, tile + j, 0:1])
                    if t == TC:
                        ins = run(hid_[:, j, T:TC], hid_[:, j, T:TC], ACT.Identity, bias=mod[:, tile + j, 1:2])
                    ins.then_inc(h_ready, 1)

            def silus(name, width, halves):
                units, base = 2 * halves, UNIT[name]

                def step(i, p):
                    for q in range(units):
                        u0 = base + p * units + q
                        act.wait_ge(acc_ready, i * 2 * units + (u0 + 1))
                        run(sg[:, u0 % 2, 0:width], acc[:, 2 * (u0 % 2), 0:width], ACT.Silu).then_inc(silu_ready, 1)
                pairs(act, 11, step)

            act.dma_start(cst[:, :], a["const"]).then_inc(const_loaded, 16)
            at, rows = ROWS["conv_w"]
            act.dma_start(rows1[at:at + rows, :], a["conv_w"].rearrange("l k (j q) -> (l k j) q", q=P)).then_inc(vec_loaded, 16)
            for name in ("q_norm", "k_norm"):
                for hf in range(2):
                    at = ROWS[name][0]
                    act.dma_start(rows1[at:at + 1, hf * 64:(hf + 1) * 64], a[name]).then_inc(vec_loaded, 16)
            act.dma_start(rows2[0:ADA_TILES, :], flat(a["b_ada"]).rearrange("(r q) -> r q", q=P)).then_inc(vec_loaded, 16)
            act.dma_start(rows2[ADA_TILES:N_BIAS, :], flat(a["b_mod_2"]).rearrange("(r q) -> r q", q=P)).then_inc(vec_loaded, 16)
            act.dma_start(dec[:, 0:4], a["ret_decay_f_2"].to_broadcast([P, 4])).then_inc(vec_loaded, 16)
            act.dma_start(dec[:, 4:8], a["ret_decay_b_2"].to_broadcast([P, 4])).then_inc(vec_loaded, 16)
            act.wait_ge(rows_zeroed, 1)
            act.dma_start(gkup[0:16, 0:256], a["gla_gk_up_f_2"][0]).then_inc(vec_loaded, 16)
            act.dma_start(gkup[16:32, 256:512], a["gla_gk_up_b_2"][0]).then_inc(vec_loaded, 16)

            for r in range(1, 6, 2):
                u = UNIT["tokens"] + r
                b = unit(u)
                run(x_[:, :, r * P:(r + 1) * P], wide(b).rearrange("p (j t) -> p j t", j=KD), ACT.Copy).then_inc(acc_free[u % 2], 1)
            act.wait_ge(vec_ready, 1)
            for blk, pair in enumerate((("c", "c_ctx"), ("c_2", "c_ctx_2"))):
                for w, name in enumerate(pair):
                    run(cnd[:, blk, :, w], v_(name, 0, KD), ACT.Silu).then_inc(cond_ready, 1)

            emptied(act, UNIT["tokens"] + 4)
            emptied(act, UNIT["tokens"] + 5)
            stat(KD, TC, lambda j: x_[:, j, :])
            act.wait_ge(decay_abs, 1)
            run(dec[:, 16:24], dec[:, 8:16], ACT.Exp, scale=-1.0).then_inc(decay_exp, 1)
            shift(0, h768, 0, TC, 1)
            silus("ffn1_in", HALF, 2)

            def updated(name, j, units):
                for q in range(units):
                    emptied(act, UNIT[name] + units * j + q)
                return x_[:, j, :] if units == 2 else x_[:, j, 0:T]

            stat(KD, TC, lambda j: updated("ffn1_out", j, 2))
            shift(1, h768, 3 * KD, TC, 2)

            def take(name, t, o, func=ACT.Copy, cols=T):
                u = UNIT[name] + t
                b = unit(u)
                src = acc[:, b, 0:T] if cols == T else acc[:, b:b + 2, 0:HALF]
                run(o, src, func).then_inc(acc_free[u % 2], 1)

            for t in range(4):
                take("q", t, qT[:, t, :])
            take("k", 0, halves(kT), cols=TC)
            for v in range(2):
                u = UNIT["v"] + v
                b = unit(u)
                run(vtok[:, 3 * v:3 * v + 3, :], acc[:, b, 0:3 * P].rearrange("p (r n) -> p r n", r=3), ACT.Copy).then_inc(acc_free[u % 2], 1)
            for t in range(4):
                take("gb", t, gb[:, t, :])
            for t in range(4):
                take("gc", t, gc[:, t, :])

            def own(u, src):
                emptied(act, u)
                return src

            for t in range(4):
                stat(1, T, lambda j, t=t: own(UNIT["q"] + t, qT[:, t, :]), t)
            stat(1, TC, lambda j: own(UNIT["k"], kT), 4)
            for kv in range(KV_HEADS):
                take("kdup", kv, halves(kdup[:, kv, :]), cols=TC)

            def branch(j):
                act.wait_ge(conv_ready, j + 1)
                return mixT[:, 4 + j, :]
            stat(4, T, branch)

            for step in range(32 + 4):
                if step < 32:
                    u = UNIT["scores"] + step
                    act.wait_ge(negmax_ready, step + 1)
                    if step >= 3:
                        act.wait_ge(probT_ready, step - 2)
                    b = unit(u)
                    run(halves(prob[:, step % 3, :]), acc[:, b:b + 2, 0:HALF], ACT.Exp, scale=HD ** -0.5,
                        bias=small[:, step % 2:step % 2 + 1], accum_out=small[:, 2 + step % 2:3 + step % 2]).then_inc(exp_ready, 1)
                if 3 <= step < 35:
                    u = step - 3
                    act.wait_ge(probT_ready, u + 1)
                    if u >= 8:
                        act.wait_ge(o_ready, u // 4 - 1)
                    run(probT[:, (u // 4) % 2, 0:3, (u % 4) * P:(u % 4 + 1) * P],
                        sums[:, 0, 0:HALF].rearrange("p (r n) -> p r n", r=3), ACT.Copy).then_inc(probT_act, 1)
                if step >= 7 and (step - 7) % 4 == 0 or step == 35:
                    h = (step - 7) // 4
                    act.wait_ge(o_ready, h + 1)
                    rows = slice(64 * (h % 2), 64 * (h % 2) + 64)
                    run(mixT[rows, h // 2, :], misc[rows, :], ACT.Copy).then_inc(o_copied, 1)

            def heads(j):
                act.wait_ge(o_copied, 8)
                return mixT[:, j, :]
            stat(4, T, heads)

            stat(KD, T, lambda j: updated("mix_out", j, 1))
            shift(2, h512, 6 * KD, T, 2)
            silus("ffn2_in", T, 1)
            stat(KD, T, lambda j: updated("ffn2_out", j, 1))

            def renormed(j):
                act.wait_ge(x1_ready, j + 1)
                emptied(act, UNIT["tokens2"])
                emptied(act, UNIT["tokens2"] + 1)
                return x_[:, j, :]
            stat(KD, TC, renormed)
            shift(3, h768, ADA_TILES, TC, 3)

            for t in range(4):
                take("rq", t, rq[:, t, :])
            for t in range(4):
                take("rk", t, halves(rk[:, t, :]), cols=TC)
            for t in range(4):
                take("rg", t, yT[:, t, :], ACT.Silu)
            for t in range(2):
                take("gq", t, gq[:, t, :])
            for t in range(2):
                take("gk", t, halves(gk[:, t, :]), cols=TC)
            for t in range(4):
                take("gg", t, yT[:, 4 + t, :], ACT.Silu)

            soft = sq[:, 0, :]
            act.wait_ge(sq_used, n.sq)
            for u in range(4):
                emptied(act, UNIT["decay"] + u)
                if u:
                    act.wait_ge(la_ready, u)
                link(run(soft, la[:, u // 2, u % 2, :], ACT.Abs))
                link(run(soft, soft, ACT.Exp, scale=-1.0))
                run(soft, soft, ACT.Ln, bias=1.0).then_inc(ln_ready, 1)

            def ret_out(h):
                act.wait_ge(o_ready, 8 + 6 * (h + 1))
                run(rq[:, h, :], [misc, mod_ps][h % 2][:, :], ACT.Copy).then_inc(o_copied, 1)

            for h in range(4):
                act.wait_ge(dist_arg, h + 1)
                if h:
                    act.wait_ge(dist_done, h)
                run(DX[:, h % 2, :], DX[:, h % 2, :], ACT.Exp)
                run(DC[:, h % 2, :], dist[:, T:], ACT.Exp, scale=dec[:, 8 + h:9 + h])
                run(sq[:, 1, 0:N_DC], dist[:, T:], ACT.Exp, scale=dec[:, 16 + h:17 + h],
                    bias=dec[:, 20 + h:21 + h]).then_inc(dist_exp, 1)
                if h:
                    ret_out(h - 1)
            ret_out(3)
            for h in range(4):
                def head(j, h=h):
                    act.wait_ge(o_copied, 9 + h)
                    return rq[:, h, :]
                stat(1, T, head, 13 + h)

            for d in range(2):
                base = UNIT[f"gla{d}"]
                e = (gE if d == 0 else gkd)[:, :, 0:T]
                g = (gG if d == 0 else gE)[:, :, 0:T]
                act.wait_ge(gla_arg, 2 * d + 1)
                run(gla_decay,
                    gG[:, :, 0:T].rearrange("p a (c i) -> p a c i", i=CHUNK)[:, :, :, CHUNK - 1],
                    ACT.Exp, scale=1.0 / GATE_NORM)
                if d:
                    act.wait_ge(acc_ready, UNIT["gla0"] + 2)
                run(e, g, ACT.Exp, scale=1.0 / GATE_NORM).then_inc(gla_exp, 1)
                act.wait_ge(gla_qk, 6 * d + 4)
                run(e, g, ACT.Exp, scale=-1.0 / GATE_NORM).then_inc(gla_exp, 1)
                act.wait_ge(gla_arg, 2 * d + 2)
                run(gE, gE, ACT.Exp, scale=1.0 / GATE_NORM).then_inc(gla_exp, 1)
                for pr in range(2):
                    u = base + pr
                    b = unit(u)
                    run(gkd_tok[:, :, pr * P:(pr + 1) * P], wide(b, 6 * P).rearrange("p (r n) -> p r n", r=6),
                        ACT.Copy).then_inc(acc_free[u % 2], 1)
            banks = [mod_ps[:, :], misc[:, :], sums[:, 0, :], sums[:, 1, :]]
            for h in range(4):
                act.wait_ge(gla_o, 4 + h + 1)
                run(og[:, h, :], banks[h], ACT.Copy).then_inc(o_copied, 1)
            for h in range(4):
                def head(j, h=h):
                    act.wait_ge(o_copied, 13 + h)
                    return og[:, h, :]
                stat(1, T, head, 17 + h)

            stat(KD, T, lambda j: updated("w_out", j, 1))
            shift(4, h512, ADA_TILES + 3 * KD, T, 3)
            for t in range(0, 16, 2):
                take("peer_q", t, pq[:, t, :])
            for u0 in range(0, 8, 2):
                u = UNIT["peer_s"] + u0
                b = unit(u)
                run(s_all[:, u0 // 2, 0:1024], wide(b), ACT.Copy).then_inc(acc_free[u % 2], 1)
            for name, dst in (("xb", xb), ("xtok", xtok)):
                for t in range(0, 4, 2):
                    u = UNIT[name] + t
                    b = unit(u)
                    run(dst[:, t, :], wide(b), ACT.Copy).then_inc(acc_free[u % 2], 1)
            for w, dst in enumerate((g2row, nfrow)):
                u = UNIT["rows"] + w
                b = unit(u)
                run(dst, wide(b), ACT.Copy).then_inc(acc_free[u % 2], 1)

            def softmax_exp(count):
                act.wait_ge(top_ready, count)
                run(p_exp, p_top, ACT.Exp, bias=p_neg, accum_out=p_sum).then_inc(p_exp_ready, 1)

            def expert_weights(i):
                act.wait_ge(dots_done, (i + 1) * PEER_K + RING)
                run(p_act, p_dot, ACT.Gelu).then_inc(gelu_ready, 1)
                act.wait_ge(weights_ready, i + 1)
                for k in range(PEER_K):
                    act.wait_ge(up_used, i * PEER_K + (k + 1))
                    run(diag[:, k, :], ident, ACT.Copy, scale=p_w[:, k:k + 1]).then_inc(diag_ready, 1)

            def expert_heads(first, last):
                with act.Fori(first, last) as i:
                    softmax_exp(i + 2)
                    expert_weights(i)

            def final_std(t):
                act.wait_ge(ssq_ready, t + 1)
                run(p_std, p_ssq, ACT.Sqrt, scale=1.0 / D, bias=c_("eps")).then_inc(fstd_ready, 1)

            softmax_exp(1)
            for t in range(4):
                first = t * PEER_H
                expert_heads(first, first + 1)
                if t:
                    final_std(t - 1)
                expert_heads(first + 1, first + PEER_H - (t == 3))
            expert_weights(4 * PEER_H - 1)
            final_std(3)

        @block.vector
        def _(dve):
            n = Tally()
            V = nc.vector

            def link(ins):
                n.step += 1
                ins.then_inc(dve_step, 1)
                dve.wait_ge(dve_step, n.step)

            def unit(u):
                dve.wait_ge(acc_ready, u + 1)
                return 2 * (u % 2)

            def free(ins, u):
                ins.then_inc(acc_free[u % 2], 1)

            def wide(b, cols=1024):
                return acc[:, b:b + 2, :].rearrange("p a n -> p (a n)")[:, 0:cols]

            def halves(o):
                return o.rearrange("p (a t) -> p a t", a=2)

            def stat():
                n.job += 1
                dve.wait_ge(rstd_ready, n.job)

            def scale(norm, hid_, t):
                for j in range(KD):
                    ins = V.scalar_tensor_tensor(hid_[:, j, 0:T], x_[:, j, 0:T], gain[:, norm, j, 0:1], rstd[:, 0:T],
                                                 ALU.mult, ALU.mult)
                    if t == TC:
                        ins = V.scalar_tensor_tensor(hid_[:, j, T:TC], x_[:, j, T:TC], gain[:, norm, j, 1:2], rstd[:, T:TC],
                                                     ALU.mult, ALU.mult)
                    ins.then_inc(h_scaled, 1)

            def modulation(stage, first, last, gain_of, half_of):
                if stage == 1:
                    dve.wait_ge(first_used, 8)
                else:
                    dve.wait_ge(partial_used, CREDIT + last - FIRST_MODS)
                link(V.tensor_tensor(mod[:, first:last, :],
                                     mod_ps[:, 2 * first:2 * last].rearrange("p (t c) -> p t c", c=2),
                                     vec[:, 128 + first:128 + last].unsqueeze(2).to_broadcast([P, last - first, 2]), ALU.add))
                for norm, name, tile in gain_of:
                    ins = V.scalar_tensor_tensor(gain[:, norm], mod[:, tile:tile + KD, :], 1.0,
                                                 v_(name, 0, KD).unsqueeze(2).to_broadcast([P, KD, 2]), ALU.add, ALU.mult)
                for ffn, tile in half_of:
                    ins = V.tensor_scalar(hgate[:, ffn], mod[:, tile:tile + KD, :], 0.5, None, ALU.mult)
                ins.then_inc(mods_ready, 1)
                dve.wait_ge(mods_ready, stage)

            def mod_products(p, m, uses, blk):
                dve.wait_ge(partial_used, m + 1)
                dve.wait_ge(mod_loaded[p], uses * 16)
                for k in range(KD):
                    if k:
                        dve.wait_ge(mod_step, m * (KD - 1) + k)
                    for c in range(2):
                        sum_, w, x1 = partial[:, p, c, :], Mw[:, p, k, :], cnd[:, blk, k, c:c + 1]
                        if k == 0:
                            ins = V.tensor_scalar(sum_, w, x1, None, ALU.mult)
                        else:
                            ins = V.scalar_tensor_tensor(sum_, w, x1, sum_, ALU.mult, ALU.add)
                    ins.then_inc(mod_step if k < KD - 1 else partial_ready, 1)

            def swiglu(name, width, sides, done, blk, first, per, count):
                units, base = 2 * sides, UNIT[name]

                def step(i, p):
                    for q in range(units):
                        u0 = base + p * units + q
                        sub, hf = q // sides, q % sides
                        for tile in range(q * per // units, (q + 1) * per // units):
                            n0 = p * per + first + tile
                            mod_products(n0 % 2, i * (2 * per) + n0, i * per + (n0 // 2 + 1), blk)
                        dve.wait_ge(silu_ready, i * 2 * units + (done + p * units + q + 1))
                        free(V.tensor_tensor(arena[:, ds(i * 4 * width * sides + ((2 * p + sub) * sides + hf) * width, width)],
                                             sg[:, u0 % 2, 0:width], acc[:, 2 * (u0 % 2) + 1, 0:width], ALU.mult), u0)
                pairs(dve, 11, step)
                for m in range(first + 11 * per, first + count):
                    mod_products(m % 2, m, m // 2 + 1, blk)

            def residual(name, sides, ffn):
                base = UNIT[name]

                def step(i, p):
                    for hf in range(sides):
                        u0 = base + p * sides + hf
                        dve.wait_ge(acc_ready, i * 2 * sides + (u0 + 1))
                        at, b = 0, 2 * (u0 % 2)
                        parts = [(0, 0, T)] if sides == 1 else [(0, 0, HALF)] if hf == 0 else [(0, HALF, T), (1, T, TC)]
                        for kind, lo, hi_ in parts:
                            x1 = resid[:, ds(i * 2 * TC + (p * TC + lo), hi_ - lo)]
                            ins = V.scalar_tensor_tensor(x1, acc[:, b, at:at + hi_ - lo],
                                                         halfg[:, ds(i * 4 + (16 * ffn + 2 * p + kind), 1)], x1,
                                                         ALU.mult, ALU.add)
                            at += hi_ - lo
                        free(ins, u0)
                pairs(dve, KD, step)

            dve.sem_inc(partial_used, CREDIT)
            V.memset(gkup[:, :], 0.0).then_inc(rows_zeroed, 1)
            for r in range(0, 6, 2):
                u = UNIT["tokens"] + r
                b = unit(u)
                free(V.tensor_copy(x_[:, :, r * P:(r + 1) * P], wide(b).rearrange("p (j t) -> p j t", j=KD)), u)
            dve.wait_ge(vec_turned, 1)
            V.tensor_copy(vec[:, 0:N_ROWS], misc[:, 0:N_ROWS])
            V.tensor_copy(vec[:, 128:128 + N_BIAS], misc[:, 128:128 + N_BIAS]).then_inc(vec_ready, 1)
            dve.wait_ge(vec_ready, 1)
            dve.wait_ge(vec_loaded, 16 * N_VEC_DMAS)
            V.scalar_tensor_tensor(dec[:, 8:16], dec[:, 0:8], -1.0, dec[:, 0:8], ALU.mult, ALU.max).then_inc(decay_abs, 1)
            stat()
            modulation(1, 0, FIRST_MODS, [(0, "norm_ffn1", KD)], [])
            scale(0, h768, TC)
            dve.wait_ge(decay_exp, 1)
            z, s_, s2, series, least = (dec[:, 16 + 8 * i:24 + 8 * i] for i in range(5))
            link(V.tensor_scalar(s2, z, 2.0, None, ALU.add))
            link(V.reciprocal(s2, s2))
            link(V.tensor_tensor(s_, z, s2, ALU.mult))
            link(V.tensor_tensor(s2, s_, s_, ALU.mult))
            link(V.tensor_scalar(series, s2, 1.0 / 19, None, ALU.mult))
            for odd in range(17, 1, -2):
                link(V.scalar_tensor_tensor(series, series, 1.0 / odd, s2, ALU.add, ALU.mult))
            link(V.scalar_tensor_tensor(series, series, 1.0, s_, ALU.add, ALU.mult))
            link(V.tensor_scalar(least, dec[:, 0:8], 0.0, None, ALU.min))
            link(V.scalar_tensor_tensor(dec[:, 8:16], series, -2.0, least, ALU.mult, ALU.add))
            V.tensor_scalar(dec[:, 16:20], dec[:, 12:16], -1.0, None, ALU.mult)
            link(V.tensor_scalar(dec[:, 20:24], dec[:, 12:16], 640.0 + P, None, ALU.mult))

            swiglu("ffn1_in", HALF, 2, 0, 0, 0, MOD_PER_SLOT[0], ADA_LATER)
            modulation(2, FIRST_MODS, ADA_TILES, [(1, "norm_mix", 4 * KD), (2, "norm_ffn2", 7 * KD)],
                       [(0, 2 * KD), (1, 8 * KD)])
            residual("ffn1_out", 2, 0)
            stat()
            scale(1, h768, TC)

            V.memset(cu[:, :, 0:1], 0.0)
            V.memset(cu[:, :, T + 1:T + 2], 0.0)
            for t in range(4):
                u = UNIT["u"] + t
                emptied(dve, UNIT["gc"] + t)
                b = unit(u)
                free(V.tensor_tensor(cu[:, t, 1:T + 1], acc[:, b, :], gc[:, t, :], ALU.mult), u)
            for t in range(5):
                width, dst = (T, qT[:, t, :]) if t < 4 else (TC, kT)
                stat()
                V.scalar_tensor_tensor(dst, dst, v_("q_norm" if t < 4 else "k_norm"), rstd[:, 0:width],
                                       ALU.mult, ALU.mult).then_inc(normed, 1)

            def rope(u, dst, cos, sin, before):
                b = unit(u)
                if before:
                    dve.wait_ge(copied, before)
                free(V.tensor_tensor(tmp[:, 0:T], acc[:, b, :], sin, ALU.mult), u)
                link(V.tensor_tensor(dst, dst, cos, ALU.mult))
                V.tensor_tensor(dst, dst, tmp[:, 0:T], ALU.add).then_inc(copied, 1)

            dve.wait_ge(pairs_loaded, 16)
            for t in range(5):
                rope(UNIT["rope_q"] + t, qT[:, t, :] if t < 4 else kT[:, 0:T], cos_pairs, sin_pairs, t)
            for t in range(4):
                y = mixT[:, 4 + t, :]
                emptied(dve, UNIT["gb"] + t)
                link(V.tensor_scalar(y, cu[:, t, 0:T], v_("conv_w", t), None, ALU.mult))
                for tap in (1, 2):
                    link(V.scalar_tensor_tensor(y, cu[:, t, tap:tap + T], v_("conv_w", tap * 4 + t), y, ALU.mult, ALU.add))
                V.tensor_tensor(y, y, gb[:, t, :], ALU.mult).then_inc(conv_ready, 1)

            def branch_norm(first, name):
                stat()
                for t in range(4):
                    y = mixT[:, first + t, :]
                    V.scalar_tensor_tensor(y, y, v_(name, t), rstd[:, 0:T], ALU.mult, ALU.mult).then_inc(normed, 1)
            branch_norm(4, "conv_out_norm")

            for step in range(32 + 3):
                if 1 <= step < 33:
                    u = step - 1
                    inv = small[:, 16 + u % 4:17 + u % 4]
                    dve.wait_ge(exp_ready, u + 1)
                    free(V.reciprocal(inv, small[:, 2 + u % 2:3 + u % 2]), UNIT["scores"] + u)
                    emptied(dve, UNIT["scores"] + u)
                    V.tensor_scalar(prob[:, u % 3, :], prob[:, u % 3, :], inv, None, ALU.mult).then_inc(prob_ready, 1)
                if step < 32:
                    b = unit(UNIT["scores"] + step)
                    top = small[:, 8 + step % 2:9 + step % 2]
                    link(V.tensor_reduce(top, acc[:, b:b + 2, 0:HALF], mybir.AxisListType.XY, ALU.max))
                    V.tensor_scalar(small[:, step % 2:step % 2 + 1], top, -HD ** -0.5, None, ALU.mult).then_inc(negmax_ready, 1)
                if step >= 3:
                    u = step - 3
                    dve.wait_ge(probT_ready, u + 1)
                    if u >= 8:
                        dve.wait_ge(o_ready, u // 4 - 1)
                    V.tensor_copy(probT[:, (u // 4) % 2, 3:6, (u % 4) * P:(u % 4 + 1) * P],
                                  sums[:, 1, 0:HALF].rearrange("p (r n) -> p r n", r=3)).then_inc(probT_dve, 1)
            branch_norm(0, "attn_out_norm")

            def gated_residual(name, gate_tile):
                for j in range(KD):
                    u = UNIT[name] + j
                    b = unit(u)
                    free(V.scalar_tensor_tensor(x_[:, j, 0:T], acc[:, b, :], mod[:, gate_tile + j, 0:1], x_[:, j, 0:T],
                                                ALU.mult, ALU.add), u)
            gated_residual("mix_out", 5 * KD)

            stat()
            scale(2, h512, T)
            swiglu("ffn2_in", T, 1, 44, 1, ADA_LATER, MOD_PER_SLOT[1], MOD_TILES)
            blk2 = ADA_TILES
            modulation(3, blk2, N_BIAS, [(3, "norm1_w_2", blk2 + KD), (4, "norm2_w_2", blk2 + 4 * KD)], [])
            residual("ffn2_out", 1, 1)
            for r in range(2):
                u = UNIT["tokens2"] + r
                b = unit(u)
                free(V.tensor_copy(x_[:, :, T + r * P:T + (r + 1) * P], wide(b).rearrange("p (j t) -> p j t", j=KD)), u)
            stat()
            for j in range(KD):
                V.scalar_tensor_tensor(x_[:, j, 0:T], x_[:, j, 0:T], v_("final_norm", j), rstd[:, 0:T],
                                       ALU.mult, ALU.mult).then_inc(x1_ready, 1)
            stat()
            scale(3, h768, TC)

            def take(name, t, o, src):
                u = UNIT[name] + t
                b = unit(u)
                free(V.tensor_copy(o, src(b)), u)

            for r in range(6):
                take("rv", r, rv[:, r, :], lambda b: acc[:, b, :])
            for r in range(6):
                take("gv", r, gv[:, r, :], lambda b: acc[:, b, :])
            take("lr", 0, halves(lr), lambda b: acc[0:32, b:b + 2, 0:HALF])

            dve.wait_ge(halves_loaded, 16)
            for t in range(8):
                rope(UNIT["rope_r"] + t, rq[:, t, :] if t < 4 else rk[:, t - 4, 0:T], cos_halves, sin_halves, 5 + t)

            soft = sq[:, 0, :]
            for u in range(4):
                b = unit(UNIT["decay"] + u)
                free(V.tensor_scalar(halves(la[:, u // 2, u % 2, :]), acc[:, b:b + 2, 0:HALF],
                                     v_(("gla_gk_bias_f_2", "gla_gk_bias_b_2")[u // 2], u % 2), None, ALU.add), UNIT["decay"] + u)
            for u in range(4):
                dve.wait_ge(ln_ready, u + 1)
                z = la[:, u // 2, u % 2, :]
                V.scalar_tensor_tensor(z, z, 0.0, soft, ALU.min, ALU.subtract).then_inc(la_ready, 1)

            def distances(h):
                x1 = DX[:, h % 2, :]
                link(V.tensor_scalar(x1, dist[:, 0:N_DX], dec[:, 16 + h:17 + h], None, ALU.mult))
                V.scalar_tensor_tensor(x1, dist[:, 0:N_DX], dec[:, 8 + h:9 + h], x1,
                                       ALU.mult, ALU.min).then_inc(dist_arg, 1)

            dve.wait_ge(dist_loaded, 16)
            distances(0)
            distances(1)
            for h in range(4):
                dve.wait_ge(dist_exp, h + 1)
                V.tensor_tensor(DX[:, h % 2, 384:384 + P], DX[:, h % 2, 384:384 + P], ident, ALU.add)
                V.tensor_tensor(DC[:, h % 2, :], DC[:, h % 2, :], sq[:, 1, 0:N_DC], ALU.add).then_inc(dist_done, 1)
                dve.wait_ge(dist_done, h + 1)
                for r in range(6):
                    u = 6 * h + r
                    b = unit(UNIT["ret"] + u)
                    if u >= 2:
                        dve.wait_ge(o_ready, 8 + u - 1)
                    decay = DX[:, h % 2, 384 - P * r:384 - P * r + T] if r < 4 else DC[:, h % 2, P - P * (r - 4):P - P * (r - 4) + T]
                    free(V.scalar_tensor_tensor(retP[:, u % 2, :], acc[:, b, :], RET_SCALE, decay, ALU.mult, ALU.mult), UNIT["ret"] + u)
                if h + 2 < 4:
                    emptied(dve, UNIT["ret"] + 6 * h + 5)
                    distances(h + 2)

            def head_norm(o, gate):
                stat()
                link(V.tensor_tensor(o, o, rstd[:, 0:T], ALU.mult))
                V.tensor_tensor(gate, gate, o, ALU.mult).then_inc(normed, 1)
            for h in range(4):
                head_norm(rq[:, h, :], yT[:, h, :])

            def chunks(x1):
                return x1.rearrange("p (c i) -> p c i", i=CHUNK)

            dve.wait_ge(o_ready, 8 + 24)
            for d in range(2):
                base = UNIT[f"gla{d}"]
                for pr in range(2):
                    ins = V.tensor_tensor_scan(gG[:, pr, :], c_("chunk_reset"), la[:, d, pr, :], 0.0, ALU.mult, ALU.add)
                if d == 0:
                    ins.then_inc(gla_arg, 1)
                    dve.wait_ge(gla_arg, 1)
                else:
                    link(ins)
                    for pr in range(2):
                        G4 = chunks(gG[:, pr, 0:T])
                        ins = V.tensor_tensor(chunks(gE[:, pr, 0:T]), G4[:, :, CHUNK - 1:CHUNK].to_broadcast([P, NCH, CHUNK]), G4, ALU.subtract)
                    link(ins)
                    for pr in range(2):
                        ins = V.tensor_tensor(gE[:, pr, 0:T], gE[:, pr, 0:T], la[:, d, pr, 0:T], ALU.add)
                    ins.then_inc(gla_arg, 1)
                    dve.wait_ge(gla_o, 4)
                e = gE if d == 0 else gkd
                dve.wait_ge(gla_exp, 3 * d + 1)
                for h in range(4):
                    V.scalar_tensor_tensor(gqz[:, h, :], gq[:, h // 2, :], c_("head_rows")[:, h % 2:h % 2 + 1], e[:, h // 2, 0:T],
                                           ALU.mult, ALU.mult).then_inc(gla_qk, 1)
                dve.wait_ge(gla_exp, 3 * d + 2)
                for pr in range(2):
                    V.tensor_tensor(gkt[:, pr, :], gk[:, pr, 0:T], e[:, pr, 0:T], ALU.mult).then_inc(gla_qk, 1)
                dve.wait_ge(gla_qk, 6 * (d + 1))
                for pr in range(2):
                    if d == 0:
                        G4 = chunks(gG[:, pr, 0:T])
                        V.tensor_tensor(chunks(gE[:, pr, 0:T]), G4[:, :, CHUNK - 1:CHUNK].to_broadcast([P, NCH, CHUNK]), G4, ALU.subtract)
                        ins = V.tensor_tensor(gE[:, pr, T:TC], gG[:, pr, TC - 1:TC].to_broadcast([P, C]), gG[:, pr, T:TC], ALU.subtract)
                    else:
                        ins = V.tensor_tensor(gE[:, pr, :], gG[:, pr, :], la[:, d, pr, :], ALU.subtract)
                ins.then_inc(gla_arg, 1)
                dve.wait_ge(gla_exp, 3 * d + 3)
                for pr in range(2):
                    V.tensor_tensor(gkd[:, pr, :], gk[:, pr, :], gE[:, pr, :], ALU.mult).then_inc(gla_kd, 1)
                link(V.memset(gP[:, :, :], 0.0))
                u = base + 2
                b = unit(u)
                order = list(range(NCH)) if d == 0 else list(range(NCH - 1, -1, -1))
                free(V.tensor_copy(gS[:, :, order[0], :], acc[:, b, 0:2 * P].rearrange("p (a v) -> p a v", a=2)), u)
                emptied(dve, u)
                for pr in range(2):
                    u = base + 3 + pr
                    b = unit(u)
                    for i in range(NCH - 1):
                        c = order[i]
                        ins = V.scalar_tensor_tensor(gS[:, pr, order[i + 1], :], gS[:, pr, c, :], gla_decay[:, pr, c:c + 1],
                                                     acc[:, b + c % 2, (c // 2) * P:(c // 2 + 1) * P], ALU.mult, ALU.add)
                        if i < NCH - 2:
                            ins.then_inc(gla_states, 1)
                            dve.wait_ge(gla_states, 12 * d + 6 * pr + i + 1)
                        else:
                            free(ins, u)
                mask = c_(("causal_f", "causal_b")[d]).bitcast(I32).unsqueeze(1).to_broadcast([P, 4, P])
                for h in range(4):
                    u = base + 5 + h
                    b = unit(u)
                    if h >= 2:
                        dve.wait_ge(gla_o, 4 * d + h - 1)
                    free(V.copy_predicated(gP[:, h % 2, :].rearrange("p (r n) -> p r n", r=4), mask,
                                           acc[:, b, :].rearrange("p (r n) -> p r n", r=4)), u)
            for h in range(4):
                head_norm(og[:, h, :], yT[:, 4 + h, :])

            gated_residual("w_out", ADA_TILES + 2 * KD)
            stat()
            scale(4, h512, T)
            for t in range(1, 16, 2):
                take("peer_q", t, pq[:, t, :], lambda b: acc[:, b, :])
            for g in range(2):
                take("keys", g, kTr[:, 8 * g:8 * g + 8, :], lambda b: wide(b).rearrange("p (j n) -> p j n", j=8))
            for g in range(2):
                emptied(dve, UNIT["keys"] + g)
            for w in range(2):
                for j in range(KD):
                    col = mod[:, ADA_TILES + 5 * KD + j, 0:1] if w == 0 else v_("norm_f_w_2", j)
                    V.tensor_scalar(rowsrc[:, w * KD + j, :], ones, col, None, ALU.mult).then_inc(rowsrc_ready, 1)
            for u0 in range(1, 8, 2):
                take("peer_s", u0, s_all[:, u0 // 2, 1024:2048], wide)
            TOPK_STEPS = 14

            def topk(i):
                done = [0]

                def step(ins):
                    done[0] += 1
                    ins.then_inc(topk_step, 1)
                    dve.wait_ge(topk_step, i * TOPK_STEPS + done[0])
                    dve.sem_inc(dve_go, 1)

                side = [slice(0, P), slice(P, 2 * P)]
                step(V.tensor_copy(s_cur, arena[:, ds(i * 256 + 8192, 256)]))
                for m in range(2):
                    ins = V.max(key_top[:, 16 * m:16 * m + 8], s_cur[:, side[m]])
                step(ins)
                for m in range(2):
                    V.max_index(key_at[:, 16 * m:16 * m + 8], key_top[:, 16 * m:16 * m + 8], s_cur[:, side[m]])
                    ins = V.match_replace(s_less[:, side[m]], key_top[:, 16 * m:16 * m + 8], s_cur[:, side[m]], -3e38)
                step(ins)
                for m in range(2):
                    ins = V.max(key_top[:, 16 * m + 8:16 * m + 16], s_less[:, side[m]])
                step(ins)
                for m in range(2):
                    V.max_index(key_at[:, 16 * m + 8:16 * m + 16], key_top[:, 16 * m + 8:16 * m + 16], s_less[:, side[m]])
                step(V.tensor_tensor(cand.rearrange("p (a b) -> p a b", a=16), key_top[:, 0:16].unsqueeze(2).to_broadcast([P, 16, 16]),
                                     key_top[:, 16:32].unsqueeze(1).to_broadcast([P, 16, 16]), ALU.add))
                V.tensor_copy(key_no, key_at)
                step(V.max(p_top[:, 0:8], cand))
                V.max_index(cand_at[:, 0:8], p_top[:, 0:8], cand)
                step(V.match_replace(cand_less, p_top[:, 0:8], cand, -3e38))
                step(V.max(p_top[:, 8:16], cand_less))
                V.tensor_scalar(p_neg, p_top[:, 0:1], -1.0, None, ALU.mult).then_inc(top_ready, 1)
                step(V.max_index(cand_at[:, 8:16], p_top[:, 8:16], cand_less))
                V.tensor_scalar(cand_half[:, 0:16], cand_at, 4, None, ALU.logical_shift_right)
                step(V.tensor_scalar(cand_half[:, 16:32], cand_at, 15, None, ALU.bitwise_and))
                step(V.tensor_copy(cand_no, cand_half))
                pick = onehot.rearrange("p (k j) -> p k j", k=32)
                step(V.tensor_tensor(pick, cand_no.unsqueeze(2).to_broadcast([P, 32, 16]),
                                     c_("iota16").unsqueeze(1).to_broadcast([P, 32, 16]), ALU.is_equal))
                for m in range(2):
                    half = pick[:, 16 * m:16 * m + 16, :]
                    ins = V.tensor_tensor(half, half, key_no[:, 16 * m:16 * m + 16].unsqueeze(1).to_broadcast([P, 16, 16]), ALU.mult)
                step(ins)
                step(V.tensor_reduce(chosen, pick, AX_X, ALU.add))
                V.scalar_tensor_tensor(idx_all[:, ds(i * PEER_K, PEER_K)], chosen[:, 0:16], float(N_KEYS), chosen[:, 16:32],
                                       ALU.mult, ALU.add).then_inc(idx_ready, 1)
                assert done[0] == TOPK_STEPS

            def softmax(i):
                dve.wait_ge(p_exp_ready, i + 1)
                dve.sem_inc(dve_go, 1)
                V.reciprocal(p_inv, p_sum).then_inc(inv_ready, 1)
                dve.wait_ge(inv_ready, i + 1)
                V.tensor_scalar(g_all[:, ds(i * PEER_K, PEER_K)], p_exp, p_inv, None, ALU.mult)

            def dots(t, i):
                for s in range(PEER_K):
                    dve.wait_ge(down_loaded[s % RING], i * 32 + 16 * (s // RING + 1))
                    V.scalar_tensor_tensor(down[:, s % RING, :], down[:, s % RING, :], 1.0, xb[:, t, :], ALU.mult, ALU.mult,
                                           accum_out=p_dot[:, s:s + 1]).then_inc(dots_done, 1)

            def weights(i):
                dve.wait_ge(gelu_ready, i + 1)
                V.tensor_tensor(p_w, p_act, g_all[:, ds(i * PEER_K, PEER_K)], ALU.mult).then_inc(weights_ready, 1)

            def finish(t):
                dve.wait_ge(tile_done, t + 1)
                if t:
                    dve.wait_ge(out_stored, t * 16)
                V.tensor_tensor(fin, acc[:, 2 * (t % 2):2 * (t % 2) + 2, :].rearrange("p a n -> p (a n)"), g2row,
                                ALU.mult).then_inc(tile_read, 1)
                dve.wait_ge(tile_read, CREDIT + t + 1)
                link(V.tensor_tensor(fin, fin, xtok[:, t, :], ALU.add))
                V.scalar_tensor_tensor(junk, fin, 1.0, fin, ALU.mult, ALU.mult, accum_out=p_ssq).then_inc(ssq_ready, 1)
                dve.wait_ge(fstd_ready, t + 1)
                link(V.reciprocal(p_rstd, p_std))
                V.scalar_tensor_tensor(fin, fin, p_rstd, nfrow, ALU.mult, ALU.mult).then_inc(fin_ready, 1)

            def heads(t, first, last):
                with dve.Fori(t * PEER_H + first, t * PEER_H + last) as i:
                    topk(i + 1)
                    dots(t, i)
                    softmax(i + 1)
                    weights(i)

            emptied(dve, UNIT["peer_s"])
            topk(0)
            for name, dst in (("xb", xb), ("xtok", xtok)):
                for t in range(1, 4, 2):
                    take(name, t, dst[:, t, :], wide)
            for w in range(2):
                emptied(dve, UNIT["rows"] + w)
            softmax(0)
            for t in range(4):
                heads(t, 0, 1)
                if t:
                    finish(t - 1)
                heads(t, 1, PEER_H - (t == 3))
            dots(3, 4 * PEER_H - 1)
            weights(4 * PEER_H - 1)
            finish(3)

        @block.gpsimd
        def _(pool):
            pool.sem_inc(dots_done, RING)
            pool.sem_inc(up_used, PEER_K)
            with pool.Fori(0, 2 * PEER_H) as pair:
                for p in range(2):
                    i = pair * 2 + p
                    pool.wait_ge(idx_ready, i + 1)
                    pool.sem_inc(pool_go, 1)
                    nc.gpsimd.tensor_copy(stage[p], idx_all[:, ds(i * PEER_K, PEER_K)]).then_inc(stage_ready, 1)
                    pool.wait_ge(stage_ready, i + 1)
                    pool.sem_inc(pool_go, 1)
                    for s in range(PEER_K):
                        pool.wait_ge(dots_done, i * PEER_K + (s + 1))
                        pool.sem_inc(pool_go, 1)
                        nc.gpsimd.indirect_dma_start(down[:, s % RING, :], None, a["peer_down_2"][0],
                                                     bass.IndirectOffsetOnAxis(ap=stage[p][:, s:s + 1], axis=0)
                                                     ).then_inc(down_loaded[s % RING], 16)
                    for s in range(PEER_K):
                        pool.wait_ge(up_used, i * PEER_K + (s + RING + 1))
                        pool.sem_inc(pool_go, 1)
                        nc.gpsimd.indirect_dma_start(up[:, s % RING, :], None, a["peer_up_2"][0],
                                                     bass.IndirectOffsetOnAxis(ap=stage[p][:, s:s + 1], axis=0)
                                                     ).then_inc(up_loaded[s % RING], 16)

        @block.sync
        def _(sp):
            sp.sem_inc(tile_read, CREDIT)

            def features(w):
                return w.rearrange("(k p) n -> p k n", p=P)

            def load(dst, src, slot):
                sp.dma_start(dst, src).then_inc(w_loaded[slot], 16)

            def slot_free(s):
                if s >= 2:
                    sp.wait_ge(acc_ready, SLOT_END[s - 2])

            def mod_load(p, m, w, col):
                if not isinstance(m, int) or m >= 2:
                    sp.wait_ge(partial_ready, m - 1)
                sp.dma_start(Mw[:, p, :, :], features(w)[:, :, ds(col, P)]).then_inc(mod_loaded[p], 16)

            def columns(s, w, col, cols=COLS):
                slot_free(s)
                for hf in range(2):
                    k = slice(4 * hf, 4 * hf + 4)
                    dst = Wk[:, s % 2, k, 0:cols] if cols > 32 else Wlr[:, s % 2, k, :]
                    load(dst, features(w)[:, k, col:col + cols], s % 2)

            def ffn_in(name, w, units, w_mod, col0, first, per, count):
                s0 = SLOT_OF[name]

                def step(i, p):
                    it, slot = i * 2 + p, (s0 + p) % 2
                    if isinstance(i, int):
                        slot_free(s0 + it)
                    else:
                        sp.wait_ge(acc_ready, it * units + (UNIT[name] - units))
                    for m in range(2):
                        load(Wk[:, slot, :, m * 256:(m + 1) * 256], features(w)[:, :, ds(it * 256 + m * FF, 256)], slot)
                    for q in range(per):
                        mod_load((p * per + first + q) % 2, it * per + (first + q), w_mod, it * (per * P) + (col0 + q * P))
                pairs(sp, 11, step, first=2)
                for q in range(11 * per, count):
                    mod_load((first + q) % 2, first + q, w_mod, col0 + q * P)

            def ffn_out(name, w, units):
                s0 = SLOT_OF[name]

                def step(i, p):
                    it, slot = i * 2 + p, (s0 + p) % 2
                    if isinstance(i, int):
                        slot_free(s0 + it)
                    else:
                        sp.wait_ge(acc_ready, it * units + (UNIT[name] - units))
                    for m in range(2):
                        f = slice(11 * m, 11 * m + 11)
                        load(Wf[:, slot, f, :], w.rearrange("(f p) n -> p f n", p=P)[:, f, ds(it * P, P)], slot)
                pairs(sp, 8, step, first=2)

            for r in range(4):
                sp.dma_start(tok[:, r, :], a["x"][0][r * P:(r + 1) * P, :]).then_inc(tok_loaded, 16)
            for r in range(2):
                sp.dma_start(tok[:, 4 + r, :], a["ctx"][0][r * P:(r + 1) * P, :]).then_inc(tok_loaded, 16)
            for name in ("c", "c_ctx", "norm_ffn1", "norm_mix", "attn_out_norm", "conv_out_norm", "norm_ffn2",
                         "final_norm", "c_2", "c_ctx_2", "norm1_w_2", "norm2_w_2", "norm_f_w_2",
                         "gla_gk_bias_f_2", "gla_gk_bias_b_2"):
                at, rows = ROWS[name]
                sp.dma_start(rows1[at:at + rows, :], flat(a[name]).rearrange("(r q) -> r q", q=P)).then_inc(vec_loaded, 16)
            for i in range(8):
                sp.dma_start(Mfirst[i], features(a["w_ada"][0])[:, :, i * 256:(i + 1) * 256]).then_inc(first_loaded[i], 16)

            ffn_in("ffn1_in", a["w_ffn1_in"][0], 4, a["w_ada"][0], FIRST_MODS * P, 0, MOD_PER_SLOT[0], ADA_LATER)
            ffn_out("ffn1_out", a["w_ffn1_out"][0], 2)
            for j in range(5):
                columns(SLOT_OF["mix_in"] + j, a["w_mix_in"][0], j * COLS, COLS if j < 4 else 256)
            sp.wait_ge(acc_ready, UNIT["rope_q"])
            sp.dma_start(hid[:, 0:2 * T], a["rope"][:, 0:2 * T]).then_inc(pairs_loaded, 16)
            for j in range(2):
                columns(SLOT_OF["mix_out"] + j, a["w_mix_out"][0], j * COLS)
            for r in range(2):
                sp.dma_start(tok2[:, r, :], a["ctx_2"][0][r * P:(r + 1) * P, :]).then_inc(tok2_loaded, 16)
            ffn_in("ffn2_in", a["w_ffn2_in"][0], 2, a["w_mod_2"][0], 0, ADA_LATER, MOD_PER_SLOT[1], MOD_TILES)
            ffn_out("ffn2_out", a["w_ffn2_out"][0], 1)

            sp.wait_ge(partial_ready, N_LATER)
            sp.dma_start(modw[:, 3072:3072 + 2 * T], a["rope"][:, 2 * T:4 * T]).then_inc(halves_loaded, 16)
            for j in range(8):
                columns(SLOT_OF["proj"] + j, a["w_in_2"][0], j * COLS, COLS if j < 7 else 32)
            sp.wait_ge(acc_ready, UNIT["rope_r"])
            sp.dma_start(dist, a["dist"]).then_inc(dist_loaded, 16)
            for j in range(2):
                columns(SLOT_OF["w_out"] + j, a["w_out_2"][0], j * COLS)
            sp.wait_ge(acc_ready, UNIT["w_out"] + 1)
            for m, name in enumerate(("peer_k1_2", "peer_k2_2")):
                sp.dma_start(knat.rearrange("p (h m) n -> p h m n", m=2)[:, :, m, :],
                             a[name][0].rearrange("h n d -> n h d")).then_inc(keys_loaded, 16)
            for j in range(4):
                columns(SLOT_OF["peer_q"] + j, a["peer_w_q_2"][0], j * COLS)

            for t in range(4):
                sp.wait_ge(fin_ready, t + 1)
                sp.dma_start(out[0][t * P:(t + 1) * P, :], fin).then_inc(out_stored, 16)
            sp.wait_ge(out_stored, 4 * 16)


def kernel(**inputs):
    import concourse.bacc as bacc
    from concourse.bass_utils import run_bass_kernel_spmd

    nc = bacc.Bacc("TRN2", target_bir_lowering=False, num_devices=1)
    arrays, aps = {}, {}
    for name, value in {**inputs, **constants()}.items():
        value = np.ascontiguousarray(value)
        arrays[f"in_{name}"] = value
        aps[name] = nc.dram_tensor(f"in_{name}", value.shape, mybir.dt.from_np(value.dtype), kind="ExternalInput").ap()
    out = nc.dram_tensor("out", (1, T, D), F32, kind="ExternalOutput").ap()
    build(nc, aps, out)
    result = run_bass_kernel_spmd(nc, [arrays], core_ids=[0])
    return result.results[0]["out"]
```

```python
from contextlib import ExitStack

import concourse.bass as bass
import numpy as np
from concourse import mybir

F32 = mybir.dt.float32
F32R = mybir.dt.float32r
U32 = mybir.dt.uint32
I32 = mybir.dt.int32
ALU = mybir.AluOpType
ACT = mybir.ActivationFunctionType
AX_X = mybir.AxisListType.X
ds = bass.ds

P = 128
D = 1024
KD = D // P
T = 512
C = 256
TC = T + C
HALF = TC // 2
FF = 2816
FT = FF // P
EPS = 1e-6
W_RING = 4
TILE = KD * P
SLOT = 4096
FIRST_MODS = 2 * KD
ADA_TILES = 9 * KD
MOD_TILES = 6 * KD
ADA_LATER, MOD_PER_SLOT = ADA_TILES - FIRST_MODS, (5, 4)
MOD_LOOPS = ((0, 2, 2), (2, 5, 1))
N_LATER = ADA_LATER + MOD_TILES
KV_HEADS, HD = 2, 64
RET_SCALE = 128 ** -0.5
GLA_SCALE = 64 ** -0.5
CHUNK = 64
NCH = T // CHUNK
GATE_NORM = 16.0
PEER_H, PEER_K, N_KEYS = 8, 16, 128
RING = 8
CREDIT = 2

UNIT = {}
_at = 0
for _name, _n in (("tokens", 6), ("ffn1_in", 44), ("ffn1_out", 16), ("q", 4), ("k", 1), ("v", 1), ("gb", 4), ("vT", 1),
                  ("gc", 4), ("u", 4), ("rope_q", 4), ("rope_k", 1), ("kdup", 2), ("scores", 32),
                  ("mix_out", 8), ("ffn2_in", 22), ("ffn2_out", 8), ("tokens2", 2), ("rq", 4), ("rk", 4),
                  ("rv", 8), ("rg", 4), ("gq", 2), ("gk", 2), ("gv", 8), ("gg", 4), ("lr", 1),
                  ("rope_r", 8), ("decay", 4), ("ret", 24), ("gla0", 9), ("gla1", 9), ("w_out", 8),
                  ("peer_q", 16), ("keys", 2), ("peer_s", 8), ("xb", 4), ("xtok", 4), ("rows", 2)):
    UNIT[_name] = _at
    _at += _n

BY_FEATURE, BY_TOKEN = (0, 1, 3, 5), (2, 4, 6, 7)

TILE_OF, TILE_END = {}, []
for _stage, _units in (("ffn1_in", [UNIT["ffn1_in"] + f // 2 * 2 + 1 for f in range(2 * FT)]),
                       ("mix_in", [UNIT[n] + t for n, m in (("q", 4), ("k", 1), ("v", 1), ("gb", 4), ("gc", 4), ("u", 4)) for t in range(m)]),
                       ("mix_out", [UNIT["mix_out"] + t for t in range(KD)]),
                       ("ffn2_in", [UNIT["ffn2_in"] + f // 2 for f in range(2 * FT)]),
                       ("proj", [UNIT[n] + t for n, m in (("rq", range(4)), ("rk", range(4)), ("rv", BY_FEATURE), ("rg", range(4)), ("gq", range(2)),
                                                          ("gk", range(2)), ("gv", BY_FEATURE), ("gg", range(4)), ("lr", range(1))) for t in m]),
                       ("w_out", [UNIT["w_out"] + t for t in range(KD)]),
                       ("peer_q", [UNIT["peer_q"] + t for t in range(2 * PEER_H)])):
    TILE_OF[_stage] = len(TILE_END)
    TILE_END += [u + 1 for u in _units]
N_TILES = len(TILE_END)
TILE_FREE = [0] * W_RING + TILE_END[:-W_RING]
for _stage, _behind in (("mix_in", "q"), ("proj", "tokens2")):
    for _s in range(W_RING):
        TILE_FREE[TILE_OF[_stage] + _s] = UNIT[_behind]

ROWS = {}
_at = 0
for _name, _n in (("c", 8), ("c_ctx", 8), ("norm_ffn1", 8), ("norm_mix", 8), ("attn_out_norm", 4),
                  ("conv_out_norm", 4), ("norm_ffn2", 8), ("final_norm", 8), ("c_2", 8), ("c_ctx_2", 8),
                  ("norm1_w_2", 8), ("norm2_w_2", 8), ("norm_f_w_2", 8), ("conv_w", 12),
                  ("q_norm", 1), ("k_norm", 1), ("gla_gk_bias_f_2", 2), ("gla_gk_bias_b_2", 2)):
    ROWS[_name] = (_at, _n)
    _at += _n
N_ROWS = _at
N_BIAS = ADA_TILES + MOD_TILES

CONST = {}
_at = 0
for _name, _n in (("ident", P), ("ones", P), ("blk64", P), ("swap_pairs", P), ("swap_halves", P),
                  ("dup0", P), ("dup1", P), ("causal_f", P), ("causal_b", P), ("chunk_reset", TC),
                  ("head_rows", 2), ("iota16", 16), ("eps", 1), ("zero", P), ("mean1024", P), ("mean512", P), ("mean128", P)):
    CONST[_name] = (_at, _n)
    _at += _n
N_CONST = _at
N_DX, N_DC = 896, 640
N_DIST = T + N_DC
N_VEC_DMAS = 26


def flat(ap):
    if len(ap.shape) == 1:
        return ap
    return ap.rearrange("a b -> (a b)")


def constants():
    t = np.zeros((P, N_CONST), np.float32)

    def put(name, value):
        at, n = CONST[name]
        t[:, at:at + n] = value

    p = np.arange(P)
    put("ident", np.eye(P))
    put("ones", 1.0)
    put("blk64", (p[:, None] // 64 == p[None, :] // 64) / 64)
    pairs, halves = np.zeros((P, P)), np.zeros((P, P))
    pairs[p[0::2] + 1, p[0::2]], pairs[p[0::2], p[0::2] + 1] = -1.0, 1.0
    halves[p[:64] + 64, p[:64]], halves[p[:64], p[:64] + 64] = -1.0, 1.0
    put("swap_pairs", pairs)
    put("swap_halves", halves)
    for kv in range(KV_HEADS):
        put(f"dup{kv}", p[:, None] == kv * 64 + p[None, :] % 64)
    same = p[:, None] // CHUNK == p[None, :] // CHUNK
    put("causal_f", same & (p[:, None] <= p[None, :]))
    put("causal_b", same & (p[:, None] >= p[None, :]))
    reset = np.ones(TC)
    reset[0:T:CHUNK], reset[T] = 0.0, 0.0
    put("chunk_reset", reset[None, :])
    put("head_rows", np.stack([p < 64, p >= 64], 1) * GLA_SCALE)
    put("iota16", np.arange(16)[None, :])
    put("eps", EPS)
    for n in (1024, 512, 128):
        put(f"mean{n}", 1.0 / n)
    tok, rope = np.arange(T), []
    for name, dim, place in (("pairs", HD, (p % 64) // 2), ("halves", 128, p % 64)):
        n = dim // 4
        inv = (np.float32(10000.0) ** (-np.arange(n, dtype=np.float32) / n)).astype(np.float32)
        ang = np.concatenate([(tok // 64).astype(np.float32)[:, None] * inv,
                              (tok % 64).astype(np.float32)[:, None] * inv], 1).T
        rope += [np.cos(ang)[place], np.sin(ang)[place]]
    dist = np.arange(N_DIST)[None, :] - 384 - p[:, None]
    return {"const": t, "dist": dist.astype(np.float32), "rope": np.concatenate(rope, 1).astype(np.float32)}


def build(nc, a, out):
    with ExitStack() as ctx:
        def sb(name, cols, dt=F32, parts=P):
            return ctx.enter_context(nc.sbuf_tensor(name, [parts, cols], dt))

        def sb_split(name, cols):
            at = -(-nc.sbuf_base // 32) * 32
            return sb(name, cols), nc.alloc_sbuf_tensor_at(name + "_parts", [P, cols], F32R, offset=at)

        def pb(name, shape):
            return ctx.enter_context(nc.psum_tensor(name, shape, F32))

        def sem(name):
            return ctx.enter_context(nc.semaphore(name))

        acc = pb("acc", [P, 4, 512])
        mod_ps = pb("mod_ps", [P, 512])
        sums = pb("sums", [P, 2, 512])
        misc = pb("misc", [P, 512])

        cst = sb("cst", N_CONST)
        resid = sb("resid", KD * TC)
        hid, hid_parts = sb_split("hid", 2 * KD * TC)
        wring, wring_parts = sb_split("wring", 2 * SLOT)
        modw = sb("modw", 2 * TILE)
        arena, arena_parts = sb_split("arena", 17148)
        vec = sb("vec", 256)
        cond = sb("cond", 32)
        mods = sb("mods", 2 * N_BIAS)
        gains = sb("gains", 5 * 16)
        halfg = sb("halfg", 2 * 16)
        squares = sb("squares", 2 * TC)
        rstd = sb("rstd", TC)
        tmp = sb("tmp", TC)
        rows1, rows2 = tmp[:, 0:P], tmp[:, P:2 * P]
        logs = tmp
        dec = sb("dec", 80)
        gkup = sb("gkup", 2 * 256, parts=32)
        small = sb("small", 24)
        partials = sb("partials", 2 * 2 * P)

        def c_(name, parts=P):
            at, n = CONST[name]
            return cst[0:parts, at:at + n]

        def v_(name, j=0, n=1):
            at = ROWS[name][0] + j
            return vec[:, at:at + n]

        ident, ones = c_("ident"), c_("ones")
        x_ = resid[:, :].rearrange("p (j t) -> p j t", j=KD)
        lo768 = hid[:, KD * TC:].rearrange("p (j t) -> p j t", j=KD)
        lo512 = hid[:, KD * TC:KD * TC + KD * T].rearrange("p (j t) -> p j t", j=KD)
        Wlo = wring[:, 0:SLOT].rearrange("p (s k n) -> p s k n", s=W_RING, k=KD)
        hi768r, lo768r = (hid_parts[:, KD * TC * i:KD * TC * (i + 1)].rearrange("p (j t) -> p j t", j=KD) for i in range(2))
        hi512r, lo512r = (hid_parts[:, KD * TC * i:KD * TC * i + KD * T].rearrange("p (j t) -> p j t", j=KD) for i in range(2))
        Wlor, Whir = (wring_parts[:, SLOT * i:SLOT * (i + 1)].rearrange("p (s k n) -> p s k n", s=W_RING, k=KD) for i in range(2))
        mix_hir, mixTr, y_hir, yTr = (arena_parts[:, at:at + KD * T].rearrange("p (j t) -> p j t", j=KD) for at in (0, 11272, 4096, 0))
        Wf = wring[:, :].rearrange("p (s n) -> p s n", s=2)[:, :, 0:FT * P].rearrange("p s (f n) -> p s f n", f=FT)
        Mw = modw[:, 0:2048].rearrange("p (s k n) -> p s k n", s=2, k=KD)
        cnd = cond[:, :].rearrange("p (b k c) -> p b k c", b=2, k=KD)
        mod = mods[:, :].rearrange("p (t c) -> p t c", c=2)
        gain = gains[:, :].rearrange("p (n k c) -> p n k c", n=5, k=KD)
        hgate = halfg[:, :].rearrange("p (n k c) -> p n k c", n=2, k=KD)
        sq = squares[:, :].rearrange("p (s t) -> p s t", s=2)

        def ar(at, *shape):
            n = int(np.prod(shape))
            v = arena[:, at:at + n]
            if len(shape) == 2:
                return v.rearrange("p (a b) -> p a b", a=shape[0])
            if len(shape) == 3:
                return v.rearrange("p (a b c) -> p a b c", a=shape[0], b=shape[1])
            return v

        def hi(at, *shape):
            n = int(np.prod(shape))
            v = hid[:, at:at + n]
            if len(shape) == 2:
                return v.rearrange("p (a b) -> p a b", a=shape[0])
            if len(shape) == 3:
                return v.rearrange("p (a b c) -> p a b c", a=shape[0], b=shape[1])
            return v

        Mfirst = [hi(2048 * i, KD, 256) for i in range(6)] + [ar(6144 + 2048 * i, KD, 256) for i in range(2)]
        partial = partials[:, :].rearrange("p (s c n) -> p s c n", s=2, c=2)
        tok = ar(0, 6, D)
        tok2 = ar(11264, 2, D)
        ff768, ff512 = ar(0, FT, TC), ar(0, FT, T)
        sg = squares[:, 0:1024].rearrange("p (s t) -> p s t", s=2)
        qT, kT = ar(0, 4, T), ar(2048, TC)
        kdup, vtok = ar(2816, 2, TC), ar(4352, 6, P)
        gb, cu, gc = ar(5120, 4, T), ar(7168, 4, T + 2), ar(9224, 4, T)
        mixT = ar(11272, KD, T)
        probT = hid[:, 0:KD * TC].rearrange("p (h r t) -> p h r t", h=2, r=6)
        prob = hi(KD * TC, 3, TC)
        cos_pairs, sin_pairs = hi(0, T), hi(T, T)
        yT = ar(0, KD, T)
        rq, rk, rv = ar(4096, 4, T), ar(6144, 4, TC), ar(9216, 6, 512)
        gv, gk = ar(12288, 6, 512), ar(15360, 2, TC)
        gq = modw[:, 0:2 * T].rearrange("p (a t) -> p a t", a=2)
        lr = modw[0:32, 2 * T:2 * T + TC]
        dist, cos_halves, sin_halves = hi(0, N_DIST), hi(1152, T), hi(1664, T)
        DX, DC = hi(3072, 2, N_DX), hi(4864, 2, N_DC)
        la = hi(6144, 2 * 2, TC).rearrange("p (d a) t -> p d a t", d=2)
        retP = hi(9216, 2, T)
        gG, gE, gkt, gS = ar(6144, 2, TC), ar(7680, 2, TC), ar(9216, 2, T), ar(10240, 2, NCH, P)
        gla_decay = dec[:, 48:64].rearrange("p (a c) -> p a c", a=2)
        gkd, gkd_tok, gqz, gP = hi(0, 2, TC), hi(1536, 6, 256), hi(3072, 4, T), hi(5120, 2, T)
        og = hi(10240, 4, T)
        pq, s_all, xb = ar(0, 16, T), ar(8192, 4, 2048), ar(0, 4, D)
        down = wring[:, :].rearrange("p (s n) -> p s n", s=RING)
        up = [arena[:, 4096 + D * i:4096 + D * (i + 1)] for i in range(4)] + [hid[:, 6144 + D * i:6144 + D * (i + 1)] for i in range(4)]
        knat, kTr = hi(4096, 16, P), modw[:, 0:2048].rearrange("p (a n) -> p a n", a=16)
        xtok = hi(0, 4, D)
        diag, rowsrc = hi(4096, 16, P), hi(4096, 16, P)
        g2row, nfrow = resid[:, 0:D], resid[:, D:2 * D]
        junk, fin = resid[:, 2 * D:3 * D], resid[:, 3 * D:4 * D]
        idx_all = squares[:, 0:512].bitcast(U32)
        g_all = squares[:, 512:1024]

        def pm(at, n):
            return hid[:, 10240 + at:10240 + at + n]

        s_cur, s_less = pm(0, 256), pm(256, 256)
        onehot = pm(512, 512)
        key_top, key_at = pm(1024, 32), pm(1056, 32).bitcast(U32)
        key_no, chosen = pm(1088, 32), pm(1120, 32)
        cand_at, cand_half = pm(1152, 16).bitcast(U32), pm(1168, 32).bitcast(U32)
        cand_no = pm(1200, 32)
        stage = [pm(1232 + 16 * i, 16).bitcast(U32) for i in range(2)]
        p_top, p_exp, p_dot, p_act, p_w = (pm(1264 + 16 * i, 16) for i in range(5))
        p_neg, p_sum, p_inv, p_ssq, p_std, p_rstd = (pm(1344 + i, 1) for i in range(6))
        cand, cand_less = pm(1360, 256), pm(1616, 256)

        tok_loaded, tok2_loaded = sem("tok_loaded"), sem("tok2_loaded")
        const_loaded, vec_loaded = sem("const_loaded"), sem("vec_loaded")
        dist_loaded, keys_loaded = sem("dist_loaded"), sem("keys_loaded")
        w_loaded = [sem(f"w_loaded{i}") for i in range(W_RING)]
        w_high, w_ready = sem("w_high"), sem("w_ready")
        f_loaded = [sem(f"f_loaded{i}") for i in range(2)]
        h_high, y_high, y_ready = sem("h_high"), sem("y_high"), sem("y_ready")
        mod_loaded = [sem(f"mod_loaded{i}") for i in range(2)]
        first_loaded = [sem(f"first_loaded{i}") for i in range(8)]
        first_used, mod_step, pool_go = sem("first_used"), sem("mod_step"), sem("pool_go")
        partial_ready, partial_used = sem("partial_ready"), sem("partial_used")
        acc_ready = sem("acc_ready")
        acc_free = [sem(f"acc_free{i}") for i in range(2)]
        rows_zeroed, vec_turned, vec_ready, cond_ready = sem("rows_zeroed"), sem("vec_turned"), sem("vec_ready"), sem("cond_ready")
        sq_ready, sq_used, rstd_ready = sem("sq_ready"), sem("sq_used"), sem("rstd_ready")
        h_scaled, h_ready, x1_ready = sem("h_scaled"), sem("h_ready"), sem("x1_ready")
        silu_ready = sem("silu_ready")
        dve_step, act_step = sem("dve_step"), sem("act_step")
        normed = sem("normed")
        copied = sem("copied")
        negmax_ready, exp_ready, prob_ready = sem("negmax_ready"), sem("exp_ready"), sem("prob_ready")
        probT_ready, probT_act, probT_dve = sem("probT_ready"), sem("probT_act"), sem("probT_dve")
        o_ready, o_copied = sem("o_ready"), sem("o_copied")

        mods_ready, conv_ready = sem("mods_ready"), sem("conv_ready")
        pairs_loaded, halves_loaded = sem("pairs_loaded"), sem("halves_loaded")
        decay_abs, decay_exp, la_ready, ln_ready = sem("decay_abs"), sem("decay_exp"), sem("la_ready"), sem("ln_ready")
        dist_arg, dist_exp, dist_done = sem("dist_arg"), sem("dist_exp"), sem("dist_done")
        gla_arg, gla_exp, gla_kd, gla_qk = sem("gla_arg"), sem("gla_exp"), sem("gla_kd"), sem("gla_qk")
        gla_states, gla_o = sem("gla_states"), sem("gla_o")
        rowsrc_ready, tile_read, tile_done = sem("rowsrc_ready"), sem("tile_read"), sem("tile_done")
        down_loaded = [sem(f"down_loaded{i}") for i in range(RING)]
        up_loaded = [sem(f"up_loaded{i}") for i in range(RING)]
        idx_ready, stage_ready = sem("idx_ready"), sem("stage_ready")
        top_ready, p_exp_ready, topk_step, dve_go = sem("top_ready"), sem("p_exp_ready"), sem("topk_step"), sem("dve_go")
        dots_done, gelu_ready, weights_ready = sem("dots_done"), sem("gelu_ready"), sem("weights_ready")
        diag_ready, up_used = sem("diag_ready"), sem("up_used")
        ssq_ready, fstd_ready, fin_ready = sem("ssq_ready"), sem("fstd_ready"), sem("fin_ready")
        out_stored, inv_ready = sem("out_stored"), sem("inv_ready")

        block = ctx.enter_context(nc.Block())

        class Tally:
            def __init__(self):
                self.sq = self.job = self.step = 0

        def pairs(eng, steps, body, first=0):
            for s in range(first):
                body(s // 2, s % 2)
            if steps // 2 > first // 2:
                with eng.Fori(first // 2, steps // 2) as i:
                    for p in range(2):
                        body(i, p)
            if steps % 2:
                body(steps // 2, 0)

        def emptied(eng, u):
            eng.wait_ge(acc_free[u % 2], u // 2 + CREDIT)

        @block.tensor
        def _(pe):
            n = Tally()
            for p in range(2):
                pe.sem_inc(acc_free[p], 1)

            def begin(u):
                pe.wait_ge(acc_free[u % 2], u // 2 + 1)
                return 2 * (u % 2)

            def product(o, w, x, k, last):
                return nc.tensor.matmul(o, w, x, start=(k == 0), stop=(k == last))

            def stat(tiles, t, weights):
                for j in range(tiles):
                    pe.wait_ge(sq_ready, n.sq + 1)
                    if j == 0 and n.job:
                        pe.wait_ge(rstd_ready, n.job)
                    s = n.sq % 2
                    if t == T:
                        mm = product(sums[:, 0, :], weights, sq[:, s, 0:T], j, tiles - 1)
                    else:
                        for hf in range(2):
                            mm = product(sums[:, hf, 0:HALF], weights, sq[:, s, hf * HALF:(hf + 1) * HALF], j, tiles - 1)
                    mm.then_inc(sq_used, 1)
                    n.sq += 1
                n.job += 1

            def mod_sum(p, m, column, conds=2):
                pe.wait_ge(partial_ready, m + 1)
                n_cols = 2 // conds
                for c in range(conds):
                    mm = nc.tensor.matmul(mod_ps[:, ds(column + c, n_cols)], partial[:, p, c, :], ones[:, 0:n_cols], start=True, stop=True)
                mm.then_inc(partial_used, 1)

            def split_product(o, s, k, cols, high, low, first, last):
                wh, wl = Whir[:, s, k, 0:cols], Wlor[:, s, k, 0:cols]
                nc.tensor.matmul(o, wh, high, start=first, stop=False)
                nc.tensor.matmul(o, wh, low, start=False, stop=False)
                return nc.tensor.matmul(o, wl, high, start=False, stop=last)

            def to_features(u, src):
                b = begin(u)
                for j in range(KD):
                    mm = nc.tensor.transpose(acc[:, b + j // 4, (j % 4) * P:(j % 4 + 1) * P],
                                             src[:, j * P:(j + 1) * P], ident)
                mm.then_inc(acc_ready, 1)

            pe.wait_ge(const_loaded, 16)
            pe.wait_ge(tok_loaded, 16 * 6)
            for r in range(6):
                to_features(UNIT["tokens"] + r, tok[:, r, :])
            pe.wait_ge(vec_loaded, 16 * N_VEC_DMAS)
            nc.tensor.transpose(misc[:, 0:N_ROWS], rows1[0:N_ROWS, :], ident[0:N_ROWS, 0:N_ROWS])
            nc.tensor.transpose(misc[:, 128:128 + N_BIAS], rows2[0:N_BIAS, :],
                                ident[0:N_BIAS, 0:N_BIAS]).then_inc(vec_turned, 1)

            stat(KD, TC, c_("mean1024"))
            pe.wait_ge(cond_ready, 4)
            for i in range(8):
                pe.wait_ge(first_loaded[i], 16)
                for t in range(2):
                    for k in range(KD):
                        mm = product(mod_ps[:, 4 * i + 2 * t:4 * i + 2 * t + 2], Mfirst[i][:, k, t * P:(t + 1) * P], cnd[:, 0, k, :], k, KD - 1)
                mm.then_inc(first_used, 1)

            def ffn_in(name, width, halves, first, per, count, h_before):
                units = 2 * halves
                high, low = (hi768r, lo768r) if halves == 2 else (hi512r, lo512r)
                base, s0 = UNIT[name], TILE_OF[name]

                def step(i, odd, conds):
                    for q in range(units):
                        sub, hf = q // halves, q % halves
                        u0 = base + q
                        b = 2 * (u0 % 2)
                        pe.wait_ge(acc_free[u0 % 2], i * halves + (u0 // 2 + 1))
                        for m in range(2):
                            s = s0 + 2 * sub + m
                            if hf == 0:
                                pe.wait_ge(w_ready, i * 4 + (s + 1))
                            for k in range(KD):
                                if isinstance(i, int) and q == 0 and m == 0:
                                    pe.wait_ge(h_ready, h_before + k + 1)
                                at = slice(hf * width, (hf + 1) * width)
                                mm = split_product(acc[:, b + m, 0:width], s % W_RING, k, P, high[:, k, at], low[:, k, at], k == 0, k == KD - 1)
                        mm.then_inc(acc_ready, 1)
                        for tile in range(q * per // units, (q + 1) * per // units):
                            m = i * per + (first + tile)
                            mod_sum((first + tile + odd * per) % 2, m, m * 2 + 2 * FIRST_MODS, conds)
                step(0, 0, 2)
                for start, stop, conds in MOD_LOOPS:
                    with pe.Fori(start, stop) as j:
                        for odd in (1, 2):
                            step(j * 2 + odd, odd, conds)
                for m in range(first + 11 * per, first + count):
                    mod_sum(m % 2, m, m * 2 + 2 * FIRST_MODS, 1)

            def ffn_out(name, width, halves, ff, uses):
                base = UNIT[name]

                def step(i, p):
                    pe.wait_ge(f_loaded[p], i * 32 + (uses * 128 + 32))
                    for hf in range(halves):
                        u0 = base + p * halves + hf
                        b = 2 * (u0 % 2)
                        pe.wait_ge(acc_free[u0 % 2], i * halves + (u0 // 2 + 1))
                        for f in range(FT):
                            mm = product(acc[:, b, 0:width], Wf[:, p, f, :],
                                         ff[:, f, hf * width:(hf + 1) * width], f, FT - 1)
                        mm.then_inc(acc_ready, 1)
                emptied(pe, base - 1)
                emptied(pe, base - 2)
                pairs(pe, 8, step)

            ffn_in("ffn1_in", HALF, 2, 0, MOD_PER_SLOT[0], ADA_LATER, 0)
            ffn_out("ffn1_out", HALF, 2, ff768, 0)
            stat(KD, TC, c_("mean1024"))

            def feature_tile(u, s, high, low, width=T, halves=1, cols=P, arriving=None, order=range(KD)):
                b = begin(u)
                pe.wait_ge(w_ready, s + 1)
                for hf in range(halves):
                    for i, k in enumerate(order):
                        if arriving and hf == 0:
                            pe.wait_ge(arriving[0], arriving[1] + i + 1)
                        at = slice(hf * width, (hf + 1) * width)
                        mm = split_product(acc[0:cols, b + hf, 0:width], s % W_RING, k, cols, high[:, k, at], low[:, k, at], i == 0, i == KD - 1)
                mm.then_inc(acc_ready, 1)

            def to_tokens(u, features):
                b = begin(u)
                for r in range(6):
                    mm = nc.tensor.transpose(acc[:, b + r // 4, (r % 4) * P:(r % 4 + 1) * P], features[:, r * P:(r + 1) * P], ident)
                mm.then_inc(acc_ready, 1)

            s = TILE_OF["mix_in"]
            for t in range(4):
                feature_tile(UNIT["q"] + t, s + t, hi768r, lo768r, arriving=(h_ready, 8) if t == 0 else None)
            for t, name in ((4, "k"), (5, "v")):
                feature_tile(UNIT[name], s + t, hi768r, lo768r, HALF, 2)
            for t in range(4):
                feature_tile(UNIT["gb"] + t, s + 6 + t, hi768r, lo768r)
            emptied(pe, UNIT["v"])
            to_tokens(UNIT["vT"], sq[:, 0, :])
            for t in range(4):
                feature_tile(UNIT["gc"] + t, s + 10 + t, hi768r, lo768r)
            for t in range(4):
                feature_tile(UNIT["u"] + t, s + 14 + t, hi768r, lo768r)

            for t in range(4):
                stat(1, T, c_("blk64"))
            stat(1, TC, c_("blk64"))
            for t in range(5):
                u = UNIT["rope_q"] + t
                b = begin(u)
                pe.wait_ge(normed, t + 1)
                nc.tensor.matmul(acc[:, b, :], c_("swap_pairs"), qT[:, t, :] if t < 4 else kT[:, 0:T],
                                 start=True, stop=True).then_inc(acc_ready, 1)
            pe.wait_ge(copied, 5)
            for kv in range(KV_HEADS):
                b = begin(UNIT["kdup"] + kv)
                for hf in range(2):
                    mm = nc.tensor.matmul(acc[:, b + hf, 0:HALF], c_(f"dup{kv}"), kT[:, hf * HALF:(hf + 1) * HALF],
                                          start=True, stop=True)
                mm.then_inc(acc_ready, 1)
            stat(4, T, c_("mean512"))

            pe.wait_ge(rstd_ready, n.job)
            emptied(pe, UNIT["kdup"])
            emptied(pe, UNIT["kdup"] + 1)

            def scores(u):
                h, t = u // 4, u % 4
                b = begin(UNIT["scores"] + u) if u < 2 else 2 * (u % 2)
                if u >= 2:
                    pe.wait_ge(exp_ready, u - 1)
                rows = slice(64 * (h % 2), 64 * (h % 2) + 64)
                for hf in range(2):
                    mm = nc.tensor.matmul(acc[:, b + hf, 0:HALF], qT[rows, h // 2, t * P:(t + 1) * P],
                                          kdup[rows, h // 4, hf * HALF:(hf + 1) * HALF], start=True, stop=True)
                mm.then_inc(acc_ready, 1)

            def turn(u):
                pe.wait_ge(prob_ready, u + 1)
                if u:
                    pe.wait_ge(probT_act, u)
                    pe.wait_ge(probT_dve, u)
                for r in range(6):
                    mm = nc.tensor.transpose(sums[:, r // 3, (r % 3) * P:(r % 3 + 1) * P],
                                             prob[:, u % 3, r * P:(r + 1) * P], ident)
                mm.then_inc(probT_ready, 1)

            def outputs(h):
                pe.wait_ge(probT_act, 4 * (h + 1))
                pe.wait_ge(probT_dve, 4 * (h + 1))
                if h:
                    pe.wait_ge(o_copied, h)
                at, kv = 64 * (h % 2), h // 4
                for r in range(6):
                    mm = product(misc[at:at + 64, :], vtok[:, r, kv * HD:(kv + 1) * HD], probT[:, h % 2, r, :], r, 5)
                mm.then_inc(o_ready, 1)

            scores(0)
            for step in range(32 + 3):
                if step + 1 < 32:
                    scores(step + 1)
                if 2 <= step < 34:
                    turn(step - 2)
                if step >= 6 and (step - 6) % 4 == 0:
                    outputs((step - 6) // 4)
            stat(4, T, c_("mean512"))

            for t in range(KD):
                feature_tile(UNIT["mix_out"] + t, TILE_OF["mix_out"] + t, mix_hir, mixTr,
                             arriving=(y_ready, 0) if t == 0 else None, order=(4, 5, 6, 7, 0, 1, 2, 3))
            stat(KD, T, c_("mean1024"))

            ffn_in("ffn2_in", T, 1, ADA_LATER, MOD_PER_SLOT[1], MOD_TILES, 16)
            ffn_out("ffn2_out", T, 1, ff512, 1)
            pe.wait_ge(tok2_loaded, 32)
            for r in range(2):
                to_features(UNIT["tokens2"] + r, tok2[:, r, :])
            stat(KD, T, c_("mean1024"))
            stat(KD, TC, c_("mean1024"))

            s = TILE_OF["proj"]

            def both(name, s):
                for c in range(4 + 1):
                    if c < 4:
                        feature_tile(UNIT[name] + BY_FEATURE[c], s + c, hi768r, lo768r, HALF, 2)
                    if c >= 1:
                        emptied(pe, UNIT[name] + BY_FEATURE[c - 1])
                        to_tokens(UNIT[name] + BY_TOKEN[c - 1], sq[:, (c - 1) % 2, :])

            for t in range(4):
                feature_tile(UNIT["rq"] + t, s + t, hi768r, lo768r, arriving=(h_ready, 24) if t == 0 else None)
            for t in range(4):
                feature_tile(UNIT["rk"] + t, s + 4 + t, hi768r, lo768r, HALF, 2)
            both("rv", s + 8)
            for t in range(4):
                feature_tile(UNIT["rg"] + t, s + 12 + t, hi768r, lo768r)
            for t in range(2):
                feature_tile(UNIT["gq"] + t, s + 16 + t, hi768r, lo768r)
            for t in range(2):
                feature_tile(UNIT["gk"] + t, s + 18 + t, hi768r, lo768r, HALF, 2)
            both("gv", s + 20)
            for t in range(4):
                feature_tile(UNIT["gg"] + t, s + 24 + t, hi768r, lo768r)
            feature_tile(UNIT["lr"], s + 28, hi768r, lo768r, HALF, 2, 32)

            for t in range(8):
                src = rq[:, t, :] if t < 4 else rk[:, t - 4, 0:T]
                emptied(pe, UNIT["rq"] + t)
                b = begin(UNIT["rope_r"] + t)
                nc.tensor.matmul(acc[:, b, :], c_("swap_halves"), src, start=True, stop=True).then_inc(acc_ready, 1)
            emptied(pe, UNIT["lr"])
            for u in range(4):
                b = begin(UNIT["decay"] + u)
                at = (u // 2) * 256 + (u % 2) * P
                for hf in range(2):
                    mm = nc.tensor.matmul(acc[:, b + hf, 0:HALF], gkup[:, at:at + P], lr[:, hf * HALF:(hf + 1) * HALF],
                                          start=True, stop=True)
                mm.then_inc(acc_ready, 1)
            pe.wait_ge(copied, 5 + 8)
            outs = [misc, mod_ps]

            def ret_scores(u):
                h, r = u // 6, u % 6
                b = begin(UNIT["ret"] + u)
                nc.tensor.matmul(acc[:, b, :], rk[:, h, r * P:(r + 1) * P], rq[:, h, :],
                                 start=True, stop=True).then_inc(acc_ready, 1)

            def ret_outputs(u):
                h, r = u // 6, u % 6
                emptied(pe, UNIT["ret"] + u)
                if r == 0 and h >= 2:
                    pe.wait_ge(o_copied, 8 + h - 1)
                mm = product(outs[h % 2][:, :], rv[:, r, h * P:(h + 1) * P], retP[:, u % 2, :], r, 5)
                mm.then_inc(o_ready, 1)

            for u in range(25):
                if u < 24:
                    ret_scores(u)
                if u >= 1:
                    ret_outputs(u - 1)
            for h in range(4):
                stat(1, T, c_("mean128"))

            banks = [mod_ps[:, :], misc[:, :], sums[:, 0, :], sums[:, 1, :]]
            pe.wait_ge(rstd_ready, n.job)
            pe.wait_ge(o_copied, 12)
            for d in range(2):
                base = UNIT[f"gla{d}"]
                for pr in range(2):
                    pe.wait_ge(gla_kd, 2 * d + pr + 1)
                    b = begin(base + pr)
                    for r in range(6):
                        mm = nc.tensor.transpose(acc[:, b + r // 4, (r % 4) * P:(r % 4 + 1) * P],
                                                 gkd[:, pr, r * P:(r + 1) * P], ident)
                    mm.then_inc(acc_ready, 1)
                emptied(pe, base)
                emptied(pe, base + 1)
                b = begin(base + 2)
                for pr in range(2):
                    for hh in range(2):
                        h, at = 2 * pr + hh, pr * P + hh * 64
                        for r in range(2):
                            mm = product(acc[hh * 64:hh * 64 + 64, b, pr * P:(pr + 1) * P], gkd_tok[:, 4 + r, at:at + 64],
                                         gv[:, 4 + r, h * P:(h + 1) * P], r, 1)
                mm.then_inc(acc_ready, 1)
                for pr in range(2):
                    b = begin(base + 3 + pr)
                    for c in range(NCH):
                        rows = slice(64 * (c % 2), 64 * (c % 2) + 64)
                        for hh in range(2):
                            h, at = 2 * pr + hh, pr * P + hh * 64
                            mm = nc.tensor.matmul(acc[hh * 64:hh * 64 + 64, b + c % 2, (c // 2) * P:(c // 2 + 1) * P],
                                                  gkd_tok[rows, c // 2, at:at + 64], gv[rows, c // 2, h * P:(h + 1) * P],
                                                  start=True, stop=True)
                    mm.then_inc(acc_ready, 1)
                def gla_out(h):
                    emptied(pe, base + 5 + h)
                    for r in range(4):
                        nc.tensor.matmul(banks[h][:, r * P:(r + 1) * P], gv[:, r, h * P:(h + 1) * P],
                                         gP[:, h % 2, r * P:(r + 1) * P], start=(d == 0 and r == 0), stop=False,
                                         skip_group_check=True)
                    for c in range(NCH):
                        mm = nc.tensor.matmul(banks[h][:, c * 64:c * 64 + 64], gS[:, h // 2, c, :],
                                              gqz[:, h, c * 64:c * 64 + 64], start=False,
                                              stop=(d == 1 and c == NCH - 1), skip_group_check=True)
                    mm.then_inc(gla_o, 1)

                pe.wait_ge(gla_qk, 6 * (d + 1))
                for h in range(4):
                    b = begin(base + 5 + h)
                    for r in range(4):
                        mm = nc.tensor.matmul(acc[:, b, r * P:(r + 1) * P], gkt[:, h // 2, r * P:(r + 1) * P],
                                              gqz[:, h, r * P:(r + 1) * P], start=True, stop=True)
                    mm.then_inc(acc_ready, 1)
                    if h == 0:
                        pe.wait_ge(gla_states, 12 * (d + 1))
                        emptied(pe, base + 3)
                        emptied(pe, base + 4)
                    else:
                        gla_out(h - 1)
                gla_out(3)
            pe.wait_ge(o_copied, 16)
            for h in range(4):
                stat(1, T, c_("mean128"))

            for t in range(KD):
                feature_tile(UNIT["w_out"] + t, TILE_OF["w_out"] + t, y_hir, yTr, arriving=(y_ready, 8) if t == 0 else None)
            stat(KD, T, c_("mean1024"))
            for t in range(2 * PEER_H):
                feature_tile(UNIT["peer_q"] + t, TILE_OF["peer_q"] + t, hi512r, lo512r, arriving=(h_ready, 32) if t == 0 else None)
            pe.wait_ge(keys_loaded, 32)
            for g in range(2):
                b = begin(UNIT["keys"] + g)
                for j in range(8):
                    mm = nc.tensor.transpose(acc[:, b + j // 4, (j % 4) * P:(j % 4 + 1) * P], knat[:, 8 * g + j, :], ident)
                mm.then_inc(acc_ready, 1)
            emptied(pe, UNIT["keys"])
            emptied(pe, UNIT["keys"] + 1)
            for u in range(8):
                b = begin(UNIT["peer_s"] + u)
                for j in range(8):
                    a8 = 8 * (u % 2) + j
                    mm = nc.tensor.matmul(acc[:, b + j // 4, (j % 4) * P:(j % 4 + 1) * P],
                                          pq[:, a8, (u // 2) * P:(u // 2 + 1) * P], kTr[:, a8, :], start=True, stop=True)
                mm.then_inc(acc_ready, 1)
            for t in range(4):
                b = begin(UNIT["xb"] + t)
                for j in range(KD):
                    for part in (hi512r, lo512r):
                        mm = nc.tensor.matmul(acc[:, b + j // 4, (j % 4) * P:(j % 4 + 1) * P], part[:, j, t * P:(t + 1) * P].bitcast(F32), ident,
                                              start=part is hi512r, stop=part is lo512r)
                mm.then_inc(acc_ready, 1)
            for t in range(4):
                b = begin(UNIT["xtok"] + t)
                for j in range(KD):
                    mm = nc.tensor.transpose(acc[:, b + j // 4, (j % 4) * P:(j % 4 + 1) * P], x_[:, j, t * P:(t + 1) * P], ident)
                mm.then_inc(acc_ready, 1)
            pe.wait_ge(rowsrc_ready, 16)
            for w in range(2):
                b = begin(UNIT["rows"] + w)
                for j in range(KD):
                    mm = nc.tensor.matmul(acc[:, b + j // 4, (j % 4) * P:(j % 4 + 1) * P], rowsrc[:, (w * KD + j), :],
                                          ident, start=True, stop=True)
                mm.then_inc(acc_ready, 1)
            emptied(pe, UNIT["rows"])
            emptied(pe, UNIT["rows"] + 1)

            for t in range(4):
                b = 2 * (t % 2)
                pe.wait_ge(tile_read, t + 1)
                for hf in range(2):
                    nc.tensor.matmul(acc[:, b + hf, :], c_("zero"), cst[:, 0:512], start=True, stop=False, skip_group_check=True)
                with pe.Fori(0, PEER_H) as h:
                    i = h + t * PEER_H
                    for k in range(PEER_K):
                        pe.wait_ge(diag_ready, i * PEER_K + (k + 1))
                        pe.wait_ge(up_loaded[k % RING], i * 32 + (16 * (k // RING) + 16))
                        for hf in range(2):
                            mm = nc.tensor.matmul(acc[:, b + hf, :], diag[:, k, :], up[k % RING][:, hf * 512:(hf + 1) * 512],
                                                  start=False, stop=False, skip_group_check=True)
                        mm.then_inc(up_used, 1)
                for hf in range(2):
                    mm = nc.tensor.matmul(acc[:, b + hf, :], c_("zero"), cst[:, 0:512], start=False, stop=True, skip_group_check=True)
                mm.then_inc(tile_done, 1)

        @block.scalar
        def _(act):
            n = Tally()

            def link(ins):
                n.step += 1
                ins.then_inc(act_step, 1)
                act.wait_ge(act_step, n.step)

            def run(o, i, func, **kw):
                return nc.scalar.activation(o, i, func, **kw)

            def unit(u):
                act.wait_ge(acc_ready, u + 1)
                return 2 * (u % 2)

            def wide(b, cols=1024):
                return acc[:, b:b + 2, :].rearrange("p a n -> p (a n)")[:, 0:cols]

            def halves(o):
                return o.rearrange("p (a t) -> p a t", a=2)

            def stat(tiles, t, source, used=0, meanwhile=()):
                for j in range(tiles):
                    if n.sq >= 2:
                        act.wait_ge(sq_used, n.sq - 1)
                    run(sq[:, n.sq % 2, 0:t], source(j), ACT.Square).then_inc(sq_ready, 1)
                    n.sq += 1
                for s in meanwhile:
                    high_part(s)
                act.wait_ge(sq_used, n.sq)
                o, mean = (logs[:, 0:T], sums[:, 0, :]) if t == T else (halves(logs[:, :]), sums[:, :, 0:HALF])
                link(run(o, mean, ACT.Ln, bias=c_("eps")))
                if used:
                    act.wait_ge(normed, used)
                run(rstd[:, 0:t], logs[:, 0:t], ACT.Exp, scale=-0.5).then_inc(rstd_ready, 1)

            def shift(norm, high, low, tile, t, stage):
                act.wait_ge(mods_ready, stage)
                for j in range(KD):
                    act.wait_ge(h_scaled, 8 * norm + j + 1)
                    ins = run(high[:, j, 0:T], low[:, j, 0:T], ACT.Identity, bias=mod[:, tile + j, 0:1])
                    if t == TC:
                        ins = run(high[:, j, T:TC], low[:, j, T:TC], ACT.Identity, bias=mod[:, tile + j, 1:2])
                    ins.then_inc(h_high, 1)

            def high_part(s, turn=0):
                act.wait_ge(w_loaded[s % W_RING], turn * 16 + (s // W_RING + 1) * 16)
                cols = 32 if s == TILE_OF["w_out"] - 1 else P
                run(Whir[:, s % W_RING, :, 0:cols], Wlo[:, s % W_RING, :, 0:cols], ACT.Copy).then_inc(w_high, 1)

            def ahead(s):
                s += W_RING
                if s < N_TILES:
                    high_part(s)

            def high_of(dst, src, j):
                run(dst[:, j, :], src[:, j, :], ACT.Copy).then_inc(y_high, 1)

            def mod_load(p, m, w, first_number):
                act.wait_ge(partial_ready, m + 1)
                act.dma_start(Mw[:, p, :, :], w.rearrange("(k p) n -> p k n", p=P)[:, :, ds(m * P + (2 - first_number) * P, P)]
                              ).then_inc(mod_loaded[p], 16)

            def silus(name, width, halves, first, per, count):
                base, s0, units = UNIT[name], TILE_OF[name], 2 * halves

                def source(m):
                    return (a["w_ada"][0], -FIRST_MODS) if m + 2 < ADA_LATER else (a["w_mod_2"][0], ADA_LATER)

                def step(i, odd):
                    for q in range(units):
                        for tile in range(q * per // units, (q + 1) * per // units):
                            m = i * per + (first + tile)
                            if not isinstance(m, int):
                                mod_load((first + tile + odd * per) % 2, m, *source(first))
                            elif m + 2 < N_LATER:
                                mod_load(m % 2, m, *source(m))
                        u0 = base + q
                        act.wait_ge(acc_ready, i * units + (u0 + 1))
                        run(sg[:, u0 % 2, 0:width], acc[:, 2 * (u0 % 2), 0:width], ACT.Silu).then_inc(silu_ready, 1)
                        if q % halves == halves - 1 and not (isinstance(i, int) and i == FT // 2 - 1):
                            for m in range(2):
                                high_part(s0 + W_RING + 2 * (q // halves) + m, i)
                step(0, 0)
                with act.Fori(0, 4) as j:
                    for odd in (1, 2):
                        step(j * 2 + odd, odd)
                for i in (9, 10):
                    step(i, i)
                for m in range(first + 11 * per, first + count):
                    if m + 2 < N_LATER:
                        mod_load(m % 2, m, *source(m))

            act.dma_start(cst[:, :], a["const"]).then_inc(const_loaded, 16)
            at, rows = ROWS["conv_w"]
            act.dma_start(rows1[at:at + rows, :], a["conv_w"].rearrange("l k (j q) -> (l k j) q", q=P)).then_inc(vec_loaded, 16)
            for name in ("q_norm", "k_norm"):
                for hf in range(2):
                    at = ROWS[name][0]
                    act.dma_start(rows1[at:at + 1, hf * 64:(hf + 1) * 64], a[name]).then_inc(vec_loaded, 16)
            act.dma_start(rows2[0:ADA_TILES, :], flat(a["b_ada"]).rearrange("(r q) -> r q", q=P)).then_inc(vec_loaded, 16)
            act.dma_start(rows2[ADA_TILES:N_BIAS, :], flat(a["b_mod_2"]).rearrange("(r q) -> r q", q=P)).then_inc(vec_loaded, 16)
            act.dma_start(dec[:, 0:4], a["ret_decay_f_2"].to_broadcast([P, 4])).then_inc(vec_loaded, 16)
            act.dma_start(dec[:, 4:8], a["ret_decay_b_2"].to_broadcast([P, 4])).then_inc(vec_loaded, 16)
            act.wait_ge(rows_zeroed, 1)
            act.dma_start(gkup[0:16, 0:256], a["gla_gk_up_f_2"][0]).then_inc(vec_loaded, 16)
            act.dma_start(gkup[16:32, 256:512], a["gla_gk_up_b_2"][0]).then_inc(vec_loaded, 16)

            for r in range(1, 6, 2):
                u = UNIT["tokens"] + r
                b = unit(u)
                run(x_[:, :, r * P:(r + 1) * P], wide(b).rearrange("p (j t) -> p j t", j=KD), ACT.Copy).then_inc(acc_free[u % 2], 1)
            act.wait_ge(vec_ready, 1)
            for blk, pair in enumerate((("c", "c_ctx"), ("c_2", "c_ctx_2"))):
                for w, name in enumerate(pair):
                    run(cnd[:, blk, :, w], v_(name, 0, KD), ACT.Silu).then_inc(cond_ready, 1)

            emptied(act, UNIT["tokens"] + 4)
            emptied(act, UNIT["tokens"] + 5)
            stat(KD, TC, lambda j: x_[:, j, :])
            act.wait_ge(decay_abs, 1)
            run(dec[:, 16:24], dec[:, 8:16], ACT.Exp, scale=-1.0).then_inc(decay_exp, 1)
            for s in range(W_RING):
                high_part(s)
            shift(0, hi768r, lo768, 0, TC, 1)
            silus("ffn1_in", HALF, 2, 0, MOD_PER_SLOT[0], ADA_LATER)

            def updated(name, j, units):
                for q in range(units):
                    emptied(act, UNIT[name] + units * j + q)
                return x_[:, j, :] if units == 2 else x_[:, j, 0:T]

            s0 = TILE_OF["mix_in"]
            stat(KD, TC, lambda j: updated("ffn1_out", j, 2), meanwhile=range(s0, s0 + W_RING))
            shift(1, hi768r, lo768, 3 * KD, TC, 2)

            def take(name, t, o, func=ACT.Copy, cols=T):
                u = UNIT[name] + t
                b = unit(u)
                src = acc[:, b, 0:T] if cols == T else acc[:, b:b + 2, 0:HALF]
                run(o, src, func).then_inc(acc_free[u % 2], 1)

            for t in range(4):
                take("q", t, qT[:, t, :])
                ahead(s0 + t)
            take("k", 0, halves(kT), cols=TC)
            ahead(s0 + 4)
            ahead(s0 + 5)
            for t in range(4):
                take("gb", t, gb[:, t, :])
                ahead(s0 + 6 + t)
            u = UNIT["vT"]
            b = unit(u)
            run(vtok, wide(b, 6 * P).rearrange("p (r n) -> p r n", r=6), ACT.Copy).then_inc(acc_free[u % 2], 1)
            for t in range(4):
                take("gc", t, gc[:, t, :])
                ahead(s0 + 10 + t)
            for t in range(4):
                ahead(s0 + 14 + t)

            def own(u, src):
                emptied(act, u)
                return src

            for t in range(4):
                stat(1, T, lambda j, t=t: own(UNIT["q"] + t, qT[:, t, :]), t)
            stat(1, TC, lambda j: own(UNIT["k"], kT), 4)
            for kv in range(KV_HEADS):
                take("kdup", kv, halves(kdup[:, kv, :]), cols=TC)

            def branch(j):
                act.wait_ge(conv_ready, j + 1)
                return mixT[:, 4 + j, :]
            stat(4, T, branch)

            for step in range(32 + 4):
                if step < 32:
                    u = UNIT["scores"] + step
                    act.wait_ge(negmax_ready, step + 1)
                    if step >= 3:
                        act.wait_ge(probT_ready, step - 2)
                    b = unit(u)
                    run(halves(prob[:, step % 3, :]), acc[:, b:b + 2, 0:HALF], ACT.Exp, scale=HD ** -0.5,
                        bias=small[:, step % 2:step % 2 + 1], accum_out=small[:, 2 + step % 2:3 + step % 2]).then_inc(exp_ready, 1)
                if 3 <= step < 35:
                    u = step - 3
                    act.wait_ge(probT_ready, u + 1)
                    if u >= 8:
                        act.wait_ge(o_ready, u // 4 - 1)
                    run(probT[:, (u // 4) % 2, 0:3, (u % 4) * P:(u % 4 + 1) * P],
                        sums[:, 0, 0:HALF].rearrange("p (r n) -> p r n", r=3), ACT.Copy).then_inc(probT_act, 1)
                if step >= 7 and (step - 7) % 4 == 0 or step == 35:
                    h = (step - 7) // 4
                    act.wait_ge(o_ready, h + 1)
                    rows = slice(64 * (h % 2), 64 * (h % 2) + 64)
                    run(mixT[rows, h // 2, :], misc[rows, :], ACT.Copy).then_inc(o_copied, 1)

            def heads(j):
                act.wait_ge(o_copied, 8)
                return mixT[:, j, :]
            act.wait_ge(o_copied, 8)
            for j in range(4, KD):
                high_of(mix_hir, mixT, j)
            stat(4, T, heads)
            for j in range(4):
                act.wait_ge(normed, 9 + j + 1)
                high_of(mix_hir, mixT, j)

            def behind(name):
                s = TILE_OF[name]
                for j in range(KD - W_RING):
                    ahead(s + j)
                stat(KD, T, lambda j: updated(name, j, 1), meanwhile=range(s + KD, s + KD + W_RING))

            behind("mix_out")
            shift(2, hi512r, lo512, 6 * KD, T, 2)
            silus("ffn2_in", T, 1, ADA_LATER, MOD_PER_SLOT[1], MOD_TILES)
            stat(KD, T, lambda j: updated("ffn2_out", j, 1))

            def renormed(j):
                act.wait_ge(x1_ready, j + 1)
                emptied(act, UNIT["tokens2"])
                emptied(act, UNIT["tokens2"] + 1)
                return x_[:, j, :]
            s0 = TILE_OF["proj"]
            stat(KD, TC, renormed, meanwhile=range(s0, s0 + W_RING))
            shift(3, hi768r, lo768, ADA_TILES, TC, 3)

            def both(name, s, dst):
                for c in range(4 + 1):
                    if c < 4:
                        ahead(s + c)
                    if c >= 1:
                        u = UNIT[name] + BY_TOKEN[c - 1]
                        b = unit(u)
                        run(dst[:, :, (c - 1) * P:c * P], wide(b, 6 * P).rearrange("p (r n) -> p r n", r=6),
                            ACT.Copy).then_inc(acc_free[u % 2], 1)

            for t in range(4):
                take("rq", t, rq[:, t, :])
                ahead(s0 + t)
            for t in range(4):
                take("rk", t, halves(rk[:, t, :]), cols=TC)
                ahead(s0 + 4 + t)
            both("rv", s0 + 8, rv)
            for t in range(4):
                take("rg", t, yT[:, t, :], ACT.Silu)
                ahead(s0 + 12 + t)
            for t in range(2):
                take("gq", t, gq[:, t, :])
                ahead(s0 + 16 + t)
            for t in range(2):
                take("gk", t, halves(gk[:, t, :]), cols=TC)
                ahead(s0 + 18 + t)
            both("gv", s0 + 20, gv)
            for t in range(4):
                take("gg", t, yT[:, 4 + t, :], ACT.Silu)
                if t == 0:
                    ahead(s0 + 24)

            soft = sq[:, 0, :]
            act.wait_ge(sq_used, n.sq)
            for u in range(4):
                emptied(act, UNIT["decay"] + u)
                if u:
                    act.wait_ge(la_ready, u)
                link(run(soft, la[:, u // 2, u % 2, :], ACT.Abs))
                link(run(soft, soft, ACT.Exp, scale=-1.0))
                run(soft, soft, ACT.Ln, bias=1.0).then_inc(ln_ready, 1)

            for s in range(TILE_OF["w_out"], TILE_OF["w_out"] + W_RING):
                high_part(s)

            def ret_out(h):
                act.wait_ge(o_ready, 8 + 6 * (h + 1))
                run(rq[:, h, :], [misc, mod_ps][h % 2][:, :], ACT.Copy).then_inc(o_copied, 1)

            for h in range(4):
                act.wait_ge(dist_arg, h + 1)
                if h:
                    act.wait_ge(dist_done, h)
                run(DX[:, h % 2, :], DX[:, h % 2, :], ACT.Exp)
                run(DC[:, h % 2, :], dist[:, T:], ACT.Exp, scale=dec[:, 8 + h:9 + h])
                run(sq[:, 1, 0:N_DC], dist[:, T:], ACT.Exp, scale=dec[:, 16 + h:17 + h],
                    bias=dec[:, 20 + h:21 + h]).then_inc(dist_exp, 1)
                if h:
                    ret_out(h - 1)
            ret_out(3)
            for h in range(4):
                def head(j, h=h):
                    act.wait_ge(o_copied, 9 + h)
                    return rq[:, h, :]
                stat(1, T, head, 13 + h)

            for d in range(2):
                base = UNIT[f"gla{d}"]
                e = (gE if d == 0 else gkd)[:, :, 0:T]
                g = (gG if d == 0 else gE)[:, :, 0:T]
                act.wait_ge(gla_arg, 2 * d + 1)
                run(gla_decay,
                    gG[:, :, 0:T].rearrange("p a (c i) -> p a c i", i=CHUNK)[:, :, :, CHUNK - 1],
                    ACT.Exp, scale=1.0 / GATE_NORM)
                if d:
                    act.wait_ge(acc_ready, UNIT["gla0"] + 2)
                run(e, g, ACT.Exp, scale=1.0 / GATE_NORM).then_inc(gla_exp, 1)
                act.wait_ge(gla_qk, 6 * d + 4)
                run(e, g, ACT.Exp, scale=-1.0 / GATE_NORM).then_inc(gla_exp, 1)
                act.wait_ge(gla_arg, 2 * d + 2)
                run(gE, gE, ACT.Exp, scale=1.0 / GATE_NORM).then_inc(gla_exp, 1)
                for pr in range(2):
                    u = base + pr
                    b = unit(u)
                    run(gkd_tok[:, :, pr * P:(pr + 1) * P], wide(b, 6 * P).rearrange("p (r n) -> p r n", r=6),
                        ACT.Copy).then_inc(acc_free[u % 2], 1)
            banks = [mod_ps[:, :], misc[:, :], sums[:, 0, :], sums[:, 1, :]]
            for h in range(4):
                act.wait_ge(gla_o, 4 + h + 1)
                run(og[:, h, :], banks[h], ACT.Copy).then_inc(o_copied, 1)
            act.wait_ge(normed, 13 + 4)
            for h in range(4):
                high_of(y_hir, yT, h)
            for h in range(4):
                def head(j, h=h):
                    act.wait_ge(o_copied, 13 + h)
                    return og[:, h, :]
                stat(1, T, head, 17 + h)
                if h:
                    high_of(y_hir, yT, 4 + h - 1)
            act.wait_ge(normed, 17 + 4)
            high_of(y_hir, yT, 7)

            behind("w_out")
            shift(4, hi512r, lo512, ADA_TILES + 3 * KD, T, 3)
            for t in range(16):
                if t % 2 == 0:
                    take("peer_q", t, pq[:, t, :])
                ahead(TILE_OF["peer_q"] + t)
            for u0 in range(0, 8, 2):
                u = UNIT["peer_s"] + u0
                b = unit(u)
                run(s_all[:, u0 // 2, 0:1024], wide(b), ACT.Copy).then_inc(acc_free[u % 2], 1)
            for name, dst in (("xb", xb), ("xtok", xtok)):
                for t in range(0, 4, 2):
                    u = UNIT[name] + t
                    b = unit(u)
                    run(dst[:, t, :], wide(b), ACT.Copy).then_inc(acc_free[u % 2], 1)
            for w, dst in enumerate((g2row, nfrow)):
                u = UNIT["rows"] + w
                b = unit(u)
                run(dst, wide(b), ACT.Copy).then_inc(acc_free[u % 2], 1)

            def softmax_exp(count):
                act.wait_ge(top_ready, count)
                run(p_exp, p_top, ACT.Exp, bias=p_neg, accum_out=p_sum).then_inc(p_exp_ready, 1)

            def expert_weights(i):
                act.wait_ge(dots_done, (i + 1) * PEER_K + RING)
                run(p_act, p_dot, ACT.Gelu).then_inc(gelu_ready, 1)
                act.wait_ge(weights_ready, i + 1)
                for k in range(PEER_K):
                    act.wait_ge(up_used, i * PEER_K + (k + 1))
                    run(diag[:, k, :], ident, ACT.Copy, scale=p_w[:, k:k + 1]).then_inc(diag_ready, 1)

            def expert_heads(first, last):
                with act.Fori(first, last) as i:
                    softmax_exp(i + 2)
                    expert_weights(i)

            def final_std(t):
                act.wait_ge(ssq_ready, t + 1)
                run(p_std, p_ssq, ACT.Sqrt, scale=1.0 / D, bias=c_("eps")).then_inc(fstd_ready, 1)

            softmax_exp(1)
            for t in range(4):
                first = t * PEER_H
                expert_heads(first, first + 1)
                if t:
                    final_std(t - 1)
                expert_heads(first + 1, first + PEER_H - (t == 3))
            expert_weights(4 * PEER_H - 1)
            final_std(3)

        @block.vector
        def _(dve):
            n = Tally()
            V = nc.vector

            def link(ins):
                n.step += 1
                ins.then_inc(dve_step, 1)
                dve.wait_ge(dve_step, n.step)

            def unit(u):
                dve.wait_ge(acc_ready, u + 1)
                return 2 * (u % 2)

            def free(ins, u):
                ins.then_inc(acc_free[u % 2], 1)

            def wide(b, cols=1024):
                return acc[:, b:b + 2, :].rearrange("p a n -> p (a n)")[:, 0:cols]

            def halves(o):
                return o.rearrange("p (a t) -> p a t", a=2)

            def stat():
                n.job += 1
                dve.wait_ge(rstd_ready, n.job)

            def scale(norm, high, low, part, t, tile):
                kinds = ((0, 0, T), (1, T, TC))[:1 if t == T else 2]
                for j in range(KD + 1):
                    if j < KD:
                        for c, lo, up_to in kinds:
                            ins = V.scalar_tensor_tensor(low[:, j, lo:up_to], x_[:, j, lo:up_to], gain[:, norm, j, c:c + 1], rstd[:, lo:up_to],
                                                         ALU.mult, ALU.mult)
                        ins.then_inc(h_scaled, 1)
                    if j >= 1:
                        dve.wait_ge(h_high, 8 * norm + j)
                        for c, lo, up_to in kinds:
                            ins = V.scalar_tensor_tensor(part[:, j - 1, lo:up_to], low[:, j - 1, lo:up_to],
                                                         mod[:, tile + j - 1, c:c + 1], high[:, j - 1, lo:up_to], ALU.add, ALU.subtract)
                        ins.then_inc(h_ready, 1)

            def low_of(part, y, high, j, count):
                dve.wait_ge(y_high, count)
                V.tensor_tensor(part[:, j, :], y[:, j, :], high[:, j, :], ALU.subtract).then_inc(y_ready, 1)

            def modulation(stage, first, last, gain_of, half_of):
                if stage == 1:
                    dve.wait_ge(first_used, 8)
                else:
                    dve.wait_ge(partial_used, CREDIT + last - FIRST_MODS)
                link(V.tensor_tensor(mod[:, first:last, :],
                                     mod_ps[:, 2 * first:2 * last].rearrange("p (t c) -> p t c", c=2),
                                     vec[:, 128 + first:128 + last].unsqueeze(2).to_broadcast([P, last - first, 2]), ALU.add))
                for norm, name, tile in gain_of:
                    ins = V.scalar_tensor_tensor(gain[:, norm], mod[:, tile:tile + KD, :], 1.0,
                                                 v_(name, 0, KD).unsqueeze(2).to_broadcast([P, KD, 2]), ALU.add, ALU.mult)
                for ffn, tile in half_of:
                    ins = V.tensor_scalar(hgate[:, ffn], mod[:, tile:tile + KD, :], 0.5, None, ALU.mult)
                ins.then_inc(mods_ready, 1)
                dve.wait_ge(mods_ready, stage)

            def mod_products(p, m, uses, blk, conds=2):
                dve.wait_ge(partial_used, m + 1)
                dve.wait_ge(mod_loaded[p], uses * 16)
                for k in range(KD):
                    if k:
                        dve.wait_ge(mod_step, m * (KD - 1) + k)
                    for c in range(conds):
                        sum_, w, x1 = partial[:, p, c, :], Mw[:, p, k, :], cnd[:, blk, k, c:c + 1]
                        if k == 0:
                            ins = V.tensor_scalar(sum_, w, x1, None, ALU.mult)
                        else:
                            ins = V.scalar_tensor_tensor(sum_, w, x1, sum_, ALU.mult, ALU.add)
                    ins.then_inc(mod_step if k < KD - 1 else partial_ready, 1)

            def swiglu(name, width, sides, done, blk, first, per, count):
                units, base = 2 * sides, UNIT[name]

                def step(j, odd, conds):
                    for q in range(units):
                        u0 = base + odd * units + q
                        sub, hf = q // sides, q % sides
                        for tile in range(q * per // units, (q + 1) * per // units):
                            n0 = odd * per + first + tile
                            mod_products(n0 % 2, j * (2 * per) + n0, j * per + (n0 // 2 + 1), blk, conds)
                        dve.wait_ge(silu_ready, j * 2 * units + (done + odd * units + q + 1))
                        free(V.tensor_tensor(arena[:, ds(j * 4 * width * sides + ((2 * odd + sub) * sides + hf) * width, width)],
                                             sg[:, u0 % 2, 0:width], acc[:, 2 * (u0 % 2) + 1, 0:width], ALU.mult), u0)
                step(0, 0, 2)
                for start, stop, conds in MOD_LOOPS:
                    with dve.Fori(start, stop) as j:
                        for odd in (1, 2):
                            step(j, odd, conds)
                for m in range(first + 11 * per, first + count):
                    mod_products(m % 2, m, m // 2 + 1, blk, 1)

            def residual(name, sides, ffn):
                base = UNIT[name]

                def step(i, p):
                    for hf in range(sides):
                        u0 = base + p * sides + hf
                        dve.wait_ge(acc_ready, i * 2 * sides + (u0 + 1))
                        at, b = 0, 2 * (u0 % 2)
                        parts = [(0, 0, T)] if sides == 1 else [(0, 0, HALF)] if hf == 0 else [(0, HALF, T), (1, T, TC)]
                        for kind, lo, hi_ in parts:
                            x1 = resid[:, ds(i * 2 * TC + (p * TC + lo), hi_ - lo)]
                            ins = V.scalar_tensor_tensor(x1, acc[:, b, at:at + hi_ - lo],
                                                         halfg[:, ds(i * 4 + (16 * ffn + 2 * p + kind), 1)], x1,
                                                         ALU.mult, ALU.add)
                            at += hi_ - lo
                        free(ins, u0)
                pairs(dve, KD, step)

            dve.sem_inc(partial_used, CREDIT)
            V.memset(gkup[:, :], 0.0).then_inc(rows_zeroed, 1)
            for r in range(0, 6, 2):
                u = UNIT["tokens"] + r
                b = unit(u)
                free(V.tensor_copy(x_[:, :, r * P:(r + 1) * P], wide(b).rearrange("p (j t) -> p j t", j=KD)), u)
            dve.wait_ge(vec_turned, 1)
            V.tensor_copy(vec[:, 0:N_ROWS], misc[:, 0:N_ROWS])
            V.tensor_copy(vec[:, 128:128 + N_BIAS], misc[:, 128:128 + N_BIAS]).then_inc(vec_ready, 1)
            dve.wait_ge(vec_ready, 1)
            dve.wait_ge(vec_loaded, 16 * N_VEC_DMAS)
            V.scalar_tensor_tensor(dec[:, 8:16], dec[:, 0:8], -1.0, dec[:, 0:8], ALU.mult, ALU.max).then_inc(decay_abs, 1)
            stat()
            modulation(1, 0, FIRST_MODS, [(0, "norm_ffn1", KD)], [])
            scale(0, hi768r, lo768, lo768r, TC, 0)
            dve.wait_ge(decay_exp, 1)
            z, s_, s2, series, least = (dec[:, 16 + 8 * i:24 + 8 * i] for i in range(5))
            link(V.tensor_scalar(s2, z, 2.0, None, ALU.add))
            link(V.reciprocal(s2, s2))
            link(V.tensor_tensor(s_, z, s2, ALU.mult))
            link(V.tensor_tensor(s2, s_, s_, ALU.mult))
            link(V.tensor_scalar(series, s2, 1.0 / 19, None, ALU.mult))
            for odd in range(17, 1, -2):
                link(V.scalar_tensor_tensor(series, series, 1.0 / odd, s2, ALU.add, ALU.mult))
            link(V.scalar_tensor_tensor(series, series, 1.0, s_, ALU.add, ALU.mult))
            link(V.tensor_scalar(least, dec[:, 0:8], 0.0, None, ALU.min))
            link(V.scalar_tensor_tensor(dec[:, 8:16], series, -2.0, least, ALU.mult, ALU.add))
            V.tensor_scalar(dec[:, 16:20], dec[:, 12:16], -1.0, None, ALU.mult)
            link(V.tensor_scalar(dec[:, 20:24], dec[:, 12:16], 640.0 + P, None, ALU.mult))

            swiglu("ffn1_in", HALF, 2, 0, 0, 0, MOD_PER_SLOT[0], ADA_LATER)
            modulation(2, FIRST_MODS, ADA_TILES, [(1, "norm_mix", 4 * KD), (2, "norm_ffn2", 7 * KD)],
                       [(0, 2 * KD), (1, 8 * KD)])
            residual("ffn1_out", 2, 0)
            stat()
            scale(1, hi768r, lo768, lo768r, TC, 3 * KD)

            u = UNIT["v"]
            b = unit(u)
            free(V.tensor_copy(halves(sq[:, 0, :]), acc[:, b:b + 2, 0:HALF]), u)
            V.memset(cu[:, :, 0:1], 0.0)
            V.memset(cu[:, :, T + 1:T + 2], 0.0)
            for t in range(4):
                u = UNIT["u"] + t
                emptied(dve, UNIT["gc"] + t)
                b = unit(u)
                free(V.tensor_tensor(cu[:, t, 1:T + 1], acc[:, b, :], gc[:, t, :], ALU.mult), u)
            for t in range(5):
                width, dst = (T, qT[:, t, :]) if t < 4 else (TC, kT)
                stat()
                V.scalar_tensor_tensor(dst, dst, v_("q_norm" if t < 4 else "k_norm"), rstd[:, 0:width],
                                       ALU.mult, ALU.mult).then_inc(normed, 1)

            def rope(u, dst, cos, sin, before):
                b = unit(u)
                if before:
                    dve.wait_ge(copied, before)
                free(V.tensor_tensor(tmp[:, 0:T], acc[:, b, :], sin, ALU.mult), u)
                link(V.tensor_tensor(dst, dst, cos, ALU.mult))
                V.tensor_tensor(dst, dst, tmp[:, 0:T], ALU.add).then_inc(copied, 1)

            dve.wait_ge(pairs_loaded, 16)
            for t in range(5):
                rope(UNIT["rope_q"] + t, qT[:, t, :] if t < 4 else kT[:, 0:T], cos_pairs, sin_pairs, t)
            for t in range(4):
                y = mixT[:, 4 + t, :]
                emptied(dve, UNIT["gb"] + t)
                link(V.tensor_scalar(y, cu[:, t, 0:T], v_("conv_w", t), None, ALU.mult))
                for tap in (1, 2):
                    link(V.scalar_tensor_tensor(y, cu[:, t, tap:tap + T], v_("conv_w", tap * 4 + t), y, ALU.mult, ALU.add))
                V.tensor_tensor(y, y, gb[:, t, :], ALU.mult).then_inc(conv_ready, 1)

            def branch_norm(first, name):
                stat()
                for t in range(4):
                    y = mixT[:, first + t, :]
                    V.scalar_tensor_tensor(y, y, v_(name, t), rstd[:, 0:T], ALU.mult, ALU.mult).then_inc(normed, 1)
            branch_norm(4, "conv_out_norm")

            for step in range(32 + 3):
                if 1 <= step < 33:
                    u = step - 1
                    inv = small[:, 16 + u % 4:17 + u % 4]
                    dve.wait_ge(exp_ready, u + 1)
                    free(V.reciprocal(inv, small[:, 2 + u % 2:3 + u % 2]), UNIT["scores"] + u)
                    emptied(dve, UNIT["scores"] + u)
                    V.tensor_scalar(prob[:, u % 3, :], prob[:, u % 3, :], inv, None, ALU.mult).then_inc(prob_ready, 1)
                if step < 32:
                    b = unit(UNIT["scores"] + step)
                    top = small[:, 8 + step % 2:9 + step % 2]
                    link(V.tensor_reduce(top, acc[:, b:b + 2, 0:HALF], mybir.AxisListType.XY, ALU.max))
                    V.tensor_scalar(small[:, step % 2:step % 2 + 1], top, -HD ** -0.5, None, ALU.mult).then_inc(negmax_ready, 1)
                if step >= 3:
                    u = step - 3
                    dve.wait_ge(probT_ready, u + 1)
                    if u >= 8:
                        dve.wait_ge(o_ready, u // 4 - 1)
                    V.tensor_copy(probT[:, (u // 4) % 2, 3:6, (u % 4) * P:(u % 4 + 1) * P],
                                  sums[:, 1, 0:HALF].rearrange("p (r n) -> p r n", r=3)).then_inc(probT_dve, 1)
            for i, j in enumerate(range(4, KD)):
                low_of(mixTr, mixT, mix_hir, j, i + 1)
            branch_norm(0, "attn_out_norm")
            for j in range(4):
                low_of(mixTr, mixT, mix_hir, j, 4 + j + 1)

            def gated_residual(name, gate_tile):
                for j in range(KD):
                    u = UNIT[name] + j
                    b = unit(u)
                    free(V.scalar_tensor_tensor(x_[:, j, 0:T], acc[:, b, :], mod[:, gate_tile + j, 0:1], x_[:, j, 0:T],
                                                ALU.mult, ALU.add), u)
            gated_residual("mix_out", 5 * KD)

            stat()
            scale(2, hi512r, lo512, lo512r, T, 6 * KD)
            swiglu("ffn2_in", T, 1, 44, 1, ADA_LATER, MOD_PER_SLOT[1], MOD_TILES)
            blk2 = ADA_TILES
            modulation(3, blk2, N_BIAS, [(3, "norm1_w_2", blk2 + KD), (4, "norm2_w_2", blk2 + 4 * KD)], [])
            residual("ffn2_out", 1, 1)
            for r in range(2):
                u = UNIT["tokens2"] + r
                b = unit(u)
                free(V.tensor_copy(x_[:, :, T + r * P:T + (r + 1) * P], wide(b).rearrange("p (j t) -> p j t", j=KD)), u)
            stat()
            for j in range(KD):
                V.scalar_tensor_tensor(x_[:, j, 0:T], x_[:, j, 0:T], v_("final_norm", j), rstd[:, 0:T],
                                       ALU.mult, ALU.mult).then_inc(x1_ready, 1)
            stat()
            scale(3, hi768r, lo768, lo768r, TC, ADA_TILES)

            def take(name, t, o, src):
                u = UNIT[name] + t
                b = unit(u)
                free(V.tensor_copy(o, src(b)), u)

            for name in ("rv", "gv"):
                for c in range(4):
                    take(name, BY_FEATURE[c], halves(sq[:, c % 2, :]), lambda b: acc[:, b:b + 2, 0:HALF])
            take("lr", 0, halves(lr), lambda b: acc[0:32, b:b + 2, 0:HALF])

            dve.wait_ge(halves_loaded, 16)
            for t in range(8):
                rope(UNIT["rope_r"] + t, rq[:, t, :] if t < 4 else rk[:, t - 4, 0:T], cos_halves, sin_halves, 5 + t)

            soft = sq[:, 0, :]
            for u in range(4):
                b = unit(UNIT["decay"] + u)
                free(V.tensor_scalar(halves(la[:, u // 2, u % 2, :]), acc[:, b:b + 2, 0:HALF],
                                     v_(("gla_gk_bias_f_2", "gla_gk_bias_b_2")[u // 2], u % 2), None, ALU.add), UNIT["decay"] + u)
            for u in range(4):
                dve.wait_ge(ln_ready, u + 1)
                z = la[:, u // 2, u % 2, :]
                V.scalar_tensor_tensor(z, z, 0.0, soft, ALU.min, ALU.subtract).then_inc(la_ready, 1)

            def distances(h):
                x1 = DX[:, h % 2, :]
                link(V.tensor_scalar(x1, dist[:, 0:N_DX], dec[:, 16 + h:17 + h], None, ALU.mult))
                V.scalar_tensor_tensor(x1, dist[:, 0:N_DX], dec[:, 8 + h:9 + h], x1,
                                       ALU.mult, ALU.min).then_inc(dist_arg, 1)

            dve.wait_ge(dist_loaded, 16)
            distances(0)
            distances(1)
            for h in range(4):
                dve.wait_ge(dist_exp, h + 1)
                V.tensor_tensor(DX[:, h % 2, 384:384 + P], DX[:, h % 2, 384:384 + P], ident, ALU.add)
                V.tensor_tensor(DC[:, h % 2, :], DC[:, h % 2, :], sq[:, 1, 0:N_DC], ALU.add).then_inc(dist_done, 1)
                dve.wait_ge(dist_done, h + 1)
                for r in range(6):
                    u = 6 * h + r
                    b = unit(UNIT["ret"] + u)
                    if u >= 2:
                        dve.wait_ge(o_ready, 8 + u - 1)
                    decay = DX[:, h % 2, 384 - P * r:384 - P * r + T] if r < 4 else DC[:, h % 2, P - P * (r - 4):P - P * (r - 4) + T]
                    free(V.scalar_tensor_tensor(retP[:, u % 2, :], acc[:, b, :], RET_SCALE, decay, ALU.mult, ALU.mult), UNIT["ret"] + u)
                if h + 2 < 4:
                    emptied(dve, UNIT["ret"] + 6 * h + 5)
                    distances(h + 2)

            def head_norm(o, gate):
                stat()
                link(V.tensor_tensor(o, o, rstd[:, 0:T], ALU.mult))
                V.tensor_tensor(gate, gate, o, ALU.mult).then_inc(normed, 1)
            for h in range(4):
                head_norm(rq[:, h, :], yT[:, h, :])

            def chunks(x1):
                return x1.rearrange("p (c i) -> p c i", i=CHUNK)

            dve.wait_ge(o_ready, 8 + 24)
            for d in range(2):
                base = UNIT[f"gla{d}"]
                for pr in range(2):
                    ins = V.tensor_tensor_scan(gG[:, pr, :], c_("chunk_reset"), la[:, d, pr, :], 0.0, ALU.mult, ALU.add)
                if d == 0:
                    ins.then_inc(gla_arg, 1)
                    dve.wait_ge(gla_arg, 1)
                else:
                    link(ins)
                    for pr in range(2):
                        G4 = chunks(gG[:, pr, 0:T])
                        ins = V.tensor_tensor(chunks(gE[:, pr, 0:T]), G4[:, :, CHUNK - 1:CHUNK].to_broadcast([P, NCH, CHUNK]), G4, ALU.subtract)
                    link(ins)
                    for pr in range(2):
                        ins = V.tensor_tensor(gE[:, pr, 0:T], gE[:, pr, 0:T], la[:, d, pr, 0:T], ALU.add)
                    ins.then_inc(gla_arg, 1)
                    dve.wait_ge(gla_o, 4)
                e = gE if d == 0 else gkd
                dve.wait_ge(gla_exp, 3 * d + 1)
                for h in range(4):
                    V.scalar_tensor_tensor(gqz[:, h, :], gq[:, h // 2, :], c_("head_rows")[:, h % 2:h % 2 + 1], e[:, h // 2, 0:T],
                                           ALU.mult, ALU.mult).then_inc(gla_qk, 1)
                dve.wait_ge(gla_exp, 3 * d + 2)
                for pr in range(2):
                    V.tensor_tensor(gkt[:, pr, :], gk[:, pr, 0:T], e[:, pr, 0:T], ALU.mult).then_inc(gla_qk, 1)
                dve.wait_ge(gla_qk, 6 * (d + 1))
                for pr in range(2):
                    if d == 0:
                        G4 = chunks(gG[:, pr, 0:T])
                        V.tensor_tensor(chunks(gE[:, pr, 0:T]), G4[:, :, CHUNK - 1:CHUNK].to_broadcast([P, NCH, CHUNK]), G4, ALU.subtract)
                        ins = V.tensor_tensor(gE[:, pr, T:TC], gG[:, pr, TC - 1:TC].to_broadcast([P, C]), gG[:, pr, T:TC], ALU.subtract)
                    else:
                        ins = V.tensor_tensor(gE[:, pr, :], gG[:, pr, :], la[:, d, pr, :], ALU.subtract)
                ins.then_inc(gla_arg, 1)
                dve.wait_ge(gla_exp, 3 * d + 3)
                for pr in range(2):
                    V.tensor_tensor(gkd[:, pr, :], gk[:, pr, :], gE[:, pr, :], ALU.mult).then_inc(gla_kd, 1)
                link(V.memset(gP[:, :, :], 0.0))
                u = base + 2
                b = unit(u)
                order = list(range(NCH)) if d == 0 else list(range(NCH - 1, -1, -1))
                free(V.tensor_copy(gS[:, :, order[0], :], acc[:, b, 0:2 * P].rearrange("p (a v) -> p a v", a=2)), u)
                emptied(dve, u)
                for pr in range(2):
                    u = base + 3 + pr
                    b = unit(u)
                    for i in range(NCH - 1):
                        c = order[i]
                        ins = V.scalar_tensor_tensor(gS[:, pr, order[i + 1], :], gS[:, pr, c, :], gla_decay[:, pr, c:c + 1],
                                                     acc[:, b + c % 2, (c // 2) * P:(c // 2 + 1) * P], ALU.mult, ALU.add)
                        if i < NCH - 2:
                            ins.then_inc(gla_states, 1)
                            dve.wait_ge(gla_states, 12 * d + 6 * pr + i + 1)
                        else:
                            free(ins, u)
                mask = c_(("causal_f", "causal_b")[d]).bitcast(I32).unsqueeze(1).to_broadcast([P, 4, P])
                for h in range(4):
                    u = base + 5 + h
                    b = unit(u)
                    if h >= 2:
                        dve.wait_ge(gla_o, 4 * d + h - 1)
                    free(V.copy_predicated(gP[:, h % 2, :].rearrange("p (r n) -> p r n", r=4), mask,
                                           acc[:, b, :].rearrange("p (r n) -> p r n", r=4)), u)
            for h in range(4):
                low_of(yTr, yT, y_hir, h, 8 + h + 1)
            for h in range(4):
                head_norm(og[:, h, :], yT[:, 4 + h, :])
                if h:
                    low_of(yTr, yT, y_hir, 4 + h - 1, 12 + h)
            low_of(yTr, yT, y_hir, 7, 16)

            gated_residual("w_out", ADA_TILES + 2 * KD)
            stat()
            scale(4, hi512r, lo512, lo512r, T, ADA_TILES + 3 * KD)
            for t in range(1, 16, 2):
                take("peer_q", t, pq[:, t, :], lambda b: acc[:, b, :])
            for g in range(2):
                take("keys", g, kTr[:, 8 * g:8 * g + 8, :], lambda b: wide(b).rearrange("p (j n) -> p j n", j=8))
            for g in range(2):
                emptied(dve, UNIT["keys"] + g)
            for w in range(2):
                for j in range(KD):
                    col = mod[:, ADA_TILES + 5 * KD + j, 0:1] if w == 0 else v_("norm_f_w_2", j)
                    V.tensor_scalar(rowsrc[:, w * KD + j, :], ones, col, None, ALU.mult).then_inc(rowsrc_ready, 1)
            for u0 in range(1, 8, 2):
                take("peer_s", u0, s_all[:, u0 // 2, 1024:2048], wide)
            TOPK_STEPS = 14

            def topk(i):
                done = [0]

                def step(ins):
                    done[0] += 1
                    ins.then_inc(topk_step, 1)
                    dve.wait_ge(topk_step, i * TOPK_STEPS + done[0])
                    dve.sem_inc(dve_go, 1)

                side = [slice(0, P), slice(P, 2 * P)]
                step(V.tensor_copy(s_cur, arena[:, ds(i * 256 + 8192, 256)]))
                for m in range(2):
                    ins = V.max(key_top[:, 16 * m:16 * m + 8], s_cur[:, side[m]])
                step(ins)
                for m in range(2):
                    V.max_index(key_at[:, 16 * m:16 * m + 8], key_top[:, 16 * m:16 * m + 8], s_cur[:, side[m]])
                    ins = V.match_replace(s_less[:, side[m]], key_top[:, 16 * m:16 * m + 8], s_cur[:, side[m]], -3e38)
                step(ins)
                for m in range(2):
                    ins = V.max(key_top[:, 16 * m + 8:16 * m + 16], s_less[:, side[m]])
                step(ins)
                for m in range(2):
                    V.max_index(key_at[:, 16 * m + 8:16 * m + 16], key_top[:, 16 * m + 8:16 * m + 16], s_less[:, side[m]])
                step(V.tensor_tensor(cand.rearrange("p (a b) -> p a b", a=16), key_top[:, 0:16].unsqueeze(2).to_broadcast([P, 16, 16]),
                                     key_top[:, 16:32].unsqueeze(1).to_broadcast([P, 16, 16]), ALU.add))
                V.tensor_copy(key_no, key_at)
                step(V.max(p_top[:, 0:8], cand))
                V.max_index(cand_at[:, 0:8], p_top[:, 0:8], cand)
                step(V.match_replace(cand_less, p_top[:, 0:8], cand, -3e38))
                step(V.max(p_top[:, 8:16], cand_less))
                V.tensor_scalar(p_neg, p_top[:, 0:1], -1.0, None, ALU.mult).then_inc(top_ready, 1)
                step(V.max_index(cand_at[:, 8:16], p_top[:, 8:16], cand_less))
                V.tensor_scalar(cand_half[:, 0:16], cand_at, 4, None, ALU.logical_shift_right)
                step(V.tensor_scalar(cand_half[:, 16:32], cand_at, 15, None, ALU.bitwise_and))
                step(V.tensor_copy(cand_no, cand_half))
                pick = onehot.rearrange("p (k j) -> p k j", k=32)
                step(V.tensor_tensor(pick, cand_no.unsqueeze(2).to_broadcast([P, 32, 16]),
                                     c_("iota16").unsqueeze(1).to_broadcast([P, 32, 16]), ALU.is_equal))
                for m in range(2):
                    half = pick[:, 16 * m:16 * m + 16, :]
                    ins = V.tensor_tensor(half, half, key_no[:, 16 * m:16 * m + 16].unsqueeze(1).to_broadcast([P, 16, 16]), ALU.mult)
                step(ins)
                step(V.tensor_reduce(chosen, pick, AX_X, ALU.add))
                V.scalar_tensor_tensor(idx_all[:, ds(i * PEER_K, PEER_K)], chosen[:, 0:16], float(N_KEYS), chosen[:, 16:32],
                                       ALU.mult, ALU.add).then_inc(idx_ready, 1)
                assert done[0] == TOPK_STEPS

            def softmax(i):
                dve.wait_ge(p_exp_ready, i + 1)
                dve.sem_inc(dve_go, 1)
                V.reciprocal(p_inv, p_sum).then_inc(inv_ready, 1)
                dve.wait_ge(inv_ready, i + 1)
                V.tensor_scalar(g_all[:, ds(i * PEER_K, PEER_K)], p_exp, p_inv, None, ALU.mult)

            def dots(t, i):
                for s in range(PEER_K):
                    dve.wait_ge(down_loaded[s % RING], i * 32 + 16 * (s // RING + 1))
                    V.scalar_tensor_tensor(down[:, s % RING, :], down[:, s % RING, :], 1.0, xb[:, t, :], ALU.mult, ALU.mult,
                                           accum_out=p_dot[:, s:s + 1]).then_inc(dots_done, 1)

            def weights(i):
                dve.wait_ge(gelu_ready, i + 1)
                V.tensor_tensor(p_w, p_act, g_all[:, ds(i * PEER_K, PEER_K)], ALU.mult).then_inc(weights_ready, 1)

            def finish(t):
                dve.wait_ge(tile_done, t + 1)
                if t:
                    dve.wait_ge(out_stored, t * 16)
                V.tensor_tensor(fin, acc[:, 2 * (t % 2):2 * (t % 2) + 2, :].rearrange("p a n -> p (a n)"), g2row,
                                ALU.mult).then_inc(tile_read, 1)
                dve.wait_ge(tile_read, CREDIT + t + 1)
                link(V.tensor_tensor(fin, fin, xtok[:, t, :], ALU.add))
                V.scalar_tensor_tensor(junk, fin, 1.0, fin, ALU.mult, ALU.mult, accum_out=p_ssq).then_inc(ssq_ready, 1)
                dve.wait_ge(fstd_ready, t + 1)
                link(V.reciprocal(p_rstd, p_std))
                V.scalar_tensor_tensor(fin, fin, p_rstd, nfrow, ALU.mult, ALU.mult).then_inc(fin_ready, 1)

            def heads(t, first, last):
                with dve.Fori(t * PEER_H + first, t * PEER_H + last) as i:
                    topk(i + 1)
                    dots(t, i)
                    softmax(i + 1)
                    weights(i)

            emptied(dve, UNIT["peer_s"])
            topk(0)
            for name, dst in (("xb", xb), ("xtok", xtok)):
                for t in range(1, 4, 2):
                    take(name, t, dst[:, t, :], wide)
            for w in range(2):
                emptied(dve, UNIT["rows"] + w)
            softmax(0)
            for t in range(4):
                heads(t, 0, 1)
                if t:
                    finish(t - 1)
                heads(t, 1, PEER_H - (t == 3))
            dots(3, 4 * PEER_H - 1)
            weights(4 * PEER_H - 1)
            finish(3)

        @block.gpsimd
        def _(pool):
            def low_part(s, turn=0):
                pool.wait_ge(w_high, turn * W_RING + (s + 1))
                p, cols = s % W_RING, 32 if s == TILE_OF["w_out"] - 1 else P
                nc.gpsimd.tensor_tensor(Wlor[:, p, :, 0:cols], Wlo[:, p, :, 0:cols], Whir[:, p, :, 0:cols],
                                        ALU.subtract).then_inc(w_ready, 1)

            rounds = (TILE_OF["w_out"] - 1) // W_RING
            with pool.Fori(0, rounds) as turn:
                for s in range(W_RING):
                    low_part(s, turn)
            for s in range(rounds * W_RING, N_TILES):
                low_part(s)

            pool.sem_inc(dots_done, RING)
            pool.sem_inc(up_used, PEER_K)
            with pool.Fori(0, 2 * PEER_H) as pair:
                for p in range(2):
                    i = pair * 2 + p
                    pool.wait_ge(idx_ready, i + 1)
                    pool.sem_inc(pool_go, 1)
                    nc.gpsimd.tensor_copy(stage[p], idx_all[:, ds(i * PEER_K, PEER_K)]).then_inc(stage_ready, 1)
                    pool.wait_ge(stage_ready, i + 1)
                    pool.sem_inc(pool_go, 1)
                    for s in range(PEER_K):
                        pool.wait_ge(dots_done, i * PEER_K + (s + 1))
                        pool.sem_inc(pool_go, 1)
                        nc.gpsimd.indirect_dma_start(down[:, s % RING, :], None, a["peer_down_2"][0],
                                                     bass.IndirectOffsetOnAxis(ap=stage[p][:, s:s + 1], axis=0)
                                                     ).then_inc(down_loaded[s % RING], 16)
                    for s in range(PEER_K):
                        pool.wait_ge(up_used, i * PEER_K + (s + RING + 1))
                        pool.sem_inc(pool_go, 1)
                        nc.gpsimd.indirect_dma_start(up[s % RING], None, a["peer_up_2"][0],
                                                     bass.IndirectOffsetOnAxis(ap=stage[p][:, s:s + 1], axis=0)
                                                     ).then_inc(up_loaded[s % RING], 16)

        @block.sync
        def _(sp):
            sp.sem_inc(tile_read, CREDIT)

            def features(w):
                return w.rearrange("(k p) n -> p k n", p=P)

            def tile_load(s, w, col, cols=P, free=None):
                if free is None:
                    free = TILE_FREE[s]
                if not isinstance(free, int) or free > 0:
                    sp.wait_ge(acc_ready, free)
                sp.dma_start(Wlo[:, s % W_RING, :, 0:cols], features(w)[:, :, ds(col, cols)]).then_inc(w_loaded[s % W_RING], 16)

            def stage_load(stage, w):
                n = w.shape[1]
                for col in range(0, n, P):
                    tile_load(TILE_OF[stage] + col // P, w, col, min(P, n - col))

            def ffn_in(name, w, halves):
                s0 = TILE_OF[name]

                def step(i):
                    for f in range(2):
                        for m in range(2):
                            s = s0 + 2 * f + m
                            free = TILE_FREE[s] if isinstance(i, int) else i * 2 * halves + (UNIT[name] + (f - 1) * halves)
                            tile_load(s, w, i * 256 + (f * P + m * FF), free=free)
                step(0)
                with sp.Fori(1, FT // 2) as i:
                    step(i)

            def ffn_out(name, w, units):
                def step(i, p):
                    it = i * 2 + p
                    if isinstance(i, int):
                        sp.wait_ge(acc_ready, UNIT[name])
                    else:
                        sp.wait_ge(acc_ready, it * units + (UNIT[name] - units))
                    for m in range(2):
                        f = slice(11 * m, 11 * m + 11)
                        sp.dma_start(Wf[:, p, f, :], w.rearrange("(f p) n -> p f n", p=P)[:, f, ds(it * P, P)]).then_inc(f_loaded[p], 16)
                pairs(sp, 8, step, first=2)

            for r in range(4):
                sp.dma_start(tok[:, r, :], a["x"][0][r * P:(r + 1) * P, :]).then_inc(tok_loaded, 16)
            for r in range(2):
                sp.dma_start(tok[:, 4 + r, :], a["ctx"][0][r * P:(r + 1) * P, :]).then_inc(tok_loaded, 16)
            for name in ("c", "c_ctx", "norm_ffn1", "norm_mix", "attn_out_norm", "conv_out_norm", "norm_ffn2",
                         "final_norm", "c_2", "c_ctx_2", "norm1_w_2", "norm2_w_2", "norm_f_w_2",
                         "gla_gk_bias_f_2", "gla_gk_bias_b_2"):
                at, rows = ROWS[name]
                sp.dma_start(rows1[at:at + rows, :], flat(a[name]).rearrange("(r q) -> r q", q=P)).then_inc(vec_loaded, 16)
            for i in range(8):
                sp.dma_start(Mfirst[i], features(a["w_ada"][0])[:, :, i * 256:(i + 1) * 256]).then_inc(first_loaded[i], 16)

            for m in range(2):
                sp.dma_start(Mw[:, m, :, :], features(a["w_ada"][0])[:, :, ds((FIRST_MODS + m) * P, P)]).then_inc(mod_loaded[m], 16)
            ffn_in("ffn1_in", a["w_ffn1_in"][0], 2)
            ffn_out("ffn1_out", a["w_ffn1_out"][0], 2)
            stage_load("mix_in", a["w_mix_in"][0])
            sp.wait_ge(acc_ready, UNIT["rope_q"])
            sp.dma_start(hid[:, 0:2 * T], a["rope"][:, 0:2 * T]).then_inc(pairs_loaded, 16)
            stage_load("mix_out", a["w_mix_out"][0])
            sp.wait_ge(acc_ready, UNIT["ffn2_in"])
            for r in range(2):
                sp.dma_start(tok2[:, r, :], a["ctx_2"][0][r * P:(r + 1) * P, :]).then_inc(tok2_loaded, 16)
            ffn_in("ffn2_in", a["w_ffn2_in"][0], 1)
            ffn_out("ffn2_out", a["w_ffn2_out"][0], 1)

            stage_load("proj", a["w_in_2"][0])
            sp.wait_ge(acc_ready, UNIT["rope_r"])
            sp.dma_start(hid[:, 1152:1152 + 2 * T], a["rope"][:, 2 * T:4 * T]).then_inc(halves_loaded, 16)
            sp.dma_start(dist, a["dist"]).then_inc(dist_loaded, 16)
            stage_load("w_out", a["w_out_2"][0])
            sp.wait_ge(acc_ready, UNIT["w_out"] + 1)
            for m, name in enumerate(("peer_k1_2", "peer_k2_2")):
                sp.dma_start(knat.rearrange("p (h m) n -> p h m n", m=2)[:, :, m, :],
                             a[name][0].rearrange("h n d -> n h d")).then_inc(keys_loaded, 16)
            stage_load("peer_q", a["peer_w_q_2"][0])

            for t in range(4):
                sp.wait_ge(fin_ready, t + 1)
                sp.dma_start(out[0][t * P:(t + 1) * P, :], fin).then_inc(out_stored, 16)
            sp.wait_ge(out_stored, 4 * 16)


def kernel(**inputs):
    import concourse.bacc as bacc
    from concourse.bass_utils import run_bass_kernel_spmd

    nc = bacc.Bacc("TRN2", target_bir_lowering=False, num_devices=1)
    arrays, aps = {}, {}
    for name, value in {**inputs, **constants()}.items():
        value = np.ascontiguousarray(value)
        arrays[f"in_{name}"] = value
        aps[name] = nc.dram_tensor(f"in_{name}", value.shape, mybir.dt.from_np(value.dtype), kind="ExternalInput").ap()
    out = nc.dram_tensor("out", (1, T, D), F32, kind="ExternalOutput").ap()
    build(nc, aps, out)
    result = run_bass_kernel_spmd(nc, [arrays], core_ids=[0])
    return result.results[0]["out"]
```
